# Optimizing a Trainium2 kernel written in Bass

```python
import math
import jax, jax.numpy as jnp
from jax import lax
import numpy as np

D_MODEL = 1024
BATCH = 1
SEQ = 128
DEPTH = 1
DEC_BATCH = 1
DEC_SEQ = 512
PAST_LEN = 128

GRID_W = 64
CONV_W = 512
CONV_K = 3
RET_HEADS = 4
RET_DK = 128
RET_DV = 128
RET_W = RET_HEADS * RET_DV
MIX_W = CONV_W + RET_W
IN_COLS = 3 * CONV_W + 2 * RET_HEADS * RET_DK + 2 * RET_W
CHUNK = 128
N_GROUPS = 4
EXPERTS_PER_GROUP = 8
N_EXPERTS = N_GROUPS * EXPERTS_PER_GROUP
TOP_K_INNER = 2
D_EXPERT = 256
ROPE_BASE = 10000.0
EPS = 1e-6

kernel_name = "hybrid_conv_retention_hmoe_diffusion_step"

def rmsnorm(x, g):
    xf = x.astype(jnp.float32)
    r = xf * lax.rsqrt(jnp.mean(xf * xf, axis=-1, keepdims=True) + EPS)
    return (r * g.astype(jnp.float32)).astype(x.dtype)

def modulation(cvec, w, b, dtype):
    h = jax.nn.silu(cvec.astype(jnp.float32)) @ w.astype(jnp.float32) + b.astype(jnp.float32)
    h = h.reshape(cvec.shape[0], 1, 6 * D_MODEL).astype(dtype)
    return jnp.split(h, 6, axis=-1)

def conv3(u, w):
    pad = [(0, 0)] * (u.ndim - 2) + [(1, 1), (0, 0)]
    up = jnp.pad(u, pad)
    return w[0] * up[..., :-2, :] + w[1] * up[..., 1:-1, :] + w[2] * up[..., 2:, :]

def grid_rope(L):
    pos = jnp.arange(L)
    row = (pos // GRID_W).astype(jnp.float32)
    col = (pos % GRID_W).astype(jnp.float32)
    n_pairs = RET_DK // 4
    freqs = ROPE_BASE ** (-(jnp.arange(n_pairs, dtype=jnp.float32) * 2.0 / (RET_DK // 2)))
    ang = jnp.concatenate([row[:, None] * freqs, col[:, None] * freqs], axis=-1)
    return jnp.cos(ang), jnp.sin(ang)

def apply_rope(x, cos, sin):
    xe = x[..., 0::2]
    xo = x[..., 1::2]
    return jnp.stack([xe * cos - xo * sin, xe * sin + xo * cos], axis=-1).reshape(x.shape)

def retention_chunked(q, k, v, log_gamma, s0):
    Bsz, H, L, dk = q.shape
    dv = v.shape[-1]
    n = L // CHUNK
    def to_chunks(t):
        return jnp.moveaxis(t.reshape(Bsz, H, n, CHUNK, t.shape[-1]), 2, 0)
    qs, ks, vs = to_chunks(q), to_chunks(k), to_chunks(v)
    idx = jnp.arange(CHUNK, dtype=jnp.float32)
    diff = idx[:, None] - idx[None, :]
    causal = diff >= 0
    lg = log_gamma[:, None, None]
    decay_mask = jnp.where(causal, jnp.exp(jnp.where(causal, diff, 0.0) * lg), 0.0)
    q_decay = jnp.exp((idx + 1.0)[None, :] * log_gamma[:, None])[..., None]
    k_decay = jnp.exp((CHUNK - 1.0 - idx)[None, :] * log_gamma[:, None])[..., None]
    chunk_decay = jnp.exp(CHUNK * log_gamma)[:, None, None]

    def step(S, inp):
        qc, kc, vc = inp
        scores = jnp.einsum('bhid,bhjd->bhij', qc, kc) * decay_mask
        inner = jnp.einsum('bhij,bhje->bhie', scores, vc)
        cross = jnp.einsum('bhid,bhde->bhie', qc * q_decay, S)
        S_new = S * chunk_decay + jnp.einsum('bhjd,bhje->bhde', kc * k_decay, vc)
        return S_new, inner + cross

    S_final, out = lax.scan(step, s0, (qs, ks, vs))
    out = jnp.moveaxis(out, 0, 2).reshape(Bsz, H, L, dv)
    return out, S_final

def mixer(xn, w_in, conv_w, w_out, a_fwd, a_bwd, s_f0, s_b0, is_grid):
    Bsz, L, _ = xn.shape
    proj = xn @ w_in
    qk_w = RET_HEADS * RET_DK
    cuts = [CONV_W, 2 * CONV_W, 3 * CONV_W, 3 * CONV_W + qk_w, 3 * CONV_W + 2 * qk_w, 3 * CONV_W + 2 * qk_w + RET_W]
    gb, gc, h, q, k, v, g = jnp.split(proj, cuts, axis=-1)

    u = gc * h
    if is_grid:
        rows = L // GRID_W
        conv = conv3(u.reshape(Bsz, rows, GRID_W, CONV_W), conv_w).reshape(Bsz, L, CONV_W)
    else:
        conv = conv3(u, conv_w)
    y_conv = gb * conv

    def heads(t, d):
        return t.reshape(Bsz, L, RET_HEADS, d).transpose(0, 2, 1, 3).astype(jnp.float32)
    qh = heads(q, RET_DK)
    kh = heads(k, RET_DK) * (RET_DK ** -0.5)
    vh = heads(v, RET_DV)
    if is_grid:
        cos, sin = grid_rope(L)
        qh = apply_rope(qh, cos, sin)
        kh = apply_rope(kh, cos, sin)
    lg_f = jnp.log1p(-jnp.exp(a_fwd.astype(jnp.float32)))
    lg_b = jnp.log1p(-jnp.exp(a_bwd.astype(jnp.float32)))
    o_f, s_f = retention_chunked(qh, kh, vh, lg_f, s_f0.astype(jnp.float32))
    flip = lambda t: jnp.flip(t, axis=2)
    o_b, s_b = retention_chunked(flip(qh), flip(kh), flip(vh), lg_b, s_b0.astype(jnp.float32))
    o = o_f + flip(o_b)
    o = o * lax.rsqrt(jnp.mean(o * o, axis=-1, keepdims=True) + EPS)
    o = o.transpose(0, 2, 1, 3).reshape(Bsz, L, RET_W).astype(xn.dtype)
    y_ret = jax.nn.silu(g) * o

    out = jnp.concatenate([y_conv, y_ret], axis=-1) @ w_out
    return out, s_f, s_b

def hier_moe(xn, w_rg, b_rg, w_re, b_re, w1, w3, w2):
    Bsz, L, D = xn.shape
    t = xn.reshape(-1, D)
    T = t.shape[0]
    lg_group = (t @ w_rg).astype(jnp.float32) + b_rg.astype(jnp.float32)
    p_group = jax.nn.softmax(lg_group, axis=-1)
    gidx = jnp.argmax(lg_group, axis=-1)
    p_sel = jnp.take_along_axis(p_group, gidx[:, None], axis=-1)[:, 0]
    lg_exp = ((t @ w_re).astype(jnp.float32) + b_re.astype(jnp.float32)).reshape(T, N_GROUPS, EXPERTS_PER_GROUP)
    lg_in = jnp.take_along_axis(lg_exp, gidx[:, None, None], axis=1)[:, 0]
    topv, topi = lax.top_k(lg_in, TOP_K_INNER)
    w_sel = jax.nn.softmax(topv, axis=-1) * p_sel[:, None]
    eidx = gidx[:, None] * EXPERTS_PER_GROUP + topi
    gates = jnp.sum(jax.nn.one_hot(eidx, N_EXPERTS, dtype=jnp.float32) * w_sel[..., None], axis=1)
    gates = gates.astype(t.dtype)

    def expert_step(acc, inp):
        w1e, w3e, w2e, ge = inp
        hid = jax.nn.silu(t @ w1e) * (t @ w3e)
        return acc + ge[:, None] * (hid @ w2e), None

    acc, _ = lax.scan(expert_step, jnp.zeros_like(t), (w1, w3, w2, gates.T))
    return acc.reshape(Bsz, L, D)

def block(x, mod, s_f0, s_b0, is_grid, p):
    (norm_mix_g, norm_ffn_g, w_in, conv_w, a_fwd, a_bwd, w_out,
     w_rg, b_rg, w_re, b_re, w1, w3, w2) = p
    sh1, sc1, g1, sh2, sc2, g2 = mod
    xn = rmsnorm(x, norm_mix_g) * (1 + sc1) + sh1
    m, s_f, s_b = mixer(xn, w_in, conv_w, w_out, a_fwd, a_bwd, s_f0, s_b0, is_grid)
    x = x + g1 * m
    xn = rmsnorm(x, norm_ffn_g) * (1 + sc2) + sh2
    x = x + g2 * hier_moe(xn, w_rg, b_rg, w_re, b_re, w1, w3, w2)
    return x, s_f, s_b

def setup_inputs(seed: int = 0) -> dict:
    key = jax.random.key(seed)
    ks = jax.random.split(key, 24)
    f32 = jnp.float32
    nrm = lambda k, shape, s: jax.random.normal(k, shape, f32) * s
    base_decay = jnp.linspace(math.log(1.0 / 32.0), math.log(1.0 / 512.0), RET_HEADS, dtype=f32)
    st_shape = (DEC_BATCH, DEPTH, RET_HEADS, RET_DK, RET_DV)
    return {
        "x_prompt": nrm(ks[0], (BATCH, SEQ, D_MODEL), 1.0),
        "x_sample": nrm(ks[1], (DEC_BATCH, DEC_SEQ, D_MODEL), 1.0),
        "state_ret_fwd": nrm(ks[2], st_shape, 0.5),
        "state_ret_bwd": nrm(ks[3], st_shape, 0.5),
        "c": nrm(ks[4], (DEC_BATCH, D_MODEL), 1.0),
        "c_ctx": nrm(ks[5], (D_MODEL,), 1.0),
        "norm_mix_g": 1.0 + nrm(ks[6], (DEPTH, D_MODEL), 0.02),
        "norm_ffn_g": 1.0 + nrm(ks[7], (DEPTH, D_MODEL), 0.02),
        "w_ada": nrm(ks[8], (DEPTH, D_MODEL, 6 * D_MODEL), 0.5 * D_MODEL ** -0.5),
        "b_ada": nrm(ks[9], (DEPTH, 6 * D_MODEL), 0.02),
        "w_in": nrm(ks[10], (DEPTH, D_MODEL, IN_COLS), D_MODEL ** -0.5),
        "conv_w": nrm(ks[11], (DEPTH, CONV_K, CONV_W), CONV_K ** -0.5),
        "ret_decay_fwd": base_decay[None, :] + nrm(ks[12], (DEPTH, RET_HEADS), 0.01),
        "ret_decay_bwd": base_decay[None, :] + nrm(ks[13], (DEPTH, RET_HEADS), 0.01),
        "w_out": nrm(ks[14], (DEPTH, MIX_W, D_MODEL), MIX_W ** -0.5),
        "w_router_group": nrm(ks[15], (DEPTH, D_MODEL, N_GROUPS), D_MODEL ** -0.5),
        "b_router_group": nrm(ks[16], (DEPTH, N_GROUPS), 0.01),
        "w_router_expert": nrm(ks[17], (DEPTH, D_MODEL, N_EXPERTS), D_MODEL ** -0.5),
        "b_router_expert": nrm(ks[18], (DEPTH, N_EXPERTS), 0.01),
        "w_gate_e": nrm(ks[19], (DEPTH, N_EXPERTS, D_MODEL, D_EXPERT), D_MODEL ** -0.5),
        "w_up_e": nrm(ks[20], (DEPTH, N_EXPERTS, D_MODEL, D_EXPERT), D_MODEL ** -0.5),
        "w_down_e": nrm(ks[21], (DEPTH, N_EXPERTS, D_EXPERT, D_MODEL), D_EXPERT ** -0.5),
        "final_norm_g": 1.0 + nrm(ks[22], (D_MODEL,), 0.02),
    }

def reference(x_prompt, x_sample, state_ret_fwd, state_ret_bwd, c, c_ctx,
              norm_mix_g, norm_ffn_g, w_ada, b_ada, w_in, conv_w,
              ret_decay_fwd, ret_decay_bwd, w_out,
              w_router_group, b_router_group, w_router_expert, b_router_expert,
              w_gate_e, w_up_e, w_down_e, final_norm_g):
    xp = x_prompt
    xs = x_sample
    new_f = []
    new_b = []
    for l in range(DEPTH):
        p = (norm_mix_g[l], norm_ffn_g[l], w_in[l], conv_w[l], ret_decay_fwd[l], ret_decay_bwd[l], w_out[l],
             w_router_group[l], b_router_group[l], w_router_expert[l], b_router_expert[l],
             w_gate_e[l], w_up_e[l], w_down_e[l])
        mod_ctx = modulation(c_ctx[None, :], w_ada[l], b_ada[l], xp.dtype)
        mod_lat = modulation(c, w_ada[l], b_ada[l], xs.dtype)
        zeros = jnp.zeros((xp.shape[0], RET_HEADS, RET_DK, RET_DV), jnp.float32)
        xp, s_f, s_b = block(xp, mod_ctx, zeros, zeros, False, p)
        xs, _, _ = block(xs, mod_lat, state_ret_fwd[:, l], state_ret_bwd[:, l], True, p)
        new_f.append(s_f)
        new_b.append(s_b)
    y_prompt = rmsnorm(xp, final_norm_g)
    y_sample = rmsnorm(xs, final_norm_g)
    new_state_ret_fwd = jnp.stack(new_f, axis=1).astype(x_prompt.dtype)
    new_state_ret_bwd = jnp.stack(new_b, axis=1).astype(x_prompt.dtype)
    return (y_prompt, y_sample, new_state_ret_fwd, new_state_ret_bwd)


_drawn_inputs = setup_inputs


def setup_inputs(seed=0):
    import zlib

    import numpy as np

    out = dict(_drawn_inputs(seed))
    spreads = {}
    factors = {'state_ret_fwd': 3.157,
     'state_ret_bwd': 3.066,
     'norm_ffn_g': 4.75,
     'b_router_group': 8.0,
     'b_router_expert': 8.0,
     'final_norm_g': 2.825}
    for name, (base, spread) in spreads.items():
        noise = np.random.default_rng([zlib.crc32(name.encode()), seed]).standard_normal(out[name].shape)
        drawn = base * np.exp(spread * noise) if base else spread * noise
        out[name] = __import__('jax').numpy.asarray(drawn.astype(out[name].dtype))
    for name, factor in factors.items():
        out[name] = (out[name] * factor).astype(out[name].dtype)
    return out
```

```python
from contextlib import ExitStack

import numpy as np

import concourse.bass as bass
from concourse import mybir

P = 128
D = 1024
KT = D // P
NT = 5
TOK = NT * P
LAT = TOK - P
GRID_W = 64
CB = 4
HEADS = 4
DH = 128
W = HEADS * DH
SL = 512
EXPERTS = 32
GROUPS = 4
PER_GROUP = 8
DE = 256
BLK = 64
PAIRS = 2 * TOK
OVB = 22
MAX_SPLIT = TOK // BLK - 1
OV_ROW0 = EXPERTS * BLK
ROWS = OV_ROW0 + OVB * BLK
EPS = 1e-6
NSLOT = 4
SLOT = KT * 2 * DE + 2 * D
ADA_FIRST = 4
ADA_ALL = 12
N_IN = 7
IN_ORDER = (1, 2, 0, 3, 4, 5, 6)
FIRST_EXPERT_ITEM = ADA_ALL + N_IN + 2

F32 = mybir.dt.float32
I32 = mybir.dt.int32
ALU = mybir.AluOpType
ACT = mybir.ActivationFunctionType
X = mybir.AxisListType.X

CONSTS = {}


def const_table():
    i = np.arange(P, dtype=np.float64)
    parts = {}
    parts["ident"] = np.eye(P)
    parts["before"] = (i[:, None] < i[None, :]) * 1.0
    parts["ones"] = np.ones((P, 1))
    parts["sel_pair"] = np.stack([i % 32 == 0, i % 32 == 1], 1) * 1.0
    bias = np.zeros((P, ADA_ALL, 32))
    for s in range(ADA_ALL):
        bias[s, s, 0:2] = 1.0
    parts["sel_bias"] = bias.reshape(P, -1)
    parts["k_pos"] = np.stack([P - 1 - i, i], 1)
    bc = lambda row: np.repeat(np.asarray(row, np.float64).reshape(1, -1), P, 0)
    parts["desc_group"] = bc(GROUPS - np.arange(GROUPS))
    parts["desc_inner"] = bc(PER_GROUP - np.arange(PER_GROUP))
    parts["splits"] = bc(BLK * (1 + np.arange(MAX_SPLIT)))
    parts["block_row"] = bc(BLK * np.arange(EXPERTS))
    parts["ov_index"] = bc(np.arange(OVB))
    early = {}
    early["fwd_gap"] = np.maximum(i[None, :] - i[:, None], 0)
    early["bwd_gap"] = np.maximum(i[:, None] - i[None, :], 0)
    early["fwd_on"] = (i[None, :] >= i[:, None]) * 1.0
    early["bwd_on"] = (i[:, None] >= i[None, :]) * 1.0
    early["q_pos_f"] = bc(i + 1)
    early["q_pos_b"] = bc(P - i)
    pos = np.arange(LAT)
    pairs = DH // 4
    freqs = (10000.0 ** (-(np.arange(pairs, dtype=np.float32) * 2.0 / (DH // 2)))).astype(np.float32)
    ang = np.concatenate([(pos // GRID_W).astype(np.float32)[:, None] * freqs,
                          (pos % GRID_W).astype(np.float32)[:, None] * freqs], -1)
    cos, sin = np.cos(ang.astype(np.float64)), np.sin(ang.astype(np.float64))
    c2 = np.repeat(cos, 2, 1)
    s2 = np.stack([-sin, sin], -1).reshape(LAT, DH)
    chunked = lambda a: a.reshape(LAT // P, P, DH).transpose(1, 0, 2).reshape(P, -1)
    rope = np.concatenate([chunked(c2), chunked(s2)], 1)
    at = 0
    for name, a in parts.items():
        CONSTS[name] = (at, at + a.shape[1])
        at += a.shape[1]
    at = 0
    for name, a in early.items():
        CONSTS[name] = (at, at + a.shape[1])
        at += a.shape[1]
    pack = lambda d: np.ascontiguousarray(np.concatenate(list(d.values()), 1).astype(np.float32))
    return pack(parts), pack(early), np.ascontiguousarray(rope.astype(np.float32))


def layer(nc, a, y_prompt, y_sample, new_f, new_b):
    kept_w = a["c_kept"].shape[1]
    early_w = a["c_early"].shape[1]
    xs_rows = nc.dram_tensor("expert_in_rows", (ROWS, D), F32, kind="Internal").ap()
    y_rows = nc.dram_tensor("expert_out_rows", (ROWS, D), F32, kind="Internal").ap()

    with ExitStack() as ctx:
        def sb(name, shape, dt=F32):
            return ctx.enter_context(nc.sbuf_tensor(name, shape, dt))

        def sem(name):
            return ctx.enter_context(nc.semaphore(name))

        bank = [ctx.enter_context(nc.psum_tensor(f"bank{b}", [P, SL], F32)) for b in range(8)]

        ring = sb("ring", [P, NSLOT, SLOT])
        x = sb("x", [P, NT, D])
        kept = sb("kept", [P, kept_w])
        cs = sb("cs", [P, KT, 32])
        cvec = sb("cvec", [P, 2, KT])
        b_ada = sb("b_ada_rows", [ADA_ALL, SL])
        modsum = sb("modsum", [P, SL])
        shift = sb("shift", [P, KT, 2])
        scale = sb("scale", [P, KT, 2])
        g_mix = sb("g_mix", [P, KT])
        conv_w = sb("conv_taps", [P, 3, CB])
        decay = sb("decay", [P, 6, 8])
        kdec = sb("kdec", [P, 2, HEADS])
        cdec = sb("cdec", [P, 2, HEADS])
        tail = [ring[:, s, KT * SL:SLOT] for s in range(NSLOT)]
        mask = tail[0][:, 0:512].rearrange("p (h n) -> p h n", h=HEADS)
        qdec = tail[0][:, 512:1536].rearrange("p (d h n) -> p d h n", d=2, h=HEADS)
        rope = tail[1][:, 0:1024].rearrange("p (d c n) -> p d c n", d=2, c=4)
        state_c = tail[1][:, 1024:2048].rearrange("p (d n) -> p d n", d=2)
        stat = sb("stat", [P, 4, NT])
        hstat = sb("hstat", [P, 3, HEADS])
        w_router = sb("w_router", [P, KT, GROUPS + EXPERTS])
        b_router = sb("b_router", [P, GROUPS + EXPERTS])
        logits = sb("logits", [P, NT, GROUPS + EXPERTS])

        arena_a = sb("arena_a", [P, KT * TOK])
        arena_b = sb("arena_b", [P, 4 * NT * W])
        arena_c = sb("arena_c", [P, CB * TOK])
        arena_d = sb("arena_d", [P, CB * TOK])

        def k(name):
            lo, hi = CONSTS[name]
            return kept[:, lo:hi]

        ident = k("ident")

        xnT = arena_a[:, :].rearrange("p (k t) -> p k t", k=KT)
        q = arena_b[:, 0:2560].rearrange("p (t n) -> p t n", t=NT)
        kk = arena_b[:, 2560:5120].rearrange("p (t n) -> p t n", t=NT)
        v = arena_b[:, 5120:7680].rearrange("p (t n) -> p t n", t=NT)
        gate = arena_b[:, 7680:10240].rearrange("p (t n) -> p t n", t=NT)
        xs = arena_b[:, 0:2048].rearrange("p (b n) -> p b n", b=2)
        early = arena_b[:, 2560:2560 + early_w]
        decay_tmp = arena_b[:, 5120:6144].rearrange("p (b h n) -> p b h n", b=2, h=HEADS)
        zeros = arena_b[:, 7680:8704]
        u = arena_c[:, :].rearrange("p (m t) -> p m t", m=CB)
        yconvT = arena_d[:, :].rearrange("p (m t) -> p m t", m=CB)
        rope_tmp = arena_c[:, 0:1024].rearrange("p (b n) -> p b n", b=2)

        def e(name):
            lo, hi = CONSTS[name]
            return early[:, lo:hi]

        yretT = arena_a[:, 0:2560].rearrange("p (m t) -> p m t", m=CB)
        sbk = arena_a[:, 2560:4608].rearrange("p (c n) -> p c n", c=4)
        sfw = arena_a[:, 4608:5120]
        qT, kT, qTf, qTb, sm = (arena_c[:, 512 * n:512 * n + 512] for n in range(5))
        kd = rope[:, 0, :, :].rearrange("p c n -> p (c n)")

        rows = arena_b[:, 0:8192].rearrange("p (c s n) -> p c s n", c=4, s=2)
        xn2T = arena_b[:, 8192:10240].rearrange("p (b k t) -> p b k t", b=2, k=KT)
        xn2 = arena_a[:, :].rearrange("p (t n) -> p t n", t=NT)
        part = arena_c[:, 0:512]
        square = arena_c[:, 512:1536]
        g_ffn = arena_c[:, 1536:2560]

        rt = arena_d[:, :]

        xe = arena_c[:, 0:2048].rearrange("p (b n) -> p b n", b=2)
        xeT = arena_d[:, 0:2048].rearrange("p (b k s) -> p b k s", b=2, k=KT)
        sgate = arena_b[:, 9216:9728].rearrange("p (b n) -> p b n", b=2)
        hid = arena_b[:, 9728:10240].rearrange("p (b n) -> p b n", b=2)
        hidT = arena_d[:, 2048:2304].rearrange("p (b c s) -> p b c s", b=2, c=2)
        ysb = arena_b[:, 8192:9216].rearrange("p (b n) -> p b n", b=2)
        posi = sb("posi", [P, NT, 2], I32)
        wsel = sb("wsel", [P, NT, 2])
        ov_tab = sb("ov_tab", [P, OVB + 1], I32)

        got = ring[:, :, :].rearrange("p s n -> p (s n)")[:, 0:4 * D].rearrange("p (b j n) -> p b j n", b=2, j=2)
        outb = ring[:, :, :].rearrange("p s n -> p (s n)")[:, 4 * D:6 * D].rearrange("p (b n) -> p b n", b=2)
        sq7 = ring[:, :, :].rearrange("p s n -> p (s n)")[:, 6 * D:7 * D]
        g_fin = arena_a[:, 0:D]

        ring_in = [sem(f"ring_in{s}") for s in range(NSLOT)]
        c_in, kept_in, x_in, small_in = sem("c_in"), sem("kept_in"), sem("x_in"), sem("small_in")
        state_in, gffn_in, gfin_in = sem("state_in"), sem("gffn_in"), sem("gfin_in")
        cs_zero, cs_ready = sem("cs_zero"), sem("cs_ready")
        mod_mm, mod_ev, modsel_mm, modcol_mm, row_ready = (sem(n) for n in (
            "mod_mm", "mod_ev", "modsel_mm", "modcol_mm", "row_ready"))
        col_ready = sem("col_ready")
        ssq_done, ms_done, root_done, rstd_done = (sem(n) for n in ("ssq_done", "ms_done", "root_done", "rstd_done"))
        xs_ready, xT_mm, xT_act, xT_dve = (sem(n) for n in ("xs_ready", "xT_mm", "xT_act", "xT_dve"))
        dec_e, dec_u, dec_ln, dec_lg, dec_act, dec_done = (sem(n) for n in (
            "dec_e", "dec_u", "dec_ln", "dec_lg", "dec_act", "dec_done"))
        zero_set, zero_out = sem("zero_set"), sem("zero_out")
        proj_mm, conv_c_ev, conv_h_ev, conv_b_ev = (sem(n) for n in ("proj_mm", "conv_c_ev", "conv_h_ev", "conv_b_ev"))
        qkvg_ev, rope_done = sem("qkvg_ev"), sem("rope_done")
        kd_ready, st_mm, st_ready, new_out = sem("kd_ready"), sem("st_mm"), sem("st_ready"), sem("new_out")
        qkT_mm, kT_ev, qT_ev, sc_mm, sm_ready, o_mm = (sem(n) for n in (
            "qkT_mm", "kT_ev", "qT_ev", "sc_mm", "sm_ready", "o_mm"))
        osq_done, oms_done, oroot_done, yr_ready, yT_mm, yT_ev = (sem(n) for n in (
            "osq_done", "oms_done", "oroot_done", "yr_ready", "yT_mm", "yT_ev"))
        wout_mm, x1_ready = sem("wout_mm"), sem("x1_ready")
        ssq2_done, ms2_done, root2_done, xn2_ready, xn2T_mm, xn2T_ev, rt_mm, lg_ready = (sem(n) for n in (
            "ssq2_done", "ms2_done", "root2_done", "xn2_ready", "xn2T_mm", "xn2T_ev", "rt_mm", "lg_ready"))
        exp_in, exp_out, chosen, rank_mm, routed, xs_out = (sem(n) for n in (
            "exp_in", "exp_out", "chosen", "rank_mm", "routed", "xs_out"))
        xe_in = [sem("xe_in0"), sem("xe_in1")]
        xe_mm, xe_ready, gu_mm, silu_done, hid_done, ht_mm, ht_ready, down_mm, y_ev = (sem(n) for n in (
            "xe_mm", "xe_ready", "gu_mm", "silu_done", "hid_done", "ht_mm", "ht_ready", "down_mm", "y_ev"))
        y_out = [sem("y_out0"), sem("y_out1")]
        y_all = sem("y_all")
        got_in = [sem("got_in0"), sem("got_in1")]
        x2_ready, ssq3_done, ms3_done, root3_done, out_ready = (sem(n) for n in (
            "x2_ready", "ssq3_done", "ms3_done", "root3_done", "out_ready"))
        stored = [sem("stored0"), sem("stored1")]
        step = sem("dve_step")

        ada_v = a["w_ada"][0].rearrange("(p k) n -> p k n", k=KT)
        win_v = a["w_in"][0].rearrange("(p k) n -> p k n", k=KT)
        wout_v = a["w_out"][0].rearrange("(k p) n -> p k n", p=P)

        items = ([("ada", s) for s in range(ADA_FIRST)] + [("in", s) for s in range(N_IN)]
                 + [("ada", s) for s in range(ADA_FIRST, ADA_ALL)] + [("out", s) for s in range(2)])
        assert len(items) == FIRST_EXPERT_ITEM

        def proj_groups(n):
            return CB * min(n, 3) + NT * max(n - 3, 0)

        def slot_of(item):
            return item % NSLOT

        def landed(eng, item):
            eng.wait_ge(ring_in[slot_of(item)], 16 * (item // NSLOT + 1))

        def wide(item):
            return ring[:, slot_of(item), 0:KT * SL].rearrange("p (k n) -> p k n", k=KT)

        early_uses = [sum(1 for n in range(FIRST_EXPERT_ITEM) if n % NSLOT == s) for s in range(NSLOT)]
        e_slot = [(FIRST_EXPERT_ITEM + j) % NSLOT for j in range(NSLOT)]

        def w_gate(s):
            return ring[:, s, 0:KT * DE].rearrange("p (k n) -> p k n", k=KT)

        def w_up(s):
            return ring[:, s, KT * DE:2 * KT * DE].rearrange("p (k n) -> p k n", k=KT)

        def w_down(s):
            return ring[:, s, 2 * KT * DE:SLOT].rearrange("p (h n) -> p h n", h=2)

        def released(eng, item):
            kind, s = items[item]
            if kind == "ada":
                eng.wait_ge(mod_mm, s + 1)
            elif kind == "in":
                eng.wait_ge(proj_mm, proj_groups(s + 1))
            else:
                eng.wait_ge(wout_mm, NT * (s + 1))

        block = ctx.enter_context(nc.Block())

        @block.sync
        def _(sp):
            sp.dma_start(kept[:, :], a["c_kept"]).then_inc(kept_in, 16)

            def expert_weights(s, gate_src, up_src, down_src):
                sp.dma_start(w_gate(s), gate_src).then_inc(ring_in[s], 16)
                sp.dma_start(w_up(s), up_src).then_inc(ring_in[s], 16)
                sp.dma_start(w_down(s), down_src).then_inc(ring_in[s], 16)

            for n, (kind, s) in enumerate(items):
                if n >= NSLOT:
                    released(sp, n - NSLOT)
                if kind == "ada":
                    src = ada_v[:, :, SL * s:SL * s + SL]
                elif kind == "in":
                    src = win_v[:, :, SL * IN_ORDER[s]:SL * IN_ORDER[s] + SL]
                else:
                    src = wout_v[:, :, SL * s:SL * s + SL]
                sp.dma_start(wide(n), src).then_inc(ring_in[slot_of(n)], 16)
            sp.wait_ge(new_out, 32)
            gv = a["w_gate_e"][0].rearrange("e (p k) n -> e p k n", k=KT)
            uv = a["w_up_e"][0].rearrange("e (p k) n -> e p k n", k=KT)
            dv = a["w_down_e"][0].rearrange("e (p h) n -> e p h n", h=2)
            for j in range(NSLOT):
                released(sp, FIRST_EXPERT_ITEM + j - NSLOT)
                expert_weights(e_slot[j], gv[j], uv[j], dv[j])
            with sp.Fori(1, EXPERTS // NSLOT) as i:
                for j in range(NSLOT):
                    sp.wait_ge(down_mm, i * NSLOT + (j + 1 - NSLOT))
                    ex = bass.ds(i * NSLOT + j, 1)
                    expert_weights(e_slot[j], gv[ex].rearrange("e p k n -> (e p) k n"),
                                   uv[ex].rearrange("e p k n -> (e p) k n"),
                                   dv[ex].rearrange("e p h n -> (e p) h n"))
            sp.wait_ge(routed, 1)
            count = sp.value_load(ov_tab[0:1, OVB:OVB + 1], min_val=0, max_val=OVB // 2 - 1)
            with sp.If(count > 0):
                with sp.Fori(0, count) as m:
                    for j in range(2):
                        sp.wait_ge(down_mm, m * 2 + (EXPERTS - 1 + j))
                        who = sp.value_load(ov_tab[0:1, bass.ds(m * 2 + j, 1)], min_val=0, max_val=EXPERTS - 1)
                        ex = bass.ds(who, 1)
                        expert_weights(e_slot[j], gv[ex].rearrange("e p k n -> (e p) k n"),
                                       uv[ex].rearrange("e p k n -> (e p) k n"),
                                       dv[ex].rearrange("e p h n -> (e p) h n"))
            sp.wait_ge(y_out[0], count * 32 + 32 * (1 + EXPERTS // 2))
            sp.wait_ge(y_out[1], count * 32 + 32 * (1 + EXPERTS // 2))
            sp.sem_inc(y_all, 1)
            for t in range(NT):
                sp.wait_ge(out_ready, t + 1)
                dst = y_prompt[0] if t == 0 else y_sample[0, P * (t - 1):P * t, :]
                sp.dma_start(dst, outb[:, t % 2, :]).then_inc(stored[t % 2], 16)
            sp.wait_ge(stored[0], 16 * 3)
            sp.wait_ge(stored[1], 16 * 2)

        @block.gpsimd
        def _(pool):
            pool.dma_start(tail[1][:, 0:1024], a["c_rope"]).then_inc(small_in, 16)
            pool.dma_start(g_mix[:, :], a["norm_mix_g"][0].rearrange("(p k) -> p k", k=KT)).then_inc(small_in, 16)
            for tap in range(3):
                pool.dma_start(conv_w[:, tap, :], a["conv_w"][0, tap].rearrange("(m p) -> p m", p=P),
                               allow_slow_non_contiguous=True).then_inc(small_in, 16)
            pool.dma_start(w_router[:, :, 0:GROUPS],
                           a["w_router_group"][0].rearrange("(p k) n -> p k n", k=KT)).then_inc(small_in, 16)
            pool.dma_start(w_router[:, :, GROUPS:],
                           a["w_router_expert"][0].rearrange("(p k) n -> p k n", k=KT)).then_inc(small_in, 16)
            pool.dma_start(b_router[:, 0:GROUPS], a["b_router_group"].partition_broadcast(P)).then_inc(small_in, 16)
            pool.dma_start(b_router[:, GROUPS:], a["b_router_expert"].partition_broadcast(P)).then_inc(small_in, 16)
            pool.wait_ge(zero_set, 1)
            pool.wait_ge(ring_in[1], 32)
            zin = zeros.rearrange("p (a n) -> p a n", a=1)
            pool.dma_start(xs_rows.rearrange("(a p) n -> p a n", p=P),
                           zin.broadcast_to([P, ROWS // P, D])).then_inc(zero_out, 16)
            pool.dma_start(y_rows[OV_ROW0:, :].rearrange("(a p) n -> p a n", p=P),
                           zin.broadcast_to([P, OVB * BLK // P, D])).then_inc(zero_out, 16)
            pool.wait_ge(proj_mm, proj_groups(N_IN))
            pool.dma_start(sbk[:, 3, :].rearrange("p (h n) -> p h n", h=HEADS),
                           a["state_ret_bwd"][0, 0].rearrange("h d e -> d h e")).then_inc(state_in, 16)
            pool.dma_start(sfw.rearrange("p (h n) -> p h n", h=HEADS),
                           a["state_ret_fwd"][0, 0].rearrange("h d e -> d h e")).then_inc(state_in, 16)
            pool.wait_ge(st_ready, 5)
            for d, dst in enumerate((new_f, new_b)):
                pool.dma_start(dst[0, 0].rearrange("h d e -> d h e"),
                               state_c[:, d, :].rearrange("p (h n) -> p h n", h=HEADS)).then_inc(new_out, 16)
            pool.wait_ge(o_mm, NT)
            pool.wait_ge(sm_ready, NT)
            pool.dma_start(g_ffn, a["norm_ffn_g"].partition_broadcast(P)).then_inc(gffn_in, 16)
            pool.wait_ge(zero_out, 32)
            pool.wait_ge(routed, 1)
            for t in range(NT):
                for j in range(2):
                    pool.indirect_dma_start(xs_rows, bass.IndirectOffsetOnAxis(ap=posi[:, t, j:j + 1], axis=0),
                                            xn2[:, t, :], None).then_inc(xs_out, 16)
            pool.wait_ge(xs_out, 16 * 2 * NT)
            pool.dma_start(g_fin, a["final_norm_g"].partition_broadcast(P)).then_inc(gfin_in, 16)
            pool.wait_ge(y_all, 1)
            for t in range(NT):
                if t >= 2:
                    pool.wait_ge(x2_ready, t - 1)
                for j in range(2):
                    pool.indirect_dma_start(got[:, t % 2, j, :], None, y_rows,
                                            bass.IndirectOffsetOnAxis(ap=posi[:, t, j:j + 1], axis=0)).then_inc(got_in[t % 2], 16)

        @block.scalar
        def _(act):
            act.dma_start(cvec[:, 0, :], a["c_ctx"].rearrange("(p k) -> p k", k=KT)).then_inc(c_in, 16)
            act.dma_start(cvec[:, 1, :], a["c"][0].rearrange("(p k) -> p k", k=KT)).then_inc(c_in, 16)
            act.dma_start(decay[:, 0, 0:4], a["ret_decay_fwd"].partition_broadcast(P)).then_inc(c_in, 16)
            act.dma_start(decay[:, 0, 4:8], a["ret_decay_bwd"].partition_broadcast(P)).then_inc(c_in, 16)
            act.dma_start(b_ada[:, :], a["b_ada"].rearrange("a (s n) -> (a s) n", n=SL)).then_inc(c_in, 16)
            act.dma_start(early, a["c_early"]).then_inc(c_in, 16)
            act.dma_start(x[:, 0, :], a["x_prompt"][0]).then_inc(x_in, 16)
            act.dma_start(x[:, 1:, :], a["x_sample"][0].rearrange("(t p) n -> p t n", p=P)).then_inc(x_in, 16)
            act.wait_ge(c_in, 96)
            act.wait_ge(cs_zero, 1)
            for s in range(2):
                act.activation(cs[:, :, s], cvec[:, s, :], ACT.Silu).then_inc(cs_ready, 1)
            act.activation(decay[:, 1, :], decay[:, 0, :], ACT.Exp).then_inc(dec_e, 1)
            act.wait_ge(dec_u, 1)
            act.activation(decay[:, 3, :], decay[:, 2, :], ACT.Ln).then_inc(dec_ln, 1)
            act.wait_ge(dec_lg, 1)
            for h in range(HEADS):
                act.activation(decay_tmp[:, 0, h, :], e("fwd_gap"), ACT.Exp, scale=decay[:, 5, h:h + 1])
                act.activation(decay_tmp[:, 1, h, :], e("bwd_gap"), ACT.Exp, scale=decay[:, 5, 4 + h:5 + h])
                act.activation(qdec[:, 0, h, :], e("q_pos_f"), ACT.Exp, scale=decay[:, 5, h:h + 1])
                act.activation(qdec[:, 1, h, :], e("q_pos_b"), ACT.Exp, scale=decay[:, 5, 4 + h:5 + h])
            for d in range(2):
                act.activation(cdec[:, d, :], decay[:, 5, 4 * d:4 * d + 4], ACT.Exp, scale=float(P))
                if d == 0:
                    act.wait_ge(kept_in, 16)
                last = act.activation(kdec[:, d, :], decay[:, 5, 4 * d:4 * d + 4], ACT.Exp, scale=k("k_pos")[:, d:d + 1])
            last.then_inc(dec_act, 1)
            act.wait_ge(x_in, 32)
            for t in range(NT):
                if t >= 2:
                    act.wait_ge(ssq_done, t - 1)
                act.activation(xs[:, t % 2, :], x[:, t, :], ACT.Square, accum_out=stat[:, 0, t:t + 1]).then_inc(ssq_done, 1)
            act.wait_ge(ms_done, 1)
            act.activation(stat[:, 2, :], stat[:, 1, :], ACT.Sqrt).then_inc(root_done, 1)
            act.wait_ge(rstd_done, 1)
            act.wait_ge(ssq_done, NT)

            def xT_evacuate(t):
                act.wait_ge(col_ready, 2)
                act.wait_ge(xT_mm, 2 * t + 2)
                s = 0 if t == 0 else 1
                for c in range(4):
                    last = act.activation(xnT[:, 4 + c, P * t:P * t + P], bank[5 + 2 * (t % 2)][:, P * c:P * c + P],
                                          ACT.Identity, scale=scale[:, 4 + c, s:s + 1], bias=shift[:, 4 + c, s:s + 1])
                last.then_inc(xT_act, 1)

            for t in range(NT):
                if t >= 2:
                    act.wait_ge(xT_mm, 2 * (t - 1))
                act.activation(xs[:, t % 2, :].rearrange("p (k q) -> p q k", q=P),
                               x[:, t, :].rearrange("p (q k) -> p q k", q=P), ACT.Copy,
                               scale=stat[:, 3, t:t + 1]).then_inc(xs_ready, 1)
                if t >= 1:
                    xT_evacuate(t - 1)
            xT_evacuate(NT - 1)
            for m in range(CB):
                act.wait_ge(proj_mm, m + 1)
                act.activation(u[:, m, 0:P], bank[2 + m % 2][:, 0:P], ACT.Copy)
                act.activation(u[:, m, P:], bank[m % 2][:, :], ACT.Copy).then_inc(conv_c_ev, 1)
            for n in range(4 * NT):
                s, t = n // NT, n % NT
                act.wait_ge(proj_mm, proj_groups(3) + n + 1)
                src = bank[4 + n % 4][:, :]
                if s == 0:
                    ins = act.activation(q[:, t, :], src, ACT.Copy)
                elif s == 1:
                    ins = act.activation(kk[:, t, :], src, ACT.Copy, scale=float(DH) ** -0.5)
                elif s == 2:
                    ins = act.activation(v[:, t, :], src, ACT.Copy)
                else:
                    if t == 0:
                        act.wait_ge(zero_out, 32)
                    ins = act.activation(gate[:, t, :], src, ACT.Silu)
                ins.then_inc(qkvg_ev, 1)
            for t in range(NT):
                act.wait_ge(qkT_mm, t + 1)
                if t >= 1:
                    act.wait_ge(sc_mm, t)
                act.activation(kT, bank[1][:, :], ACT.Copy).then_inc(kT_ev, 1)
                act.wait_ge(o_mm, t + 1)
                act.activation(q[:, t, :], bank[3][:, :], ACT.Square).then_inc(osq_done, 1)
                act.wait_ge(oms_done, t + 1)
                act.activation(hstat[:, 1, :], hstat[:, 0, :], ACT.Sqrt).then_inc(oroot_done, 1)
                act.wait_ge(yT_mm, t + 1)
                act.activation(yretT[:, :, P * t:P * t + P], bank[5][:, :].rearrange("p (m t) -> p m t", m=CB),
                               ACT.Copy).then_inc(yT_ev, 1)
            for t in range(NT):
                act.wait_ge(x1_ready, NT + t + 1)
                if t >= 1:
                    act.wait_ge(ssq2_done, t)
                act.activation(square, x[:, t, :], ACT.Square, accum_out=stat[:, 0, t:t + 1]).then_inc(ssq2_done, 1)
                act.wait_ge(ms2_done, t + 1)
                act.activation(stat[:, 2, t:t + 1], stat[:, 1, t:t + 1], ACT.Sqrt).then_inc(root2_done, 1)
                act.wait_ge(xn2T_mm, t + 1)
                if t >= 2:
                    act.wait_ge(rt_mm, t - 1)
                for half in range(2):
                    last = act.activation(xn2T[:, t % 2, 4 * half:4 * half + 4, :],
                                          bank[4 + half][:, :].rearrange("p (k t) -> p k t", k=4), ACT.Copy)
                last.then_inc(xn2T_ev, 1)
            act.wait_ge(exp_in, 1)
            act.activation(rt[:, 40:60], rt[:, 20:40], ACT.Exp).then_inc(exp_out, 1)
            act.wait_ge(exp_in, 2)
            act.activation(rt[:, 65:70], rt[:, 60:65], ACT.Exp).then_inc(exp_out, 1)

            def load_rows(p_, at):
                act.dma_start(xe[:, p_, :], xs_rows[bass.ds(at, P), :]).then_inc(xe_in[p_], 16)

            act.sem_inc(y_out[0], 32)
            act.sem_inc(y_out[1], 32)
            act.sem_inc(y_ev, 2)
            act.wait_ge(xs_out, 16 * 2 * NT)
            act.wait_ge(ssq2_done, NT)
            act.wait_ge(xn2_ready, NT)
            for n in range(2):
                act.dma_start(xe[:, n, :], xs_rows[P * n:P * n + P, :]).then_inc(xe_in[n], 16)

            def silu(n, p_):
                act.wait_ge(gu_mm, n + 1)
                act.activation(sgate[BLK:2 * BLK, p_, :], bank[2 + p_][0:BLK, 0:DE], ACT.Silu).then_inc(silu_done, 1)

            def results(n, p_, stored_before):
                act.wait_ge(ht_mm, n + 1)
                act.activation(hidT[:, p_, :, :], bank[4 + p_][:, 0:2 * BLK].rearrange("p (c s) -> p c s", c=2),
                               ACT.Copy).then_inc(ht_ready, 1)
                act.wait_ge(down_mm, n + 1)
                act.wait_ge(y_out[p_], stored_before)
                act.activation(ysb[:, p_, :], bank[6 + p_][:, :], ACT.Copy).then_inc(y_ev, 1)
                act.wait_ge(y_ev, n + 3)
                for half in range(2):
                    act.dma_start(y_rows[bass.ds(n * BLK, BLK), SL * half:SL * half + SL],
                                  ysb[BLK * half:BLK * half + BLK, p_, :]).then_inc(y_out[p_], 16)

            with act.Fori(0, EXPERTS // NSLOT) as i:
                for j in range(NSLOT):
                    n = i * NSLOT + j
                    silu(n, j % 2)
                    if j % 2 == 0:
                        load_rows(j // 2, n * BLK + 2 * P)
                    results(n, j % 2, i * (32 * NSLOT // 2) + 32 * (1 + j // 2))
            act.wait_ge(routed, 1)
            count = act.value_load(ov_tab[0:1, OVB:OVB + 1], min_val=0, max_val=OVB // 2 - 1)
            with act.If(count > 0):
                with act.Fori(0, count) as m:
                    act.wait_ge(xe_mm, m * 2 + (EXPERTS + 2))
                    load_rows(0, m * P + (EXPERTS // 2 + 1) * P)
                    for j in range(2):
                        silu(m * 2 + (EXPERTS + j), j)
                    for j in range(2):
                        results(m * 2 + (EXPERTS + j), j, m * 32 + 32 * (1 + EXPERTS // 2))
            act.wait_ge(xe_in[0], 16 * (EXPERTS // 4 + 1))
            act.wait_ge(xe_in[1], 16 * (EXPERTS // 4 + 1))
            for t in range(NT):
                act.wait_ge(x2_ready, t + 1)
                if t >= 1:
                    act.wait_ge(ssq3_done, t)
                act.activation(sq7, x[:, t, :], ACT.Square, accum_out=stat[:, 0, t:t + 1]).then_inc(ssq3_done, 1)
                act.wait_ge(ms3_done, t + 1)
                act.activation(stat[:, 2, t:t + 1], stat[:, 1, t:t + 1], ACT.Sqrt).then_inc(root3_done, 1)

        @block.tensor
        def _(pe):
            def mod_slice(s, item, out):
                landed(pe, item)
                w = wide(item)
                pe.matmul(out[0:32, :], k("sel_bias")[0:ADA_ALL, 32 * s:32 * s + 32], b_ada[:, :], start=True, stop=False)
                for kt in range(KT):
                    j = kt % 4
                    last = pe.matmul(out[32 * j:32 * j + 32, :], cs[:, kt, :], w[:, kt, :],
                                     start=(0 < kt < 4), stop=(kt >= 4))
                last.then_inc(mod_mm, 1)

            pe.wait_ge(kept_in, 16)
            pe.wait_ge(c_in, 96)
            pe.wait_ge(cs_ready, 2)
            for s in range(ADA_FIRST):
                if s >= 2:
                    pe.wait_ge(mod_ev, s - 1)
                mod_slice(s, s, bank[s % 2])
                pe.wait_ge(mod_ev, s + 1)
                half = s % 2
                ms = modsum[:, :].rearrange("p (q k) -> p k q", k=KT)
                for kt in range(KT):
                    last = pe.matmul(bank[2 + s // 2][64 * half:64 * half + 64, 2 * kt:2 * kt + 2], ms[:, kt, :],
                                     k("sel_pair"), start=True, stop=True)
                last.then_inc(modcol_mm, 1)
            for t in range(NT):
                pe.wait_ge(xs_ready, t + 1)
                if t >= 2:
                    pe.wait_ge(xT_dve, t - 1)
                    pe.wait_ge(xT_act, t - 1)
                for half in range(2):
                    for c in range(4):
                        kt = 4 * half + c
                        last = pe.transpose(bank[4 + 2 * (t % 2) + half][:, P * c:P * c + P],
                                            xs[:, t % 2, P * kt:P * kt + P], ident)
                    last.then_inc(xT_mm, 1)
            pe.wait_ge(xT_dve, NT)
            pe.wait_ge(xT_act, NT)
            for n in range(3 * CB):
                s, m = n // CB, n % CB
                if m == 0:
                    landed(pe, ADA_FIRST + s)
                if n >= 2:
                    done = (conv_c_ev, conv_h_ev, conv_b_ev)[(n - 2) // CB]
                    pe.wait_ge(done, (n - 2) % CB + 1)
                w = wide(ADA_FIRST + s)
                for kt in range(KT):
                    pe.matmul(bank[n % 2][:, :], w[:, kt, P * m:P * m + P], xnT[:, kt, P:], start=(kt == 0), stop=(kt == KT - 1))
                for kt in range(KT):
                    last = pe.matmul(bank[2 + n % 2][:, 0:P], w[:, kt, P * m:P * m + P], xnT[:, kt, 0:P],
                                     start=(kt == 0), stop=(kt == KT - 1))
                last.then_inc(proj_mm, 1)
            for n in range(4 * NT):
                s, t = n // NT, n % NT
                if t == 0:
                    landed(pe, ADA_FIRST + 3 + s)
                if n >= 4:
                    pe.wait_ge(qkvg_ev, n - 3)
                w = wide(ADA_FIRST + 3 + s)
                for kt in range(KT):
                    last = pe.matmul(bank[4 + n % 4][:, :], xnT[:, kt, P * t:P * t + P], w[:, kt, :],
                                     start=(kt == 0), stop=(kt == KT - 1))
                last.then_inc(proj_mm, 1)
            pe.wait_ge(qkvg_ev, 4 * NT)
            pe.wait_ge(rope_done, 8)
            pe.wait_ge(conv_b_ev, CB)
            pe.wait_ge(dec_done, 1)

            def state_update(c, n):
                pe.wait_ge(kd_ready, n + 1)
                if n >= 1:
                    pe.wait_ge(st_ready, n)
                for h in range(HEADS):
                    last = pe.matmul(bank[4][:, DH * h:DH * h + DH], kd[:, DH * h:DH * h + DH], v[:, c, DH * h:DH * h + DH],
                                     start=True, stop=True)
                last.then_inc(st_mm, 1)

            for n, c in enumerate((4, 3, 2)):
                state_update(c, n)
            for t in range(NT):
                if t >= 1:
                    pe.wait_ge(kT_ev, t)
                    pe.wait_ge(qT_ev, t)
                for h in range(HEADS):
                    pe.transpose(bank[0][:, P * h:P * h + P], q[:, t, DH * h:DH * h + DH], ident)
                for h in range(HEADS):
                    last = pe.transpose(bank[1][:, P * h:P * h + P], kk[:, t, DH * h:DH * h + DH], ident)
                last.then_inc(qkT_mm, 1)
                pe.wait_ge(kT_ev, t + 1)
                pe.wait_ge(qT_ev, t + 1)
                if t >= 1:
                    pe.wait_ge(sm_ready, t)
                for h in range(HEADS):
                    last = pe.matmul(bank[2][:, P * h:P * h + P], kT[:, P * h:P * h + P], qT[:, P * h:P * h + P],
                                     start=True, stop=True)
                last.then_inc(sc_mm, 1)
                if t == 0:
                    state_update(0, 3)
                    state_update(0, 4)
                if t >= 2:
                    pe.wait_ge(st_ready, 5 + t - 1)
                pe.wait_ge(sm_ready, t + 1)
                if t >= 1:
                    pe.wait_ge(yr_ready, t)
                    pe.wait_ge(state_in, 32)
                for h in range(HEADS):
                    cols = slice(DH * h, DH * h + DH)
                    last = pe.matmul(bank[3][:, cols], sm[:, cols], v[:, t, cols], start=True, stop=(t == 0))
                    if t >= 1:
                        pe.matmul(bank[3][:, cols], qTf[:, cols], sfw[:, cols], start=False, stop=False)
                        last = pe.matmul(bank[3][:, cols], qTb[:, cols], sbk[:, t - 1, cols], start=False, stop=True)
                last.then_inc(o_mm, 1)
                if 1 <= t <= 3:
                    state_update(t, 4 + t)
                pe.wait_ge(yr_ready, t + 1)
                for h in range(HEADS):
                    last = pe.transpose(bank[5][:, P * h:P * h + P], q[:, t, DH * h:DH * h + DH], ident)
                last.then_inc(yT_mm, 1)
                pe.wait_ge(yT_ev, t + 1)
            for s in range(ADA_FIRST, ADA_ALL):
                n = s - ADA_FIRST
                mod_slice(s, N_IN + s, bank[6 + s % 2])
                pe.wait_ge(mod_ev, s + 1)
                if n >= 2:
                    pe.wait_ge(row_ready, n - 1)
                pe.matmul(bank[2 * (n % 2)][:, :], k("sel_pair")[:, 0:1].broadcast_to([P, P]), modsum[:, :], start=True, stop=True)
                pe.matmul(bank[2 * (n % 2) + 1][:, :], k("sel_pair")[:, 1:2].broadcast_to([P, P]), modsum[:, :],
                          start=True, stop=True).then_inc(modsel_mm, 1)
            pe.wait_ge(row_ready, ADA_ALL - ADA_FIRST)
            for n in range(2 * NT):
                half, t = n // NT, n % NT
                if t == 0:
                    landed(pe, ADA_ALL + N_IN + half)
                if n >= 4:
                    pe.wait_ge(x1_ready, n - 3)
                w = wide(ADA_ALL + N_IN + half)
                for kt in range(KT):
                    lhs = yconvT[:, kt, P * t:P * t + P] if kt < CB else yretT[:, kt - CB, P * t:P * t + P]
                    last = pe.matmul(bank[n % 4][:, :], lhs, w[:, kt, :], start=(kt == 0), stop=(kt == KT - 1))
                last.then_inc(wout_mm, 1)
            pe.wait_ge(small_in, 16 * 9)
            for t in range(NT):
                pe.wait_ge(xn2_ready, t + 1)
                if t >= 1:
                    pe.wait_ge(xn2T_ev, t)
                for kt in range(KT):
                    last = pe.transpose(bank[4 + kt // 4][:, P * (kt % 4):P * (kt % 4) + P], xn2[:, t, P * kt:P * kt + P], ident)
                last.then_inc(xn2T_mm, 1)
                pe.wait_ge(xn2T_ev, t + 1)
                if t >= 1:
                    pe.wait_ge(lg_ready, t)
                for kt in range(KT):
                    last = pe.matmul(bank[6][:, 0:GROUPS + EXPERTS], xn2T[:, t % 2, kt, :], w_router[:, kt, :],
                                     start=(kt == 0), stop=(kt == KT - 1))
                last.then_inc(rt_mm, 1)
            pe.wait_ge(chosen, 1)
            both = rt[:, 480:640]
            pe.matmul(bank[7][:, 0:160], k("before"), both, start=True, stop=True)
            pe.matmul(bank[7][:, 160:320], k("ones").broadcast_to([P, P]), both, start=True, stop=True).then_inc(rank_mm, 1)

            def rows_T(p_, tiles):
                for kt in tiles:
                    last = pe.transpose(bank[kt // 4][:, P * (kt % 4):P * (kt % 4) + P], xe[:, p_, P * kt:P * kt + P], ident)
                    if kt % 4 == 3:
                        last.then_inc(xe_mm, 1)

            def gate_up(s, p_, pair, hid_before=None):
                for kt in range(KT):
                    lhs = xeT[:, pair, kt, BLK * p_:BLK * p_ + BLK]
                    pe.matmul(bank[2 + p_][0:BLK, 0:DE], lhs, w_gate(s)[:, kt, :], start=(kt == 0), stop=(kt == KT - 1))
                    if hid_before is not None and kt == KT - 1:
                        pe.wait_ge(hid_done, hid_before)
                    last = pe.matmul(bank[2 + p_][BLK:2 * BLK, 0:DE], lhs, w_up(s)[:, kt, :],
                                     start=(kt == 0), stop=(kt == KT - 1))
                last.then_inc(gu_mm, 1)

            def hidden_T(p_):
                for c in range(2):
                    last = pe.transpose(bank[4 + p_][:, BLK * c:BLK * c + BLK], hid[0:BLK, p_, P * c:P * c + P],
                                        ident[0:BLK, 0:BLK])
                last.then_inc(ht_mm, 1)

            def down(s, p_, hid_next=None):
                for c in range(2):
                    for half in range(2):
                        if hid_next is not None and c == 1 and half == 1:
                            pe.wait_ge(hid_done, hid_next)
                        last = pe.matmul(bank[6 + p_][BLK * half:BLK * half + BLK, :], hidT[:, p_, c, :],
                                         w_down(s)[:, c, SL * half:SL * half + SL], start=(c == 0), stop=(c == 1))
                last.then_inc(down_mm, 1)

            pe.wait_ge(routed, 1)
            pe.wait_ge(xe_in[0], 16)
            rows_T(0, range(KT))
            with pe.Fori(0, EXPERTS // NSLOT) as i:
                for j in range(NSLOT):
                    n = i * NSLOT + j
                    s, p_, pair = e_slot[j], j % 2, j // 2
                    pe.wait_ge(ring_in[s], i * 48 + (16 * early_uses[s] + 48))
                    pe.wait_ge(xe_ready, i * NSLOT + 2 * (pair + 1))
                    pe.wait_ge(hid_done, n + 1)
                    gate_up(s, p_, pair)
                    pe.wait_ge(xe_in[1 - pair], i * 16 + 16 * (1 + pair))
                    rows_T(1 - pair, range(4 * p_, 4 * p_ + 3))
                    pe.wait_ge(hid_done, n + 3)
                    rows_T(1 - pair, range(4 * p_ + 3, 4 * p_ + 4))
                    hidden_T(p_)
                    pe.wait_ge(ht_ready, n + 1)
                    pe.wait_ge(y_ev, n + 1)
                    down(s, p_)
            count = pe.value_load(ov_tab[0:1, OVB:OVB + 1], min_val=0, max_val=OVB // 2 - 1)
            with pe.If(count > 0):
                with pe.Fori(0, count) as m:
                    for j in range(2):
                        s = e_slot[j]
                        pe.wait_ge(ring_in[s], m * 48 + (16 * early_uses[s] + 48 * (EXPERTS // NSLOT + 1)))
                        if j == 0:
                            pe.wait_ge(xe_ready, m * 2 + (EXPERTS + 2))
                        gate_up(s, j, 0, None if j == 0 else m * 2 + (EXPERTS + 3))
                    for j in range(2):
                        hidden_T(j)
                        pe.wait_ge(ht_ready, m * 2 + (EXPERTS + 1 + j))
                        pe.wait_ge(y_ev, m * 2 + (EXPERTS + 1 + j))
                        down(e_slot[j], j, m * 2 + (EXPERTS + 4) if j == 0 else None)
                    pe.wait_ge(xe_in[0], m * 16 + 16 * (EXPERTS // 4 + 2))
                    rows_T(0, range(KT))

        @block.vector
        def _(dve):
            steps = [0]

            def then(ins):
                steps[0] += 1
                ins.then_inc(step, 1)
                dve.wait_ge(step, steps[0])

            def tt(out, in0, in1, op):
                return dve.tensor_tensor(out, in0, in1, op)

            dve.memset(cs[:, :, :], 0.0).then_inc(cs_zero, 1)
            dve.memset(zeros, 0.0).then_inc(zero_set, 1)
            dve.wait_ge(dec_e, 1)
            dve.tensor_scalar(decay[:, 2, :], decay[:, 1, :], -1.0, 1.0, ALU.mult, ALU.add).then_inc(dec_u, 1)
            dve.wait_ge(dec_u, 1)
            then(dve.tensor_scalar(decay[:, 4, :], decay[:, 2, :], -1.0, 1.0, ALU.mult, ALU.add))
            then(dve.tensor_scalar(decay[:, 5, :], decay[:, 4, :], 0.0, None, ALU.is_equal))
            then(tt(decay[:, 4, :], decay[:, 4, :], decay[:, 5, :], ALU.add))
            then(dve.reciprocal(decay[:, 4, :], decay[:, 4, :]))
            dve.wait_ge(dec_ln, 1)
            then(tt(decay[:, 3, :], decay[:, 3, :], decay[:, 5, :], ALU.subtract))
            then(tt(decay[:, 3, :], decay[:, 3, :], decay[:, 4, :], ALU.mult))
            tt(decay[:, 5, :], decay[:, 3, :], decay[:, 1, :], ALU.mult).then_inc(dec_lg, 1)
            dve.wait_ge(dec_act, 1)
            dve.wait_ge(c_in, 96)

            def heads_of(row):
                return row.rearrange("p (a n) -> p a n", a=1).broadcast_to([P, HEADS, P])

            then(tt(mask[:, :, :], decay_tmp[:, 0], heads_of(e("fwd_on")), ALU.mult))
            then(tt(decay_tmp[:, 1], decay_tmp[:, 1], heads_of(e("bwd_on")), ALU.mult))
            tt(mask[:, :, :], mask[:, :, :], decay_tmp[:, 1], ALU.add).then_inc(dec_done, 1)
            dve.wait_ge(ssq_done, NT)
            dve.tensor_scalar(stat[:, 1, :], stat[:, 0, :], 1.0 / D, EPS, ALU.mult, ALU.add).then_inc(ms_done, 1)
            dve.wait_ge(root_done, 1)
            dve.reciprocal(stat[:, 3, :], stat[:, 2, :]).then_inc(rstd_done, 1)
            for s in range(ADA_FIRST):
                dve.wait_ge(mod_mm, s + 1)
                if s >= 1:
                    dve.wait_ge(modcol_mm, s)
                dve.tensor_copy(modsum[:, :], bank[s % 2][:, :]).then_inc(mod_ev, 1)
            dve.wait_ge(modcol_mm, ADA_FIRST)
            dve.wait_ge(small_in, 16 * 9)
            pair = lambda b: bank[b][:, 0:2 * KT].rearrange("p (k s) -> p k s", s=2)
            dve.tensor_copy(shift[:, :, :], pair(2)).then_inc(col_ready, 1)
            dve.scalar_tensor_tensor(out=scale[:, :, :], in0=pair(3), scalar=1.0,
                                     in1=g_mix[:, :].rearrange("p (k a) -> p k a", a=1).broadcast_to([P, KT, 2]),
                                     op0=ALU.add, op1=ALU.mult).then_inc(col_ready, 1)
            dve.wait_ge(col_ready, 2)
            for t in range(NT):
                dve.wait_ge(xT_mm, 2 * t + 1)
                s = 0 if t == 0 else 1
                for c in range(4):
                    last = dve.tensor_scalar(xnT[:, c, P * t:P * t + P], bank[4 + 2 * (t % 2)][:, P * c:P * c + P],
                                             scale[:, c, s:s + 1], shift[:, c, s:s + 1], ALU.mult, ALU.add)
                last.then_inc(xT_dve, 1)
            for m in range(CB):
                dve.wait_ge(proj_mm, CB + m + 1)
                dve.wait_ge(conv_c_ev, CB)
                tt(u[:, m, 0:P], u[:, m, 0:P], bank[2 + m % 2][:, 0:P], ALU.mult)
                tt(u[:, m, P:], u[:, m, P:], bank[m % 2][:, :], ALU.mult).then_inc(conv_h_ev, 1)
            dve.wait_ge(conv_h_ev, CB)
            spans = ((0, P, P), (P, TOK, GRID_W))
            for m in range(CB):
                for lo, hi, w in spans:
                    o = yconvT[:, m, lo:hi].rearrange("p (r w) -> p r w", w=w)
                    i_ = u[:, m, lo:hi].rearrange("p (r w) -> p r w", w=w)
                    then(dve.tensor_scalar(o, i_, conv_w[:, 1, m:m + 1], None, ALU.mult))
                    then(dve.scalar_tensor_tensor(out=o[:, :, 1:], in0=i_[:, :, 0:w - 1], scalar=conv_w[:, 0, m:m + 1],
                                                  in1=o[:, :, 1:], op0=ALU.mult, op1=ALU.add))
                    then(dve.scalar_tensor_tensor(out=o[:, :, 0:w - 1], in0=i_[:, :, 1:], scalar=conv_w[:, 2, m:m + 1],
                                                  in1=o[:, :, 0:w - 1], op0=ALU.mult, op1=ALU.add))
            for m in range(CB):
                dve.wait_ge(proj_mm, 2 * CB + m + 1)
                tt(yconvT[:, m, 0:P], yconvT[:, m, 0:P], bank[2 + m % 2][:, 0:P], ALU.mult)
                tt(yconvT[:, m, P:], yconvT[:, m, P:], bank[m % 2][:, :], ALU.mult).then_inc(conv_b_ev, 1)
            for n in range(2 * (NT - 1)):
                dst = (q, kk)[n // (NT - 1)]
                t = n % (NT - 1) + 1
                dve.wait_ge(qkvg_ev, NT * (n // (NT - 1)) + t + 1)
                heads = lambda r: r.rearrange("p (a n) -> p a n", a=1).broadcast_to([P, HEADS, DH])
                cur = dst[:, t, :].rearrange("p (h n) -> p h n", h=HEADS)
                pairs = cur.rearrange("p h (n two) -> p h n two", two=2)
                t0 = rope_tmp[:, 0, :].rearrange("p (h n) -> p h n", h=HEADS)
                t1 = rope_tmp[:, 1, :].rearrange("p (h n two) -> p h n two", h=HEADS, two=2)
                sn = heads(rope[:, 1, t - 1, :]).rearrange("p h (n two) -> p h n two", two=2)
                if n:
                    dve.wait_ge(rope_done, n)
                tt(t0, cur, heads(rope[:, 0, t - 1, :]), ALU.mult)
                tt(t1[:, :, :, 0], pairs[:, :, :, 1], sn[:, :, :, 0], ALU.mult)
                then(tt(t1[:, :, :, 1], pairs[:, :, :, 0], sn[:, :, :, 1], ALU.mult))
                tt(cur, t0, rope_tmp[:, 1, :].rearrange("p (h n) -> p h n", h=HEADS), ALU.add).then_inc(rope_done, 1)

            def col_heads(c):
                return c.rearrange("p (h a) -> p h a", a=1).broadcast_to([P, HEADS, DH])

            def decay_keys(c, d, before):
                if before:
                    dve.wait_ge(st_mm, before)
                tt(kd.rearrange("p (h n) -> p h n", h=HEADS), kk[:, c, :].rearrange("p (h n) -> p h n", h=HEADS),
                   col_heads(kdec[:, d, :]), ALU.mult).then_inc(kd_ready, 1)

            dve.wait_ge(qkvg_ev, 4 * NT)
            dve.wait_ge(rope_done, 8)
            dve.wait_ge(state_in, 32)
            for n, c in enumerate((4, 3, 2)):
                decay_keys(c, 1, n)
                then(tt(sbk[:, c - 2, :].rearrange("p (h n) -> p h n", h=HEADS),
                        sbk[:, c - 1, :].rearrange("p (h n) -> p h n", h=HEADS), col_heads(cdec[:, 1, :]), ALU.mult))
                dve.wait_ge(st_mm, n + 1)
                tt(sbk[:, c - 2, :], sbk[:, c - 2, :], bank[4][:, :], ALU.add).then_inc(st_ready, 1)
                dve.wait_ge(st_ready, n + 1)
            for t in range(NT):
                dve.wait_ge(qkT_mm, t + 1)
                if t >= 1:
                    dve.wait_ge(o_mm, t)
                    tt(qTf, bank[0][:, :], qdec[:, 0, :, :].rearrange("p h n -> p (h n)"), ALU.mult)
                    tt(qTb, bank[0][:, :], qdec[:, 1, :, :].rearrange("p h n -> p (h n)"), ALU.mult)
                dve.tensor_copy(qT, bank[0][:, :]).then_inc(qT_ev, 1)
                dve.wait_ge(sc_mm, t + 1)
                tt(sm, bank[2][:, :], mask[:, :, :].rearrange("p h n -> p (h n)"), ALU.mult).then_inc(sm_ready, 1)
                if t == 0:
                    for d in range(2):
                        decay_keys(0, d, 3 + d)
                        dve.wait_ge(st_mm, 4 + d)
                        dve.tensor_copy(state_c[:, d, :], bank[4][:, :]).then_inc(st_ready, 1)
                if 1 <= t <= 3:
                    decay_keys(t, 0, 4 + t)
                    dve.wait_ge(o_mm, t + 1)
                    then(tt(sfw.rearrange("p (h n) -> p h n", h=HEADS), sfw.rearrange("p (h n) -> p h n", h=HEADS),
                            col_heads(cdec[:, 0, :]), ALU.mult))
                    dve.wait_ge(st_mm, 5 + t)
                    tt(sfw, sfw, bank[4][:, :], ALU.add).then_inc(st_ready, 1)
                    dve.wait_ge(st_ready, 5 + t)
                dve.wait_ge(osq_done, t + 1)
                then(dve.tensor_reduce(hstat[:, 2, :], q[:, t, :].rearrange("p (h n) -> p h n", h=HEADS), X, ALU.add))
                dve.tensor_scalar(hstat[:, 0, :], hstat[:, 2, :], 1.0 / DH, EPS, ALU.mult, ALU.add).then_inc(oms_done, 1)
                then(tt(q[:, t, :], bank[3][:, :], gate[:, t, :], ALU.mult))
                dve.wait_ge(oroot_done, t + 1)
                then(dve.reciprocal(hstat[:, 2, :], hstat[:, 1, :]))
                tt(q[:, t, :].rearrange("p (h n) -> p h n", h=HEADS), q[:, t, :].rearrange("p (h n) -> p h n", h=HEADS),
                   col_heads(hstat[:, 2, :]), ALU.mult).then_inc(yr_ready, 1)
            dve.wait_ge(yT_mm, NT)
            dve.wait_ge(gffn_in, 16)
            for s in range(ADA_FIRST, ADA_ALL):
                n = s - ADA_FIRST
                dve.wait_ge(mod_mm, s + 1)
                if n >= 1:
                    dve.wait_ge(modsel_mm, n)
                dve.tensor_copy(modsum[:, :], bank[6 + s % 2][:, :]).then_inc(mod_ev, 1)
                dve.wait_ge(modsel_mm, n + 1)
                chunk, half = n // 2, n % 2
                cols = slice(SL * half, SL * half + SL)
                for side in range(2):
                    src = bank[2 * (n % 2) + side][:, :]
                    if chunk == 2:
                        last = dve.scalar_tensor_tensor(out=rows[:, chunk, side, cols], in0=src, scalar=1.0,
                                                        in1=g_ffn[:, cols], op0=ALU.add, op1=ALU.mult)
                    else:
                        last = dve.tensor_copy(rows[:, chunk, side, cols], src)
                last.then_inc(row_ready, 1)
            dve.wait_ge(row_ready, ADA_ALL - ADA_FIRST)
            for n in range(2 * NT):
                half, t = n // NT, n % NT
                cols = slice(SL * half, SL * half + SL)
                dve.wait_ge(wout_mm, n + 1)
                if n:
                    dve.wait_ge(x1_ready, n)
                then(tt(part, bank[n % 4][:, :], rows[:, 0, min(t, 1), cols], ALU.mult))
                tt(x[:, t, cols], x[:, t, cols], part, ALU.add).then_inc(x1_ready, 1)
            dve.wait_ge(x1_ready, 2 * NT)

            def router_logits(t):
                dve.wait_ge(rt_mm, t + 1)
                tt(logits[:, t, :], bank[6][:, 0:GROUPS + EXPERTS], b_router[:, :], ALU.add).then_inc(lg_ready, 1)

            for t in range(NT):
                dve.wait_ge(ssq2_done, t + 1)
                dve.tensor_scalar(stat[:, 1, t:t + 1], stat[:, 0, t:t + 1], 1.0 / D, EPS, ALU.mult, ALU.add).then_inc(ms2_done, 1)
                dve.wait_ge(root2_done, t + 1)
                then(dve.reciprocal(stat[:, 3, t:t + 1], stat[:, 2, t:t + 1]))
                side = min(t, 1)
                as_qk = lambda r: r.rearrange("p (q k) -> p q k", q=P)
                dst = xn2[:, t, :].rearrange("p (k q) -> p q k", q=P)
                then(dve.scalar_tensor_tensor(out=dst, in0=as_qk(x[:, t, :]), scalar=stat[:, 3, t:t + 1],
                                              in1=as_qk(rows[:, 2, side, :]), op0=ALU.mult, op1=ALU.mult))
                tt(dst, dst, as_qk(rows[:, 1, side, :]), ALU.add).then_inc(xn2_ready, 1)
                if t >= 1:
                    router_logits(t - 1)
            router_logits(NT - 1)
            dve.wait_ge(lg_ready, NT)

            def r3(lo, n, m):
                return rt[:, lo:lo + n * m].rearrange("p (t n) -> p t n", t=n)

            def over(ap, shape):
                return ap.rearrange("p (t a) -> p t a", a=1).broadcast_to(shape)

            def row_over(ap, n, m):
                return ap.rearrange("p (a n) -> p a n", a=1).broadcast_to([P, n, m])

            lgg, lge = logits[:, :, 0:GROUPS], logits[:, :, GROUPS:]
            gmax, gsum, psel = rt[:, 0:5], rt[:, 5:10], rt[:, 10:15]
            top = rt[:, 15:20]
            dg, eg = r3(20, NT, GROUPS), r3(40, NT, GROUPS)
            d21, e21 = rt[:, 60:65], rt[:, 65:70]
            m1, m2 = rt[:, 70:75], rt[:, 75:80]
            ohg = r3(80, NT, GROUPS)
            inner, inner2 = r3(100, NT, PER_GROUP), r3(140, NT, PER_GROUP)
            oh = [r3(180, NT, PER_GROUP), r3(220, NT, PER_GROUP)]
            g4, g8 = [NT, GROUPS], [NT, PER_GROUP]

            def first_max(values, out, desc, best, n):
                then(dve.tensor_reduce(best, values, X, ALU.max))
                then(tt(out, values, over(best, [P, NT, n]), ALU.is_equal))
                then(tt(out, out, row_over(desc, NT, n), ALU.mult))
                then(dve.tensor_reduce(top, out, X, ALU.max))
                then(tt(out, out, over(top, [P, NT, n]), ALU.is_equal))

            first_max(lgg, ohg, k("desc_group"), gmax, GROUPS)
            tt(dg, lgg, over(gmax, [P, NT, GROUPS]), ALU.subtract).then_inc(exp_in, 1)
            spread = rt[:, 1280:1440].rearrange("p (t g j) -> p t g j", t=NT, g=GROUPS)
            as_tgj = lambda r: r.rearrange("p t (g j) -> p t g j", g=GROUPS)
            over_j = ohg.rearrange("p t (g a) -> p t g a", a=1).broadcast_to([P, NT, GROUPS, PER_GROUP])
            then(tt(spread, as_tgj(lge), over_j, ALU.mult))
            then(dve.tensor_reduce(inner, spread.rearrange("p t g j -> p t j g"), X, ALU.add))
            first_max(inner, oh[0], k("desc_inner"), m1, PER_GROUP)
            then(dve.scalar_tensor_tensor(out=inner2, in0=oh[0], scalar=-1e30, in1=inner, op0=ALU.mult, op1=ALU.add))
            first_max(inner2, oh[1], k("desc_inner"), m2, PER_GROUP)
            dve.wait_ge(exp_in, 1)
            tt(d21, m2, m1, ALU.subtract).then_inc(exp_in, 1)
            a1, a2, both = rt[:, 640:800], rt[:, 800:960], rt[:, 480:640]
            for j, dst in enumerate((a1, a2)):
                over_g = oh[j].rearrange("p t (a j) -> p t a j", a=1).broadcast_to([P, NT, GROUPS, PER_GROUP])
                then(tt(dst.rearrange("p (t g j) -> p t g j", t=NT, g=GROUPS), over_g, over_j, ALU.mult))
            tt(both, a1, a2, ALU.add).then_inc(chosen, 1)
            dve.wait_ge(exp_out, 2)
            then(dve.tensor_reduce(gsum, eg, X, ALU.add))
            then(dve.reciprocal(psel, gsum))
            then(dve.tensor_scalar(m1, e21, 1.0, None, ALU.add))
            then(dve.reciprocal(m1, m1))
            then(tt(wsel[:, :, 0], m1, psel, ALU.mult))
            then(tt(wsel[:, :, 1], wsel[:, :, 0], e21, ALU.mult))
            dve.wait_ge(rank_mm, 1)
            rank, cnt = rt[:, 960:1120], rt[:, 1120:1280]
            then(dve.tensor_copy(rt[:, 960:1280], bank[7][:, 0:320]))
            rank_t = lambda t: rank[:, 32 * t:32 * t + 32]
            cnt_t = lambda t: cnt[:, 32 * t:32 * t + 32]
            for t in range(1, NT):
                tt(rank_t(t), rank_t(t), cnt_t(t - 1), ALU.add)
                then(tt(cnt_t(t), cnt_t(t), cnt_t(t - 1), ALU.add))
            total = cnt_t(NT - 1)
            nov = rt[:, 1440:1472]
            over_m = total.rearrange("p (e a) -> p e a", a=1).broadcast_to([P, EXPERTS, MAX_SPLIT])
            grid = rt[:, 1500:1500 + EXPERTS * MAX_SPLIT].rearrange("p (e m) -> p e m", e=EXPERTS)
            then(tt(grid, over_m, row_over(k("splits"), EXPERTS, MAX_SPLIT), ALU.is_gt))
            then(dve.tensor_reduce(nov, grid, X, ALU.add))
            run = [rt[:, 1800:1848], rt[:, 1848:1896]]
            then(dve.memset(rt[:, 1800:1896], 0.0))
            then(dve.tensor_copy(run[0][:, 16:48], nov))
            cur = 0
            for hop in (1, 2, 4, 8, 16):
                then(tt(run[1 - cur][:, 16:48], run[cur][:, 16:48], run[cur][:, 16 - hop:48 - hop], ALU.add))
                cur = 1 - cur
            ends = run[cur][:, 16:48]
            jump = rt[:, 1900:1932]
            then(tt(jump, ends, nov, ALU.subtract))
            then(dve.tensor_scalar(jump, jump, float(BLK), float(OV_ROW0 - BLK), ALU.mult, ALU.add))
            then(tt(jump, jump, k("block_row"), ALU.subtract))
            beyond = rt[:, 1940:2100]
            then(dve.tensor_scalar(beyond, rank, float(BLK), None, ALU.is_ge))
            then(tt(beyond.rearrange("p (t e) -> p t e", t=NT), beyond.rearrange("p (t e) -> p t e", t=NT),
                    row_over(jump, NT, EXPERTS), ALU.mult))
            then(tt(rank, rank, beyond, ALU.add))
            then(tt(rank.rearrange("p (t e) -> p t e", t=NT), rank.rearrange("p (t e) -> p t e", t=NT),
                    row_over(k("block_row"), NT, EXPERTS), ALU.add))
            posf = rt[:, 2100:2110].rearrange("p (t j) -> p t j", j=2)
            for j, sel in enumerate((a1, a2)):
                then(tt(sel, sel, rank, ALU.mult))
                then(dve.tensor_reduce(posf[:, :, j], sel.rearrange("p (t e) -> p t e", t=NT), X, ALU.add))
            then(dve.tensor_copy(posi[:, :, :], posf))
            own = rt[:, 0:OVB * EXPERTS].rearrange("p (b e) -> p b e", b=OVB)
            ends_over = ends.rearrange("p (a e) -> p a e", a=1).broadcast_to([P, OVB, EXPERTS])
            index_over = k("ov_index").rearrange("p (b a) -> p b a", a=1).broadcast_to([P, OVB, EXPERTS])
            then(tt(own, ends_over, index_over, ALU.is_le))
            then(dve.tensor_reduce(rt[:, 2120:2120 + OVB], own, X, ALU.add))
            then(dve.tensor_scalar(rt[:, 2120:2120 + OVB], rt[:, 2120:2120 + OVB], float(EXPERTS - 1), None, ALU.min))
            pair_on = rt[:, 2150:2150 + OVB // 2]
            then(tt(pair_on, k("ov_index").rearrange("p (m two) -> p m two", two=2)[:, :, 0],
                    ends[:, EXPERTS - 1:EXPERTS].broadcast_to([P, OVB // 2]), ALU.is_lt))
            then(dve.tensor_reduce(rt[:, 2120 + OVB:2121 + OVB], pair_on, X, ALU.add))
            dve.tensor_copy(ov_tab[:, :], rt[:, 2120:2121 + OVB]).then_inc(routed, 1)

            dve.sem_inc(hid_done, 2)
            dve.wait_ge(routed, 1)

            def rows_evacuate(pair, half):
                dve.tensor_copy(xeT[:, pair, 4 * half:4 * half + 4, :],
                                bank[half][:, :].rearrange("p (k s) -> p k s", k=4)).then_inc(xe_ready, 1)

            def hidden(p_):
                tt(hid[0:BLK, p_, :].rearrange("p (c q) -> p q c", c=2),
                   sgate[BLK:2 * BLK, p_, :].rearrange("p (q c) -> p q c", c=2),
                   bank[2 + p_][BLK:2 * BLK, 0:DE].rearrange("p (q c) -> p q c", c=2), ALU.mult).then_inc(hid_done, 1)

            for half in range(2):
                dve.wait_ge(xe_mm, half + 1)
                rows_evacuate(0, half)
            with dve.Fori(0, EXPERTS // NSLOT) as i:
                for j in range(NSLOT):
                    n = i * NSLOT + j
                    dve.wait_ge(silu_done, n + 1)
                    hidden(j % 2)
                    dve.wait_ge(xe_mm, n + 3)
                    rows_evacuate(1 - j // 2, j % 2)
            count = dve.value_load(ov_tab[0:1, OVB:OVB + 1], min_val=0, max_val=OVB // 2 - 1)
            with dve.If(count > 0):
                with dve.Fori(0, count) as m:
                    for j in range(2):
                        dve.wait_ge(silu_done, m * 2 + (EXPERTS + 1 + j))
                        hidden(j)
                    for half in range(2):
                        dve.wait_ge(xe_mm, m * 2 + (EXPERTS + 3 + half))
                        rows_evacuate(0, half)

            dve.wait_ge(gfin_in, 16)
            for t in range(NT):
                side = min(t, 1)
                g0, g1 = got[:, t % 2, 0, :], got[:, t % 2, 1, :]
                dve.wait_ge(got_in[t % 2], 32 * (t // 2 + 1))
                then(dve.tensor_scalar(g0, g0, wsel[:, t, 0:1], None, ALU.mult))
                then(dve.scalar_tensor_tensor(out=g0, in0=g1, scalar=wsel[:, t, 1:2], in1=g0, op0=ALU.mult, op1=ALU.add))
                then(tt(g0, g0, rows[:, 3, side, :], ALU.mult))
                tt(x[:, t, :], x[:, t, :], g0, ALU.add).then_inc(x2_ready, 1)
                dve.wait_ge(ssq3_done, t + 1)
                dve.tensor_scalar(stat[:, 1, t:t + 1], stat[:, 0, t:t + 1], 1.0 / D, EPS, ALU.mult, ALU.add).then_inc(ms3_done, 1)
                dve.wait_ge(root3_done, t + 1)
                then(dve.reciprocal(stat[:, 3, t:t + 1], stat[:, 2, t:t + 1]))
                if t >= 2:
                    dve.wait_ge(stored[t % 2], 16 * (t // 2))
                dve.wait_ge(x2_ready, t + 1)
                dve.scalar_tensor_tensor(out=outb[:, t % 2, :], in0=x[:, t, :], scalar=stat[:, 3, t:t + 1], in1=g_fin,
                                         op0=ALU.mult, op1=ALU.mult).then_inc(out_ready, 1)


_OUTS = [((1, P, D), "float32"), ((1, LAT, D), "float32"), ((1, 1, HEADS, DH, DH), "float32"),
         ((1, 1, HEADS, DH, DH), "float32")]
_INS = ["x_prompt", "x_sample", "state_ret_fwd", "state_ret_bwd", "c", "c_ctx", "norm_mix_g", "norm_ffn_g", "w_ada",
        "b_ada", "w_in", "conv_w", "ret_decay_fwd", "ret_decay_bwd", "w_out", "w_router_group", "b_router_group",
        "w_router_expert", "b_router_expert", "w_gate_e", "w_up_e", "w_down_e", "final_norm_g"]


def kernel(**inputs):
    import concourse.bacc as bacc
    from concourse.bass_utils import run_bass_kernel_spmd as run

    kept, early, rope = const_table()
    arrays = {f"in_{n}": np.ascontiguousarray(inputs[n]) for n in _INS}
    arrays["in_final_norm_g"] = arrays["in_final_norm_g"].reshape(1, D)
    arrays["in_c_kept"], arrays["in_c_early"], arrays["in_c_rope"] = kept, early, rope
    nc = bacc.Bacc("TRN2", target_bir_lowering=False, num_devices=1)
    a = {n[3:]: nc.dram_tensor(n, v.shape, mybir.dt.from_np(v.dtype), kind="ExternalInput").ap() for n, v in arrays.items()}
    outs = [nc.dram_tensor(f"out_{i}", s, mybir.dt.from_np(np.dtype(d)), kind="ExternalOutput").ap()
            for i, (s, d) in enumerate(_OUTS)]
    layer(nc, a, *outs)
    r = run(nc, [arrays], core_ids=[0])
    return tuple(r.results[0][f"out_{i}"] for i in range(len(_OUTS)))
```

```python
from contextlib import ExitStack

import numpy as np

import concourse.bass as bass
from concourse import mybir

P = 128
D = 1024
KT = D // P
NT = 5
TOK = NT * P
LAT = TOK - P
GRID_W = 64
CB = 4
HEADS = 4
DH = 128
W = HEADS * DH
SL = 512
EXPERTS = 32
GROUPS = 4
PER_GROUP = 8
DE = 256
BLK = 64
PAIRS = 2 * TOK
OVB = 22
MAX_SPLIT = TOK // BLK - 1
OV_ROW0 = EXPERTS * BLK
ROWS = OV_ROW0 + OVB * BLK
EPS = 1e-6
NSLOT = 4
SLOT = KT * 2 * DE + 2 * D
ADA_FIRST = 4
ADA_ALL = 12
N_IN = 7
IN_ORDER = (1, 2, 0, 3, 4, 5, 6)
FIRST_EXPERT_ITEM = ADA_ALL + N_IN + 2
MOD_TURNS = ((4, 5), (6, 7), (8, 9), (10,), (11,))
FAR = 65536
CHOICE = (640, 1280)
RANK = 256
BEFORE = 1920
BOTH = 1440

F32 = mybir.dt.float32
I32 = mybir.dt.int32
ALU = mybir.AluOpType
ACT = mybir.ActivationFunctionType
X = mybir.AxisListType.X

CONSTS = {}


def const_table():
    i = np.arange(P, dtype=np.float64)
    parts = {}
    parts["ident"] = np.eye(P)
    parts["before"] = (i[:, None] < i[None, :]) * 1.0
    parts["ones"] = np.ones((P, 1))
    parts["sel_pair"] = np.stack([i % 32 == 0, i % 32 == 1], 1) * 1.0
    bias = np.zeros((P, ADA_ALL, 32))
    for s in range(ADA_ALL):
        bias[s, s, 0:2] = 1.0
    parts["sel_bias"] = bias.reshape(P, -1)
    parts["k_pos"] = np.stack([P - 1 - i, i], 1)
    bc = lambda row: np.repeat(np.asarray(row, np.float64).reshape(1, -1), P, 0)
    parts["desc_group"] = bc(GROUPS - np.arange(GROUPS))
    parts["desc_inner"] = bc(PER_GROUP - np.arange(PER_GROUP))
    parts["splits"] = bc(BLK * (1 + np.arange(MAX_SPLIT)))
    parts["block_row"] = bc(BLK * np.arange(EXPERTS))
    parts["ov_index"] = bc(np.arange(OVB))
    early = {}
    early["fwd_gap"] = np.maximum(i[None, :] - i[:, None], 0)
    early["bwd_gap"] = np.maximum(i[:, None] - i[None, :], 0)
    early["fwd_on"] = (i[None, :] >= i[:, None]) * 1.0
    early["bwd_on"] = (i[:, None] >= i[None, :]) * 1.0
    early["q_pos_f"] = bc(i + 1)
    early["q_pos_b"] = bc(P - i)
    pos = np.arange(LAT)
    pairs = DH // 4
    freqs = (10000.0 ** (-(np.arange(pairs, dtype=np.float32) * 2.0 / (DH // 2)))).astype(np.float32)
    ang = np.concatenate([(pos // GRID_W).astype(np.float32)[:, None] * freqs,
                          (pos % GRID_W).astype(np.float32)[:, None] * freqs], -1)
    cos, sin = np.cos(ang.astype(np.float64)), np.sin(ang.astype(np.float64))
    c2 = np.repeat(cos, 2, 1)
    s2 = np.stack([-sin, sin], -1).reshape(LAT, DH)
    chunked = lambda a: a.reshape(LAT // P, P, DH).transpose(1, 0, 2).reshape(P, -1)
    rope = np.concatenate([chunked(c2), chunked(s2)], 1)
    at = 0
    for name, a in parts.items():
        CONSTS[name] = (at, at + a.shape[1])
        at += a.shape[1]
    at = 0
    for name, a in early.items():
        CONSTS[name] = (at, at + a.shape[1])
        at += a.shape[1]
    pack = lambda d: np.ascontiguousarray(np.concatenate(list(d.values()), 1).astype(np.float32))
    return pack(parts), pack(early), np.ascontiguousarray(rope.astype(np.float32))


def layer(nc, a, y_prompt, y_sample, new_f, new_b):
    kept_w = a["c_kept"].shape[1]
    early_w = a["c_early"].shape[1]
    xs_rows = nc.dram_tensor("expert_in_rows", (ROWS, D), F32, kind="Internal").ap()
    mod_rows = nc.dram_tensor("mod_rows", (4, 2, D), F32, kind="Internal").ap()
    y_rows = nc.dram_tensor("expert_out_rows", (ROWS, D), F32, kind="Internal").ap()

    with ExitStack() as ctx:
        def sb(name, shape, dt=F32):
            return ctx.enter_context(nc.sbuf_tensor(name, shape, dt))

        def sem(name):
            return ctx.enter_context(nc.semaphore(name))

        bank = [ctx.enter_context(nc.psum_tensor(f"bank{b}", [P, SL], F32)) for b in range(8)]

        ring = sb("ring", [P, NSLOT, SLOT])
        x = sb("x", [P, NT, D])
        kept = sb("kept", [P, kept_w])
        cs = sb("cs", [P, KT, 32])
        cvec = sb("cvec", [P, 2, KT])
        b_ada = sb("b_ada_rows", [ADA_ALL, SL])
        modsum = sb("modsum", [P, SL])
        shift = sb("shift", [P, KT, 2])
        scale = sb("scale", [P, KT, 2])
        g_mix = sb("g_mix", [P, KT])
        conv_w = sb("conv_taps", [P, 3, CB])
        decay = sb("decay", [P, 6, 8])
        kdec = sb("kdec", [P, 2, HEADS])
        cdec = sb("cdec", [P, 2, HEADS])
        tail = [ring[:, s, KT * SL:SLOT] for s in range(NSLOT)]
        mask = tail[0][:, 0:512].rearrange("p (h n) -> p h n", h=HEADS)
        qdec = tail[0][:, 512:1536].rearrange("p (d h n) -> p d h n", d=2, h=HEADS)
        rope = tail[1][:, 0:1024].rearrange("p (d c n) -> p d c n", d=2, c=4)
        state_c = tail[1][:, 1024:2048].rearrange("p (d n) -> p d n", d=2)
        modrow = tail[2][:, 0:1024].rearrange("p (h n) -> p h n", h=2)
        stat = sb("stat", [P, 4, NT])
        hstat = sb("hstat", [P, 3, HEADS])
        w_router = sb("w_router", [P, KT, GROUPS + EXPERTS])
        b_router = sb("b_router", [P, GROUPS + EXPERTS])
        logits = sb("logits", [P, NT, GROUPS + EXPERTS])

        arena_a = sb("arena_a", [P, KT * TOK])
        arena_b = sb("arena_b", [P, 4 * NT * W])
        arena_c = sb("arena_c", [P, CB * TOK])
        arena_d = sb("arena_d", [P, CB * TOK])

        def k(name):
            lo, hi = CONSTS[name]
            return kept[:, lo:hi]

        ident = k("ident")

        xnT = arena_a[:, :].rearrange("p (k t) -> p k t", k=KT)
        q = arena_b[:, 0:2560].rearrange("p (t n) -> p t n", t=NT)
        kk = arena_b[:, 2560:5120].rearrange("p (t n) -> p t n", t=NT)
        v = arena_b[:, 5120:7680].rearrange("p (t n) -> p t n", t=NT)
        gate = arena_b[:, 7680:10240].rearrange("p (t n) -> p t n", t=NT)
        xs = arena_b[:, 0:2048].rearrange("p (b n) -> p b n", b=2)
        early = arena_b[:, 2560:2560 + early_w]
        decay_tmp = arena_b[:, 5120:6144].rearrange("p (b h n) -> p b h n", b=2, h=HEADS)
        zeros = arena_b[:, 7680:8704]
        u = arena_c[:, :].rearrange("p (m t) -> p m t", m=CB)
        yconvT = arena_d[:, :].rearrange("p (m t) -> p m t", m=CB)
        rope_tmp = arena_c[:, 0:1024].rearrange("p (b n) -> p b n", b=2)

        def e(name):
            lo, hi = CONSTS[name]
            return early[:, lo:hi]

        yretT = arena_a[:, 0:2560].rearrange("p (t m n) -> p t m n", t=NT, m=CB)
        sbk = tail[3].rearrange("p (c n) -> p c n", c=4)
        sfw = tail[0][:, 1536:2048]
        qT, kT, qTf0, qTb0, sm = (arena_c[:, 512 * n:512 * n + 512] for n in range(5))
        qTf = [qTf0, tail[2][:, 1024:1536]]
        qTb = [qTb0, tail[2][:, 1536:2048]]
        kd = rope[:, 0, :, :].rearrange("p c n -> p (c n)")

        rows = [arena_b[:, 2 * D * c:2 * D * c + 2 * D].rearrange("p (s n) -> p s n", s=2) for c in range(4)]
        xn2T = arena_b[:, 8192:10240].rearrange("p (b k t) -> p b k t", b=2, k=KT)
        xn2 = [arena_a[:, D * ((t + 3) % NT):D * ((t + 3) % NT) + D] for t in range(NT)]
        part = arena_c[:, 0:512]
        square = arena_c[:, 512:1536]
        g_ffn = arena_c[:, 1536:2560]

        rt = arena_d[:, :]

        xe = arena_c[:, 0:2048].rearrange("p (b n) -> p b n", b=2)
        xeT = arena_b[:, 0:2048].rearrange("p (b k s) -> p b k s", b=2, k=KT)
        sgate = arena_b[:, 9216:9728].rearrange("p (b n) -> p b n", b=2)
        hid = arena_b[:, 9728:10240].rearrange("p (b n) -> p b n", b=2)
        hidT = arena_b[:, 2048:2304].rearrange("p (b c s) -> p b c s", b=2, c=2)
        ysb = arena_b[:, 8192:9216].rearrange("p (b n) -> p b n", b=2)
        posi = sb("posi", [P, NT, 2], I32)
        pos_own = sb("pos_own", [P, NT, 2], I32)
        pos_ov = sb("pos_ov", [P, NT, 2], I32)
        wsel = sb("wsel", [P, NT, 2])
        ov_tab = sb("ov_tab", [P, OVB + 1], I32)

        flat = ring[:, :, :].rearrange("p s n -> p (s n)")
        got = flat[:, 0:2 * NT * D].rearrange("p (t j n) -> p t j n", t=NT, j=2)
        outb = flat[:, 2 * NT * D:(2 * NT + 2) * D].rearrange("p (b n) -> p b n", b=2)
        sq7 = flat[:, (2 * NT + 2) * D:(2 * NT + 3) * D]
        g_fin = arena_a[:, 0:D]

        ring_in = [sem(f"ring_in{s}") for s in range(NSLOT)]
        c_in, kept_in, x_in, small_in = sem("c_in"), sem("kept_in"), sem("x_in"), sem("small_in")
        decay_in, g_mix_in = sem("decay_in"), sem("g_mix_in")
        state_in, gffn_in, gfin_in = sem("state_in"), sem("gffn_in"), sem("gfin_in")
        cs_zero, cs_ready = sem("cs_zero"), sem("cs_ready")
        mod_mm, mod_ev, modrow_mm, modcol_mm, modrow_ev, mod_out = (sem(n) for n in (
            "mod_mm", "mod_ev", "modrow_mm", "modcol_mm", "modrow_ev", "mod_out"))
        rows_in = [sem(f"rows_in{c}") for c in range(4)]
        scale2_ready = sem("scale2_ready")
        col_ready = sem("col_ready")
        ssq_done, ms_done, root_done, rstd_done = (sem(n) for n in ("ssq_done", "ms_done", "root_done", "rstd_done"))
        xs_ready, xT_mm, xT_act, xT_dve, xn_act, xn_dve = (sem(n) for n in (
            "xs_ready", "xT_mm", "xT_act", "xT_dve", "xn_act", "xn_dve"))
        dec_e, dec_u, dec_ln, dec_lg, dec_act, dec_done = (sem(n) for n in (
            "dec_e", "dec_u", "dec_ln", "dec_lg", "dec_act", "dec_done"))
        zero_set, zero_out = sem("zero_set"), sem("zero_out")
        proj_mm, conv_c_ev, conv_h_ev, conv_b_ev = (sem(n) for n in ("proj_mm", "conv_c_ev", "conv_h_ev", "conv_b_ev"))
        qkvg_ev, rope_done = sem("qkvg_ev"), sem("rope_done")
        kd_ready, st_mm, st_ready, new_out = sem("kd_ready"), sem("st_mm"), sem("st_ready"), sem("new_out")
        qkT_mm, kT_ev, qT_ev, sc_mm, sm_ready, o_mm = (sem(n) for n in (
            "qkT_mm", "kT_ev", "qT_ev", "sc_mm", "sm_ready", "o_mm"))
        osq_done, oms_done, oroot_done, yr_ready, yT_mm, yT_ev = (sem(n) for n in (
            "osq_done", "oms_done", "oroot_done", "yr_ready", "yT_mm", "yT_ev"))
        wout_mm, x1_ready = sem("wout_mm"), sem("x1_ready")
        ssq2_done, ms2_done, root2_done, xn2_ready, xn2T_mm, xn2T_ev, rt_mm, lg_ready = (sem(n) for n in (
            "ssq2_done", "ms2_done", "root2_done", "xn2_ready", "xn2T_mm", "xn2T_ev", "rt_mm", "lg_ready"))
        exp_in, exp_out, chosen, rank_mm, placed, routed, xs_out, ov_out, ov_done = (sem(n) for n in (
            "exp_in", "exp_out", "chosen", "rank_mm", "placed", "routed", "xs_out", "ov_out", "ov_done"))
        xe_in = [sem("xe_in0"), sem("xe_in1")]
        xe_mm, xe_ready, gu_mm, silu_done, hid_done, ht_mm, ht_ready, down_mm, y_ev = (sem(n) for n in (
            "xe_mm", "xe_ready", "gu_mm", "silu_done", "hid_done", "ht_mm", "ht_ready", "down_mm", "y_ev"))
        y_out = [sem("y_out0"), sem("y_out1")]
        y_all = sem("y_all")
        got_in = [sem(f"got_in{t}") for t in range(NT)]
        part0_ready = sem("part0_ready")
        x2_ready, ssq3_done, ms3_done, root3_done, out_ready = (sem(n) for n in (
            "x2_ready", "ssq3_done", "ms3_done", "root3_done", "out_ready"))
        stored = [sem("stored0"), sem("stored1")]
        step = sem("dve_step")

        ada_v = a["w_ada"][0].rearrange("(p k) n -> p k n", k=KT)
        win_v = a["w_in"][0].rearrange("(p k) n -> p k n", k=KT)
        wout_v = a["w_out"][0].rearrange("(k p) n -> p k n", p=P)

        items = ([("ada", s) for s in range(ADA_FIRST)] + [("in", s) for s in range(N_IN)]
                 + [("ada", s) for s in range(ADA_FIRST, ADA_ALL)] + [("out", s) for s in range(2)])
        assert len(items) == FIRST_EXPERT_ITEM

        def proj_groups(n):
            return CB * min(n, 3) + NT * max(n - 3, 0)

        def st_bank(n):
            return 3 if n < 5 else 4

        def slot_of(item):
            return item % NSLOT

        def landed(eng, item):
            eng.wait_ge(ring_in[slot_of(item)], 16 * (item // NSLOT + 1))

        def wide(item):
            return ring[:, slot_of(item), 0:KT * SL].rearrange("p (k n) -> p k n", k=KT)

        early_uses = [sum(1 for n in range(FIRST_EXPERT_ITEM) if n % NSLOT == s) for s in range(NSLOT)]
        e_slot = [(FIRST_EXPERT_ITEM + j) % NSLOT for j in range(NSLOT)]

        def w_gate(s):
            return ring[:, s, 0:KT * DE].rearrange("p (k n) -> p k n", k=KT)

        def w_up(s):
            return ring[:, s, KT * DE:2 * KT * DE].rearrange("p (k n) -> p k n", k=KT)

        def w_down(s):
            return ring[:, s, 2 * KT * DE:SLOT].rearrange("p (h n) -> p h n", h=2)

        def released(eng, item):
            kind, s = items[item]
            if kind == "ada":
                eng.wait_ge(mod_mm, s + 1)
            elif kind == "in":
                eng.wait_ge(proj_mm, proj_groups(s + 1))
            else:
                eng.wait_ge(wout_mm, 2 * NT - 1 + s)

        block = ctx.enter_context(nc.Block())

        @block.sync
        def _(sp):
            sp.dma_start(cvec[:, 0, :], a["c_ctx"].rearrange("(p k) -> p k", k=KT)).then_inc(c_in, 16)
            sp.dma_start(cvec[:, 1, :], a["c"][0].rearrange("(p k) -> p k", k=KT)).then_inc(c_in, 16)
            sp.dma_start(b_ada[:, :], a["b_ada"].rearrange("a (s n) -> (a s) n", n=SL)).then_inc(c_in, 16)
            sp.dma_start(kept[:, :], a["c_kept"]).then_inc(kept_in, 16)
            sp.dma_start(x[:, 0, :], a["x_prompt"][0]).then_inc(x_in, 16)
            sp.dma_start(x[:, 1:, :], a["x_sample"][0].rearrange("(t p) n -> p t n", p=P)).then_inc(x_in, 16)

            def expert_weights(s, gate_src, up_src, down_src):
                sp.dma_start(w_gate(s), gate_src).then_inc(ring_in[s], 16)
                sp.dma_start(w_up(s), up_src).then_inc(ring_in[s], 16)
                sp.dma_start(w_down(s), down_src).then_inc(ring_in[s], 16)

            for n, (kind, s) in enumerate(items):
                if n >= NSLOT:
                    released(sp, n - NSLOT)
                if kind == "ada":
                    src = ada_v[:, :, SL * s:SL * s + SL]
                elif kind == "in":
                    src = win_v[:, :, SL * IN_ORDER[s]:SL * IN_ORDER[s] + SL]
                else:
                    src = wout_v[:, :, SL * s:SL * s + SL]
                sp.dma_start(wide(n), src).then_inc(ring_in[slot_of(n)], 16)
            sp.wait_ge(new_out, 32)
            sp.wait_ge(mod_out, 16 * 4)
            for c in range(4):
                sp.wait_ge(rows_in[c], 16)
            gv = a["w_gate_e"][0].rearrange("e (p k) n -> e p k n", k=KT)
            uv = a["w_up_e"][0].rearrange("e (p k) n -> e p k n", k=KT)
            dv = a["w_down_e"][0].rearrange("e (p h) n -> e p h n", h=2)
            for j in range(NSLOT):
                released(sp, FIRST_EXPERT_ITEM + j - NSLOT)
                expert_weights(e_slot[j], gv[j], uv[j], dv[j])
            with sp.Fori(1, EXPERTS // NSLOT) as i:
                for j in range(NSLOT):
                    sp.wait_ge(down_mm, i * NSLOT + (j + 1 - NSLOT))
                    ex = bass.ds(i * NSLOT + j, 1)
                    expert_weights(e_slot[j], gv[ex].rearrange("e p k n -> (e p) k n"),
                                   uv[ex].rearrange("e p k n -> (e p) k n"),
                                   dv[ex].rearrange("e p h n -> (e p) h n"))
            sp.wait_ge(routed, 1)
            count = sp.value_load(ov_tab[0:1, OVB:OVB + 1], min_val=0, max_val=OVB // 2 - 1)
            with sp.If(count > 0):
                with sp.Fori(0, count) as m:
                    for j in range(2):
                        sp.wait_ge(down_mm, m * 2 + (EXPERTS - 1 + j))
                        who = sp.value_load(ov_tab[0:1, bass.ds(m * 2 + j, 1)], min_val=0, max_val=EXPERTS - 1)
                        ex = bass.ds(who, 1)
                        expert_weights(e_slot[j], gv[ex].rearrange("e p k n -> (e p) k n"),
                                       uv[ex].rearrange("e p k n -> (e p) k n"),
                                       dv[ex].rearrange("e p h n -> (e p) h n"))
            sp.wait_ge(y_out[0], count * 32 + 32 * (1 + EXPERTS // 2))
            sp.wait_ge(y_out[1], count * 32 + 32 * (1 + EXPERTS // 2))
            sp.sem_inc(y_all, 1)
            for t in range(NT):
                sp.wait_ge(out_ready, t + 1)
                dst = y_prompt[0] if t == 0 else y_sample[0, P * (t - 1):P * t, :]
                sp.dma_start(dst, outb[:, t % 2, :]).then_inc(stored[t % 2], 16)
            sp.wait_ge(stored[0], 16 * 3)
            sp.wait_ge(stored[1], 16 * 2)

        @block.gpsimd
        def _(pool):
            pool.dma_start(g_mix[:, :], a["norm_mix_g"][0].rearrange("(p k) -> p k", k=KT)).then_inc(g_mix_in, 16)
            pool.wait_ge(ring_in[ADA_FIRST % NSLOT], 32)
            pool.dma_start(tail[1][:, 0:1024], a["c_rope"]).then_inc(small_in, 16)
            for tap in range(3):
                pool.dma_start(conv_w[:, tap, :], a["conv_w"][0, tap].rearrange("(m p) -> p m", p=P),
                               allow_slow_non_contiguous=True).then_inc(small_in, 16)
            pool.dma_start(w_router[:, :, 0:GROUPS],
                           a["w_router_group"][0].rearrange("(p k) n -> p k n", k=KT)).then_inc(small_in, 16)
            pool.dma_start(w_router[:, :, GROUPS:],
                           a["w_router_expert"][0].rearrange("(p k) n -> p k n", k=KT)).then_inc(small_in, 16)
            pool.dma_start(b_router[:, 0:GROUPS], a["b_router_group"].partition_broadcast(P)).then_inc(small_in, 16)
            pool.dma_start(b_router[:, GROUPS:], a["b_router_expert"].partition_broadcast(P)).then_inc(small_in, 16)
            pool.dma_start(sbk[:, 3, :].rearrange("p (h n) -> p h n", h=HEADS),
                           a["state_ret_bwd"][0, 0].rearrange("h d e -> d h e")).then_inc(state_in, 16)
            pool.dma_start(sfw.rearrange("p (h n) -> p h n", h=HEADS),
                           a["state_ret_fwd"][0, 0].rearrange("h d e -> d h e")).then_inc(state_in, 16)
            pool.wait_ge(zero_set, 1)
            pool.wait_ge(ring_in[slot_of(6)], 32)
            zin = zeros.rearrange("p (a n) -> p a n", a=1)
            pool.dma_start(xs_rows.rearrange("(a p) n -> p a n", p=P),
                           zin.broadcast_to([P, ROWS // P, D])).then_inc(zero_out, 16)
            pool.dma_start(y_rows[OV_ROW0:, :].rearrange("(a p) n -> p a n", p=P),
                           zin.broadcast_to([P, OVB * BLK // P, D])).then_inc(zero_out, 16)
            pool.wait_ge(st_ready, 5)
            for d, dst in enumerate((new_f, new_b)):
                pool.dma_start(dst[0, 0].rearrange("h d e -> d h e"),
                               state_c[:, d, :].rearrange("p (h n) -> p h n", h=HEADS)).then_inc(new_out, 16)
            for c in range(4):
                pool.wait_ge(modrow_ev, 2 * c + 2)
                pool.dma_start(mod_rows[c].rearrange("s (h n) -> s h n", h=2), modrow[32 * c:32 * c + 2, :, :]).then_inc(mod_out, 16)
            pool.wait_ge(yT_mm, NT)
            pool.wait_ge(o_mm, NT)
            pool.wait_ge(mod_out, 16 * 4)
            for c in (0, 2, 1, 3):
                pool.dma_start(rows[c], mod_rows[c].partition_broadcast(P)).then_inc(rows_in[c], 16)
                if c == 0:
                    pool.dma_start(g_ffn, a["norm_ffn_g"].partition_broadcast(P)).then_inc(gffn_in, 16)
            pool.wait_ge(zero_out, 32)
            for t in range(NT):
                pool.wait_ge(placed, t + 1)
                for j in range(2):
                    pool.indirect_dma_start(xs_rows, bass.IndirectOffsetOnAxis(ap=pos_own[:, t, j:j + 1], axis=0),
                                            xn2[t], None, bounds_check=OV_ROW0 - 1, oob_is_err=False).then_inc(xs_out, 16)
            pool.wait_ge(routed, 1)
            count = pool.value_load(ov_tab[0:1, OVB:OVB + 1], min_val=0, max_val=OVB // 2 - 1)
            with pool.If(count > 0):
                for t in range(NT):
                    for j in range(2):
                        pool.indirect_dma_start(xs_rows, bass.IndirectOffsetOnAxis(ap=pos_ov[:, t, j:j + 1], axis=0),
                                                xn2[t], None, bounds_check=ROWS - 1, oob_is_err=False).then_inc(ov_out, 16)
                pool.wait_ge(ov_out, 16 * 2 * NT)
            pool.sem_inc(ov_done, 1)
            pool.wait_ge(xs_out, 16 * 2 * NT)
            pool.dma_start(g_fin, a["final_norm_g"].partition_broadcast(P)).then_inc(gfin_in, 16)
            pool.wait_ge(y_all, 1)
            for t in range(NT):
                for j in range(2):
                    pool.indirect_dma_start(got[:, t, j, :], None, y_rows,
                                            bass.IndirectOffsetOnAxis(ap=posi[:, t, j:j + 1], axis=0)).then_inc(got_in[t], 16)

        @block.scalar
        def _(act):
            act.dma_start(decay[:, 0, 0:4], a["ret_decay_fwd"].partition_broadcast(P)).then_inc(decay_in, 16)
            act.dma_start(decay[:, 0, 4:8], a["ret_decay_bwd"].partition_broadcast(P)).then_inc(decay_in, 16)
            act.dma_start(early, a["c_early"]).then_inc(decay_in, 16)
            act.wait_ge(c_in, 16 * 3)
            act.wait_ge(cs_zero, 1)
            for s in range(2):
                act.activation(cs[:, :, s], cvec[:, s, :], ACT.Silu).then_inc(cs_ready, 1)
            act.wait_ge(x_in, 32)
            for t in range(NT):
                if t >= 2:
                    act.wait_ge(ssq_done, t - 1)
                act.activation(xs[:, t % 2, :], x[:, t, :], ACT.Square, accum_out=stat[:, 0, t:t + 1]).then_inc(ssq_done, 1)
            act.wait_ge(ms_done, 1)
            act.activation(stat[:, 2, :], stat[:, 1, :], ACT.Sqrt).then_inc(root_done, 1)
            act.wait_ge(rstd_done, 1)
            act.wait_ge(ssq_done, NT)

            def xT_evacuate(t):
                act.wait_ge(xT_mm, 2 * t + 2)
                act.activation(xnT[:, 4:8, P * t:P * t + P], bank[5 + 2 * (t % 2)][:, :].rearrange("p (k t) -> p k t", k=4),
                               ACT.Copy).then_inc(xT_act, 1)

            for t in range(NT):
                if t >= 2:
                    act.wait_ge(xT_mm, 2 * (t - 1))
                act.activation(xs[:, t % 2, :].rearrange("p (k q) -> p q k", q=P),
                               x[:, t, :].rearrange("p (q k) -> p q k", q=P), ACT.Copy,
                               scale=stat[:, 3, t:t + 1]).then_inc(xs_ready, 1)
                if t >= 1:
                    xT_evacuate(t - 1)
            xT_evacuate(NT - 1)
            act.wait_ge(col_ready, 2)
            act.wait_ge(xT_dve, 1)
            act.wait_ge(xT_act, 1)
            for kt in range(KT):
                act.activation(xnT[:, kt, 0:P], xnT[:, kt, 0:P], ACT.Identity, scale=scale[:, kt, 0:1],
                               bias=shift[:, kt, 0:1]).then_inc(xn_act, 1)
            act.wait_ge(decay_in, 16 * 3)
            act.activation(decay[:, 1, :], decay[:, 0, :], ACT.Exp).then_inc(dec_e, 1)
            act.wait_ge(dec_u, 1)
            act.activation(decay[:, 3, :], decay[:, 2, :], ACT.Ln).then_inc(dec_ln, 1)
            act.wait_ge(dec_lg, 1)
            for h in range(HEADS):
                act.activation(decay_tmp[:, 0, h, :], e("fwd_gap"), ACT.Exp, scale=decay[:, 5, h:h + 1])
                act.activation(decay_tmp[:, 1, h, :], e("bwd_gap"), ACT.Exp, scale=decay[:, 5, 4 + h:5 + h])
                act.activation(qdec[:, 0, h, :], e("q_pos_f"), ACT.Exp, scale=decay[:, 5, h:h + 1])
                act.activation(qdec[:, 1, h, :], e("q_pos_b"), ACT.Exp, scale=decay[:, 5, 4 + h:5 + h])
            for d in range(2):
                act.activation(cdec[:, d, :], decay[:, 5, 4 * d:4 * d + 4], ACT.Exp, scale=float(P))
                if d == 0:
                    act.wait_ge(kept_in, 16)
                last = act.activation(kdec[:, d, :], decay[:, 5, 4 * d:4 * d + 4], ACT.Exp, scale=k("k_pos")[:, d:d + 1])
            last.then_inc(dec_act, 1)
            for m in range(CB):
                act.wait_ge(proj_mm, m + 1)
                act.activation(u[:, m, 0:P], bank[2 + m % 2][:, 0:P], ACT.Copy)
                act.activation(u[:, m, P:], bank[m % 2][:, :], ACT.Copy).then_inc(conv_c_ev, 1)
            for n in range(4 * NT):
                s, t = n // NT, n % NT
                act.wait_ge(proj_mm, proj_groups(3) + n + 1)
                src = bank[4 + n % 4][:, :]
                if s == 0:
                    ins = act.activation(q[:, t, :], src, ACT.Copy)
                elif s == 1:
                    ins = act.activation(kk[:, t, :], src, ACT.Copy, scale=float(DH) ** -0.5)
                elif s == 2:
                    ins = act.activation(v[:, t, :], src, ACT.Copy)
                else:
                    if t == 0:
                        act.wait_ge(zero_out, 32)
                    ins = act.activation(gate[:, t, :], src, ACT.Silu)
                ins.then_inc(qkvg_ev, 1)
            def keys_T(t):
                act.wait_ge(qkT_mm, t + 1)
                if t >= 1:
                    act.wait_ge(sc_mm, t)
                act.activation(kT, bank[1][:, :], ACT.Copy).then_inc(kT_ev, 1)

            def mod_sum(s):
                n = s - ADA_FIRST
                act.wait_ge(mod_mm, s + 1)
                if n >= 1:
                    act.wait_ge(modrow_mm, n)
                act.activation(modsum[:, :], bank[6][:, :], ACT.Copy).then_inc(mod_ev, 1)

            def mod_row(s):
                n = s - ADA_FIRST
                c = n // 2
                act.wait_ge(modrow_mm, n + 1)
                act.activation(modrow[32 * c:32 * c + 2, n % 2, :], bank[7][32 * c:32 * c + 2, :], ACT.Copy).then_inc(modrow_ev, 1)

            keys_T(0)
            for t in range(NT):
                if t + 1 < NT:
                    keys_T(t + 1)
                act.wait_ge(o_mm, t + 1)
                act.activation(q[:, t, :], bank[3][:, :], ACT.Square).then_inc(osq_done, 1)
                act.wait_ge(oms_done, t + 1)
                act.activation(hstat[:, 1, :], hstat[:, 0, :], ACT.Sqrt).then_inc(oroot_done, 1)
                mod_sum(MOD_TURNS[t][0])
                if t >= 1:
                    mod_row(MOD_TURNS[t - 1][-1])
                act.wait_ge(yT_mm, t + 1)
                act.activation(yretT[:, t, :, :], bank[5][:, :].rearrange("p (m t) -> p m t", m=CB),
                               ACT.Copy).then_inc(yT_ev, 1)
                if len(MOD_TURNS[t]) > 1:
                    mod_row(MOD_TURNS[t][0])
                    mod_sum(MOD_TURNS[t][1])
            mod_row(MOD_TURNS[-1][-1])
            for t in range(NT):
                act.wait_ge(x1_ready, 2 * t + 2)
                if t >= 1:
                    act.wait_ge(ssq2_done, t)
                act.activation(square, x[:, t, :], ACT.Square, accum_out=stat[:, 0, t:t + 1]).then_inc(ssq2_done, 1)
                act.wait_ge(ms2_done, t + 1)
                act.activation(stat[:, 2, t:t + 1], stat[:, 1, t:t + 1], ACT.Sqrt).then_inc(root2_done, 1)
                if t >= 2:
                    act.wait_ge(rt_mm, t - 1)
                for half in range(2):
                    act.wait_ge(xn2T_mm, 2 * t + half + 1)
                    act.activation(xn2T[:, t % 2, 4 * half:4 * half + 4, :],
                                   bank[4 + half][:, :].rearrange("p (k t) -> p k t", k=4), ACT.Copy).then_inc(xn2T_ev, 1)

            def load_rows(p_, at):
                act.dma_start(xe[:, p_, :], xs_rows[bass.ds(at, P), :]).then_inc(xe_in[p_], 16)

            act.sem_inc(y_out[0], 32)
            act.sem_inc(y_out[1], 32)
            act.sem_inc(y_ev, 2)
            act.wait_ge(xs_out, 16 * 2 * NT)
            act.wait_ge(ssq2_done, NT)
            act.wait_ge(xn2_ready, NT)
            for n in range(2):
                act.dma_start(xe[:, n, :], xs_rows[P * n:P * n + P, :]).then_inc(xe_in[n], 16)

            def silu(n, p_):
                act.wait_ge(gu_mm, n + 1)
                act.activation(sgate[BLK:2 * BLK, p_, :], bank[2 + p_][0:BLK, 0:DE], ACT.Silu).then_inc(silu_done, 1)

            def results(n, p_, stored_before):
                act.wait_ge(ht_mm, n + 1)
                act.activation(hidT[:, p_, :, :], bank[4 + p_][:, 0:2 * BLK].rearrange("p (c s) -> p c s", c=2),
                               ACT.Copy).then_inc(ht_ready, 1)
                act.wait_ge(down_mm, n + 1)
                act.wait_ge(y_out[p_], stored_before)
                act.activation(ysb[:, p_, :], bank[6 + p_][:, :], ACT.Copy).then_inc(y_ev, 1)
                act.wait_ge(y_ev, n + 3)
                for half in range(2):
                    act.dma_start(y_rows[bass.ds(n * BLK, BLK), SL * half:SL * half + SL],
                                  ysb[BLK * half:BLK * half + BLK, p_, :]).then_inc(y_out[p_], 16)

            act.wait_ge(exp_in, 1)
            act.activation(rt[:, 40:60], rt[:, 20:40], ACT.Exp)
            act.activation(rt[:, 65:70], rt[:, 60:65], ACT.Exp).then_inc(exp_out, 1)
            with act.Fori(0, EXPERTS // NSLOT) as i:
                for j in range(NSLOT):
                    n = i * NSLOT + j
                    silu(n, j % 2)
                    if j == 2:
                        act.wait_ge(ov_done, 1)
                    if j % 2 == 0:
                        load_rows(j // 2, n * BLK + 2 * P)
                    results(n, j % 2, i * (32 * NSLOT // 2) + 32 * (1 + j // 2))
            act.wait_ge(routed, 1)
            count = act.value_load(ov_tab[0:1, OVB:OVB + 1], min_val=0, max_val=OVB // 2 - 1)
            with act.If(count > 0):
                with act.Fori(0, count) as m:
                    act.wait_ge(xe_mm, m * 2 + (EXPERTS + 2))
                    load_rows(0, m * P + (EXPERTS // 2 + 1) * P)
                    for j in range(2):
                        silu(m * 2 + (EXPERTS + j), j)
                    for j in range(2):
                        results(m * 2 + (EXPERTS + j), j, m * 32 + 32 * (1 + EXPERTS // 2))
            act.wait_ge(xe_in[0], 16 * (EXPERTS // 4 + 1))
            act.wait_ge(xe_in[1], 16 * (EXPERTS // 4 + 1))
            def first_part(t):
                act.wait_ge(got_in[t], 32)
                act.activation(got[:, t, 0, :], got[:, t, 0, :], ACT.Copy, scale=wsel[:, t, 0:1]).then_inc(part0_ready, 1)

            act.wait_ge(routed, 1)
            first_part(0)
            for t in range(NT):
                if t + 1 < NT:
                    first_part(t + 1)
                act.wait_ge(x2_ready, t + 1)
                if t >= 1:
                    act.wait_ge(ssq3_done, t)
                act.activation(sq7, x[:, t, :], ACT.Square, accum_out=stat[:, 0, t:t + 1]).then_inc(ssq3_done, 1)
                act.wait_ge(ms3_done, t + 1)
                act.activation(stat[:, 2, t:t + 1], stat[:, 1, t:t + 1], ACT.Sqrt).then_inc(root3_done, 1)

        @block.tensor
        def _(pe):
            def mod_slice(s, item, out):
                landed(pe, item)
                w = wide(item)
                pe.matmul(out[0:32, :], k("sel_bias")[0:ADA_ALL, 32 * s:32 * s + 32], b_ada[:, :], start=True, stop=False)
                for kt in range(KT):
                    j = kt % 4
                    last = pe.matmul(out[32 * j:32 * j + 32, :], cs[:, kt, :], w[:, kt, :],
                                     start=(0 < kt < 4), stop=(kt >= 4))
                last.then_inc(mod_mm, 1)

            pe.wait_ge(kept_in, 16)
            pe.wait_ge(c_in, 16 * 3)
            pe.wait_ge(cs_ready, 2)
            def normed_T(t):
                pe.wait_ge(xs_ready, t + 1)
                if t >= 2:
                    pe.wait_ge(xT_dve, t - 1)
                    pe.wait_ge(xT_act, t - 1)
                for half in range(2):
                    for c in range(4):
                        kt = 4 * half + c
                        last = pe.transpose(bank[4 + 2 * (t % 2) + half][:, P * c:P * c + P],
                                            xs[:, t % 2, P * kt:P * kt + P], ident)
                    last.then_inc(xT_mm, 1)

            for s in range(ADA_FIRST):
                if s >= 2:
                    pe.wait_ge(mod_ev, s - 1)
                mod_slice(s, s, bank[s % 2])
                if s == 1:
                    for t in range(NT):
                        normed_T(t)
                pe.wait_ge(mod_ev, s + 1)
                half = s % 2
                ms = modsum[:, :].rearrange("p (q k) -> p k q", k=KT)
                for kt in range(KT):
                    last = pe.matmul(bank[2 + s // 2][64 * half:64 * half + 64, 2 * kt:2 * kt + 2], ms[:, kt, :],
                                     k("sel_pair"), start=True, stop=True)
                last.then_inc(modcol_mm, 1)
            for n in range(3 * CB):
                s, m = n // CB, n % CB
                if m == 0:
                    landed(pe, ADA_FIRST + s)
                if n >= 2:
                    done = (conv_c_ev, conv_h_ev, conv_b_ev)[(n - 2) // CB]
                    pe.wait_ge(done, (n - 2) % CB + 1)
                w = wide(ADA_FIRST + s)
                for kt in range(KT):
                    if n == 0:
                        pe.wait_ge(xn_dve, kt + 1)
                    pe.matmul(bank[n % 2][:, :], w[:, kt, P * m:P * m + P], xnT[:, kt, P:], start=(kt == 0), stop=(kt == KT - 1))
                if n == 0:
                    pe.wait_ge(xn_act, KT)
                for kt in range(KT):
                    last = pe.matmul(bank[2 + n % 2][:, 0:P], w[:, kt, P * m:P * m + P], xnT[:, kt, 0:P],
                                     start=(kt == 0), stop=(kt == KT - 1))
                last.then_inc(proj_mm, 1)
            def state_update(c, n):
                pe.wait_ge(kd_ready, n + 1)
                if n >= 1:
                    pe.wait_ge(st_ready, n)
                for h in range(HEADS):
                    last = pe.matmul(bank[st_bank(n)][:, DH * h:DH * h + DH], kd[:, DH * h:DH * h + DH], v[:, c, DH * h:DH * h + DH],
                                     start=True, stop=True)
                last.then_inc(st_mm, 1)

            for n in range(4 * NT):
                s, t = n // NT, n % NT
                if t == 0:
                    landed(pe, ADA_FIRST + 3 + s)
                if n >= 4:
                    pe.wait_ge(qkvg_ev, n - 3)
                w = wide(ADA_FIRST + 3 + s)
                for kt in range(KT):
                    last = pe.matmul(bank[4 + n % 4][:, :], xnT[:, kt, P * t:P * t + P], w[:, kt, :],
                                     start=(kt == 0), stop=(kt == KT - 1))
                last.then_inc(proj_mm, 1)
                if s == 3:
                    if t == 0:
                        pe.wait_ge(qkvg_ev, 3 * NT)
                        pe.wait_ge(conv_b_ev, CB)
                    state_update((4, 3, 2, 0, 0)[t], t)
            pe.wait_ge(qkvg_ev, 4 * NT)
            pe.wait_ge(rope_done, 8)
            pe.wait_ge(conv_b_ev, CB)
            pe.wait_ge(dec_done, 1)

            def query_key_T(t):
                if t >= 1:
                    pe.wait_ge(kT_ev, t)
                    pe.wait_ge(qT_ev, t)
                for h in range(HEADS):
                    pe.transpose(bank[0][:, P * h:P * h + P], q[:, t, DH * h:DH * h + DH], ident)
                for h in range(HEADS):
                    last = pe.transpose(bank[1][:, P * h:P * h + P], kk[:, t, DH * h:DH * h + DH], ident)
                last.then_inc(qkT_mm, 1)

            def scores(t):
                pe.wait_ge(kT_ev, t + 1)
                pe.wait_ge(qT_ev, t + 1)
                if t >= 1:
                    pe.wait_ge(sm_ready, t)
                for h in range(HEADS):
                    last = pe.matmul(bank[2][:, P * h:P * h + P], kT[:, P * h:P * h + P], qT[:, P * h:P * h + P],
                                     start=True, stop=True)
                last.then_inc(sc_mm, 1)

            def mod_row(s):
                c = (s - ADA_FIRST) // 2
                pe.wait_ge(mod_ev, s + 1)
                if s > ADA_FIRST:
                    pe.wait_ge(modrow_ev, s - ADA_FIRST)
                pe.matmul(bank[7][32 * c:32 * c + 2, :], k("sel_pair"), modsum[:, :], start=True, stop=True).then_inc(modrow_mm, 1)

            query_key_T(0)
            scores(0)
            for t in range(NT):
                if t + 1 < NT:
                    query_key_T(t + 1)
                pe.wait_ge(st_ready, 5 + max(t - 1, 0))
                pe.wait_ge(sm_ready, t + 1)
                if t >= 1:
                    pe.wait_ge(yr_ready, t)
                    pe.wait_ge(state_in, 32)
                for h in range(HEADS):
                    cols = slice(DH * h, DH * h + DH)
                    last = pe.matmul(bank[3][:, cols], sm[:, cols], v[:, t, cols], start=True, stop=(t == 0))
                    if t >= 1:
                        pe.matmul(bank[3][:, cols], qTf[t % 2][:, cols], sfw[:, cols], start=False, stop=False)
                        last = pe.matmul(bank[3][:, cols], qTb[t % 2][:, cols], sbk[:, t - 1, cols], start=False, stop=True)
                last.then_inc(o_mm, 1)
                if 1 <= t <= 3:
                    state_update(t, 4 + t)
                s = MOD_TURNS[t][0]
                mod_slice(s, N_IN + s, bank[6])
                if t + 1 < NT:
                    scores(t + 1)
                mod_row(s)
                pe.wait_ge(yr_ready, t + 1)
                if t >= 1:
                    pe.wait_ge(yT_ev, t)
                for h in range(HEADS):
                    last = pe.transpose(bank[5][:, P * h:P * h + P], q[:, t, DH * h:DH * h + DH], ident)
                last.then_inc(yT_mm, 1)
                for s in MOD_TURNS[t][1:]:
                    mod_slice(s, N_IN + s, bank[6])
                    mod_row(s)
            pe.wait_ge(yT_ev, NT)
            pe.wait_ge(modrow_ev, ADA_ALL - ADA_FIRST)

            def project(t, half):
                n = 2 * t + half
                if t == 0:
                    landed(pe, ADA_ALL + N_IN + half)
                if n >= 4:
                    pe.wait_ge(x1_ready, n - 3)
                w = wide(ADA_ALL + N_IN + half)
                for kt in range(KT):
                    lhs = yconvT[:, kt, P * t:P * t + P] if kt < CB else yretT[:, t, kt - CB, :]
                    last = pe.matmul(bank[n % 4][:, :], lhs, w[:, kt, :], start=(kt == 0), stop=(kt == KT - 1))
                last.then_inc(wout_mm, 1)

            def router_T(t):
                pe.wait_ge(xn2_ready, t + 1)
                for kt in range(KT):
                    if t >= 1 and kt % 4 == 0:
                        pe.wait_ge(xn2T_ev, 2 * t - 1 + kt // 4)
                    last = pe.transpose(bank[4 + kt // 4][:, P * (kt % 4):P * (kt % 4) + P], xn2[t][:, P * kt:P * kt + P], ident)
                    if kt % 4 == 3:
                        last.then_inc(xn2T_mm, 1)

            def router(t):
                pe.wait_ge(xn2T_ev, 2 * t + 2)
                if t >= 1:
                    pe.wait_ge(lg_ready, t)
                for kt in range(KT):
                    last = pe.matmul(bank[6][:, 0:GROUPS + EXPERTS], xn2T[:, t % 2, kt, :], w_router[:, kt, :],
                                     start=(kt == 0), stop=(kt == KT - 1))
                last.then_inc(rt_mm, 1)

            def ranks(t):
                pe.wait_ge(chosen, t + 1)
                if t >= 1:
                    pe.wait_ge(placed, t)
                both = rt[:, BOTH + EXPERTS * (t % 2):BOTH + EXPERTS * (t % 2) + EXPERTS]
                pe.matmul(bank[7][:, 0:32], k("before"), both, start=True, stop=True)
                pe.matmul(bank[7][:, 32:64], k("ones").broadcast_to([P, P]), both, start=True, stop=True).then_inc(rank_mm, 1)

            pe.wait_ge(small_in, 16 * 8)
            for t in range(NT):
                project(t, 0)
                if t >= 1:
                    router_T(t - 1)
                project(t, 1)
                if t >= 1:
                    router(t - 1)
                if t >= 2:
                    ranks(t - 2)
            router_T(NT - 1)
            router(NT - 1)
            ranks(NT - 2)
            ranks(NT - 1)

            def rows_T(p_, tiles):
                for kt in tiles:
                    last = pe.transpose(bank[kt // 4][:, P * (kt % 4):P * (kt % 4) + P], xe[:, p_, P * kt:P * kt + P], ident)
                    if kt % 4 == 3:
                        last.then_inc(xe_mm, 1)

            def gate_up(s, p_, pair, hid_before=None):
                for kt in range(KT):
                    lhs = xeT[:, pair, kt, BLK * p_:BLK * p_ + BLK]
                    pe.matmul(bank[2 + p_][0:BLK, 0:DE], lhs, w_gate(s)[:, kt, :], start=(kt == 0), stop=(kt == KT - 1))
                    if hid_before is not None and kt == KT - 1:
                        pe.wait_ge(hid_done, hid_before)
                    last = pe.matmul(bank[2 + p_][BLK:2 * BLK, 0:DE], lhs, w_up(s)[:, kt, :],
                                     start=(kt == 0), stop=(kt == KT - 1))
                last.then_inc(gu_mm, 1)

            def hidden_T(p_):
                for c in range(2):
                    last = pe.transpose(bank[4 + p_][:, BLK * c:BLK * c + BLK], hid[0:BLK, p_, P * c:P * c + P],
                                        ident[0:BLK, 0:BLK])
                last.then_inc(ht_mm, 1)

            def down(s, p_, hid_next=None):
                for c in range(2):
                    for half in range(2):
                        if hid_next is not None and c == 1 and half == 1:
                            pe.wait_ge(hid_done, hid_next)
                        last = pe.matmul(bank[6 + p_][BLK * half:BLK * half + BLK, :], hidT[:, p_, c, :],
                                         w_down(s)[:, c, SL * half:SL * half + SL], start=(c == 0), stop=(c == 1))
                last.then_inc(down_mm, 1)

            pe.wait_ge(placed, NT)
            pe.wait_ge(xe_in[0], 16)
            rows_T(0, range(KT))
            with pe.Fori(0, EXPERTS // NSLOT) as i:
                for j in range(NSLOT):
                    n = i * NSLOT + j
                    s, p_, pair = e_slot[j], j % 2, j // 2
                    pe.wait_ge(ring_in[s], i * 48 + (16 * early_uses[s] + 48))
                    pe.wait_ge(xe_ready, i * NSLOT + 2 * (pair + 1))
                    pe.wait_ge(hid_done, n + 1)
                    gate_up(s, p_, pair)
                    pe.wait_ge(xe_in[1 - pair], i * 16 + 16 * (1 + pair))
                    rows_T(1 - pair, range(4 * p_, 4 * p_ + 3))
                    pe.wait_ge(hid_done, n + 3)
                    rows_T(1 - pair, range(4 * p_ + 3, 4 * p_ + 4))
                    hidden_T(p_)
                    pe.wait_ge(ht_ready, n + 1)
                    pe.wait_ge(y_ev, n + 1)
                    down(s, p_)
            pe.wait_ge(routed, 1)
            count = pe.value_load(ov_tab[0:1, OVB:OVB + 1], min_val=0, max_val=OVB // 2 - 1)
            with pe.If(count > 0):
                with pe.Fori(0, count) as m:
                    for j in range(2):
                        s = e_slot[j]
                        pe.wait_ge(ring_in[s], m * 48 + (16 * early_uses[s] + 48 * (EXPERTS // NSLOT + 1)))
                        if j == 0:
                            pe.wait_ge(xe_ready, m * 2 + (EXPERTS + 2))
                        gate_up(s, j, 0, None if j == 0 else m * 2 + (EXPERTS + 3))
                    for j in range(2):
                        hidden_T(j)
                        pe.wait_ge(ht_ready, m * 2 + (EXPERTS + 1 + j))
                        pe.wait_ge(y_ev, m * 2 + (EXPERTS + 1 + j))
                        down(e_slot[j], j, m * 2 + (EXPERTS + 4) if j == 0 else None)
                    pe.wait_ge(xe_in[0], m * 16 + 16 * (EXPERTS // 4 + 2))
                    rows_T(0, range(KT))

        @block.vector
        def _(dve):
            steps = [0]

            def then(ins):
                steps[0] += 1
                ins.then_inc(step, 1)
                dve.wait_ge(step, steps[0])

            def tt(out, in0, in1, op):
                return dve.tensor_tensor(out, in0, in1, op)

            dve.memset(cs[:, :, :], 0.0).then_inc(cs_zero, 1)
            dve.memset(zeros, 0.0).then_inc(zero_set, 1)
            dve.wait_ge(ssq_done, NT)
            dve.tensor_scalar(stat[:, 1, :], stat[:, 0, :], 1.0 / D, EPS, ALU.mult, ALU.add).then_inc(ms_done, 1)
            dve.wait_ge(root_done, 1)
            dve.reciprocal(stat[:, 3, :], stat[:, 2, :]).then_inc(rstd_done, 1)
            for s in range(ADA_FIRST):
                dve.wait_ge(mod_mm, s + 1)
                if s >= 1:
                    dve.wait_ge(modcol_mm, s)
                dve.tensor_copy(modsum[:, :], bank[s % 2][:, :]).then_inc(mod_ev, 1)
                if s == 0:
                    for t in range(NT):
                        dve.wait_ge(xT_mm, 2 * t + 1)
                        dve.tensor_copy(xnT[:, 0:4, P * t:P * t + P],
                                        bank[4 + 2 * (t % 2)][:, :].rearrange("p (k t) -> p k t", k=4)).then_inc(xT_dve, 1)
            dve.wait_ge(modcol_mm, ADA_FIRST)
            dve.wait_ge(g_mix_in, 16)
            pair = lambda b: bank[b][:, 0:2 * KT].rearrange("p (k s) -> p k s", s=2)
            dve.tensor_copy(shift[:, :, :], pair(2)).then_inc(col_ready, 1)
            dve.scalar_tensor_tensor(out=scale[:, :, :], in0=pair(3), scalar=1.0,
                                     in1=g_mix[:, :].rearrange("p (k a) -> p k a", a=1).broadcast_to([P, KT, 2]),
                                     op0=ALU.add, op1=ALU.mult).then_inc(col_ready, 1)
            dve.wait_ge(col_ready, 2)
            dve.wait_ge(xT_act, NT)
            dve.wait_ge(xT_dve, NT)
            for kt in range(KT):
                dve.tensor_scalar(xnT[:, kt, P:], xnT[:, kt, P:], scale[:, kt, 1:2], shift[:, kt, 1:2],
                                  ALU.mult, ALU.add).then_inc(xn_dve, 1)
            dve.wait_ge(dec_e, 1)
            dve.tensor_scalar(decay[:, 2, :], decay[:, 1, :], -1.0, 1.0, ALU.mult, ALU.add).then_inc(dec_u, 1)
            dve.wait_ge(dec_u, 1)
            then(dve.tensor_scalar(decay[:, 4, :], decay[:, 2, :], -1.0, 1.0, ALU.mult, ALU.add))
            then(dve.tensor_scalar(decay[:, 5, :], decay[:, 4, :], 0.0, None, ALU.is_equal))
            then(tt(decay[:, 4, :], decay[:, 4, :], decay[:, 5, :], ALU.add))
            then(dve.reciprocal(decay[:, 4, :], decay[:, 4, :]))
            dve.wait_ge(dec_ln, 1)
            then(tt(decay[:, 3, :], decay[:, 3, :], decay[:, 5, :], ALU.subtract))
            then(tt(decay[:, 3, :], decay[:, 3, :], decay[:, 4, :], ALU.mult))
            tt(decay[:, 5, :], decay[:, 3, :], decay[:, 1, :], ALU.mult).then_inc(dec_lg, 1)
            dve.wait_ge(dec_act, 1)

            def heads_of(row):
                return row.rearrange("p (a n) -> p a n", a=1).broadcast_to([P, HEADS, P])

            then(tt(mask[:, :, :], decay_tmp[:, 0], heads_of(e("fwd_on")), ALU.mult))
            then(tt(decay_tmp[:, 1], decay_tmp[:, 1], heads_of(e("bwd_on")), ALU.mult))
            tt(mask[:, :, :], mask[:, :, :], decay_tmp[:, 1], ALU.add).then_inc(dec_done, 1)
            for m in range(CB):
                dve.wait_ge(proj_mm, CB + m + 1)
                dve.wait_ge(conv_c_ev, CB)
                tt(u[:, m, 0:P], u[:, m, 0:P], bank[2 + m % 2][:, 0:P], ALU.mult)
                tt(u[:, m, P:], u[:, m, P:], bank[m % 2][:, :], ALU.mult).then_inc(conv_h_ev, 1)
            dve.wait_ge(small_in, 16 * 8)
            dve.wait_ge(conv_h_ev, CB)
            spans = ((0, P, P), (P, TOK, GRID_W))
            for m in range(CB):
                for lo, hi, w in spans:
                    o = yconvT[:, m, lo:hi].rearrange("p (r w) -> p r w", w=w)
                    i_ = u[:, m, lo:hi].rearrange("p (r w) -> p r w", w=w)
                    then(dve.tensor_scalar(o, i_, conv_w[:, 1, m:m + 1], None, ALU.mult))
                    then(dve.scalar_tensor_tensor(out=o[:, :, 1:], in0=i_[:, :, 0:w - 1], scalar=conv_w[:, 0, m:m + 1],
                                                  in1=o[:, :, 1:], op0=ALU.mult, op1=ALU.add))
                    then(dve.scalar_tensor_tensor(out=o[:, :, 0:w - 1], in0=i_[:, :, 1:], scalar=conv_w[:, 2, m:m + 1],
                                                  in1=o[:, :, 0:w - 1], op0=ALU.mult, op1=ALU.add))
            for m in range(CB):
                dve.wait_ge(proj_mm, 2 * CB + m + 1)
                tt(yconvT[:, m, 0:P], yconvT[:, m, 0:P], bank[2 + m % 2][:, 0:P], ALU.mult)
                tt(yconvT[:, m, P:], yconvT[:, m, P:], bank[m % 2][:, :], ALU.mult).then_inc(conv_b_ev, 1)
            for n in range(2 * (NT - 1)):
                dst = (q, kk)[n // (NT - 1)]
                t = n % (NT - 1) + 1
                dve.wait_ge(qkvg_ev, NT * (n // (NT - 1)) + t + 1)
                heads = lambda r: r.rearrange("p (a n) -> p a n", a=1).broadcast_to([P, HEADS, DH])
                cur = dst[:, t, :].rearrange("p (h n) -> p h n", h=HEADS)
                pairs = cur.rearrange("p h (n two) -> p h n two", two=2)
                t0 = rope_tmp[:, 0, :].rearrange("p (h n) -> p h n", h=HEADS)
                t1 = rope_tmp[:, 1, :].rearrange("p (h n two) -> p h n two", h=HEADS, two=2)
                sn = heads(rope[:, 1, t - 1, :]).rearrange("p h (n two) -> p h n two", two=2)
                if n:
                    dve.wait_ge(rope_done, n)
                tt(t0, cur, heads(rope[:, 0, t - 1, :]), ALU.mult)
                tt(t1[:, :, :, 0], pairs[:, :, :, 1], sn[:, :, :, 0], ALU.mult)
                then(tt(t1[:, :, :, 1], pairs[:, :, :, 0], sn[:, :, :, 1], ALU.mult))
                tt(cur, t0, rope_tmp[:, 1, :].rearrange("p (h n) -> p h n", h=HEADS), ALU.add).then_inc(rope_done, 1)

            def col_heads(c):
                return c.rearrange("p (h a) -> p h a", a=1).broadcast_to([P, HEADS, DH])

            def decay_keys(c, d, before):
                if before:
                    dve.wait_ge(st_mm, before)
                tt(kd.rearrange("p (h n) -> p h n", h=HEADS), kk[:, c, :].rearrange("p (h n) -> p h n", h=HEADS),
                   col_heads(kdec[:, d, :]), ALU.mult).then_inc(kd_ready, 1)

            dve.wait_ge(rope_done, 8)
            dve.wait_ge(state_in, 32)
            for n, c in enumerate((4, 3, 2)):
                decay_keys(c, 1, n)
                then(tt(sbk[:, c - 2, :].rearrange("p (h n) -> p h n", h=HEADS),
                        sbk[:, c - 1, :].rearrange("p (h n) -> p h n", h=HEADS), col_heads(cdec[:, 1, :]), ALU.mult))
                dve.wait_ge(st_mm, n + 1)
                tt(sbk[:, c - 2, :], sbk[:, c - 2, :], bank[st_bank(n)][:, :], ALU.add).then_inc(st_ready, 1)
                dve.wait_ge(st_ready, n + 1)
            for d in range(2):
                decay_keys(0, d, 3 + d)
                dve.wait_ge(st_mm, 4 + d)
                dve.tensor_copy(state_c[:, d, :], bank[st_bank(3 + d)][:, :]).then_inc(st_ready, 1)
            dve.wait_ge(qkvg_ev, 4 * NT)
            as_heads = lambda r: r.rearrange("p (h n) -> p h n", h=HEADS)

            def queries_T(t):
                dve.wait_ge(qkT_mm, t + 1)
                if t >= 1:
                    if t >= 3:
                        dve.wait_ge(o_mm, t - 1)
                    tt(qTf[t % 2], bank[0][:, :], qdec[:, 0, :, :].rearrange("p h n -> p (h n)"), ALU.mult)
                    tt(qTb[t % 2], bank[0][:, :], qdec[:, 1, :, :].rearrange("p h n -> p (h n)"), ALU.mult)
                    dve.wait_ge(sc_mm, t)
                dve.tensor_copy(qT, bank[0][:, :]).then_inc(qT_ev, 1)

            def masked(t):
                dve.wait_ge(sc_mm, t + 1)
                if t >= 1:
                    dve.wait_ge(o_mm, t)
                tt(sm, bank[2][:, :], mask[:, :, :].rearrange("p h n -> p (h n)"), ALU.mult).then_inc(sm_ready, 1)

            queries_T(0)
            masked(0)
            for t in range(NT):
                if t + 1 < NT:
                    queries_T(t + 1)
                if 1 <= t <= 3:
                    decay_keys(t, 0, 4 + t)
                dve.wait_ge(osq_done, t + 1)
                then(dve.tensor_reduce(hstat[:, 2, :], as_heads(q[:, t, :]), X, ALU.add))
                dve.tensor_scalar(hstat[:, 0, :], hstat[:, 2, :], 1.0 / DH, EPS, ALU.mult, ALU.add).then_inc(oms_done, 1)
                then(tt(q[:, t, :], bank[3][:, :], gate[:, t, :], ALU.mult))
                dve.wait_ge(oroot_done, t + 1)
                then(dve.reciprocal(hstat[:, 2, :], hstat[:, 1, :]))
                tt(as_heads(q[:, t, :]), as_heads(q[:, t, :]), col_heads(hstat[:, 2, :]), ALU.mult).then_inc(yr_ready, 1)
                if 1 <= t <= 3:
                    then(tt(as_heads(sfw), as_heads(sfw), col_heads(cdec[:, 0, :]), ALU.mult))
                    dve.wait_ge(st_mm, 5 + t)
                    tt(sfw, sfw, bank[4][:, :], ALU.add).then_inc(st_ready, 1)
                    dve.wait_ge(st_ready, 5 + t)
                if t + 1 < NT:
                    masked(t + 1)

            dve.wait_ge(rows_in[0], 16)

            def residual(t, half):
                n = 2 * t + half
                cols = slice(SL * half, SL * half + SL)
                dve.wait_ge(wout_mm, n + 1)
                if n:
                    dve.wait_ge(x1_ready, n)
                then(tt(part, bank[n % 4][:, :], rows[0][:, min(t, 1), cols], ALU.mult))
                tt(x[:, t, cols], x[:, t, cols], part, ALU.add).then_inc(x1_ready, 1)

            def second_norm(t):
                dve.wait_ge(x1_ready, 2 * t + 2)
                dve.wait_ge(scale2_ready, 1)
                dve.wait_ge(ssq2_done, t + 1)
                dve.tensor_scalar(stat[:, 1, t:t + 1], stat[:, 0, t:t + 1], 1.0 / D, EPS, ALU.mult, ALU.add).then_inc(ms2_done, 1)
                dve.wait_ge(root2_done, t + 1)
                then(dve.reciprocal(stat[:, 3, t:t + 1], stat[:, 2, t:t + 1]))
                side = min(t, 1)
                as_qk = lambda r: r.rearrange("p (q k) -> p q k", q=P)
                dst = xn2[t].rearrange("p (k q) -> p q k", q=P)
                then(dve.scalar_tensor_tensor(out=dst, in0=as_qk(x[:, t, :]), scalar=stat[:, 3, t:t + 1],
                                              in1=as_qk(rows[2][:, side, :]), op0=ALU.mult, op1=ALU.mult))
                tt(dst, dst, as_qk(rows[1][:, side, :]), ALU.add).then_inc(xn2_ready, 1)

            def over(ap, n):
                return ap.rearrange("p (t a) -> p t a", a=1).broadcast_to([P, ap.shape[1], n])

            def row_over(ap, n):
                return ap.rearrange("p (a m) -> p a m", a=1).broadcast_to([P, n, ap.shape[1]])

            eq4, eq8, top = rt[:, 100:104], rt[:, 104:112], rt[:, 112:113]
            ohg, oh1, oh2 = rt[:, 116:120], rt[:, 120:128], rt[:, 128:136]
            inner, inner2 = rt[:, 136:144], rt[:, 144:152]
            best = lambda j, t: rt[:, 160 + 5 * j + t:161 + 5 * j + t]
            choice = lambda j, t: rt[:, CHOICE[j] + 32 * t:CHOICE[j] + 32 * t + 32]
            both = lambda t: rt[:, BOTH + 32 * (t % 2):BOTH + 32 * (t % 2) + 32]
            rank = lambda t: rt[:, RANK + 32 * t:RANK + 32 * t + 32]
            before = lambda t: rt[:, BEFORE + 32 * t:BEFORE + 32 * t + 32]
            spread = rt[:, 200:232].rearrange("p (g j) -> p g j", g=GROUPS)
            own_row = rt[:, 800:832]
            far = rt[:, 832:864]
            posf = rt[:, 864:866]

            def first_max(values, desc, best, out):
                n = [P, values.shape[1]]
                tmp = eq4 if n[1] == GROUPS else eq8
                then(dve.tensor_reduce(best, values, X, ALU.max))
                then(tt(tmp, values, best.broadcast_to(n), ALU.is_equal))
                then(tt(tmp, tmp, desc, ALU.mult))
                then(dve.tensor_reduce(top, tmp, X, ALU.max))
                then(tt(out, tmp, top.broadcast_to(n), ALU.is_equal))

            def choose(t):
                dve.wait_ge(rt_mm, t + 1)
                tt(logits[:, t, :], bank[6][:, 0:GROUPS + EXPERTS], b_router[:, :], ALU.add).then_inc(lg_ready, 1)
                dve.wait_ge(lg_ready, t + 1)
                lgg, lge = logits[:, t, 0:GROUPS], logits[:, t, GROUPS:]
                first_max(lgg, k("desc_group"), best(0, t), ohg)
                tt(rt[:, 20 + 4 * t:24 + 4 * t], lgg, best(0, t).broadcast_to([P, GROUPS]), ALU.subtract)
                then(tt(spread, lge.rearrange("p (g j) -> p g j", g=GROUPS), over(ohg, PER_GROUP), ALU.mult))
                then(dve.tensor_reduce(inner, spread.rearrange("p g j -> p j g"), X, ALU.add))
                first_max(inner, k("desc_inner"), best(1, t), oh1)
                then(dve.scalar_tensor_tensor(out=inner2, in0=oh1, scalar=-1e30, in1=inner, op0=ALU.mult, op1=ALU.add))
                first_max(inner2, k("desc_inner"), best(2, t), oh2)
                for j, oh in enumerate((oh1, oh2)):
                    then(tt(choice(j, t).rearrange("p (g j) -> p g j", g=GROUPS), row_over(oh, GROUPS), over(ohg, PER_GROUP),
                            ALU.mult))
                tt(both(t), choice(0, t), choice(1, t), ALU.add).then_inc(chosen, 1)

            def place(t):
                dve.wait_ge(rank_mm, t + 1)
                then(tt(rank(t), bank[7][:, 0:32], before(t), ALU.add))
                then(tt(before(t + 1), bank[7][:, 32:64], before(t), ALU.add))
                then(dve.tensor_scalar(far, rank(t), float(BLK), float(FAR), ALU.is_ge, ALU.mult))
                then(tt(own_row, rank(t), k("block_row"), ALU.add))
                then(tt(own_row, own_row, far, ALU.add))
                for j in range(2):
                    then(tt(spread.rearrange("p g j -> p (g j)"), choice(j, t), own_row, ALU.mult))
                    then(dve.tensor_reduce(posf[:, j:j + 1], spread.rearrange("p g j -> p (g j)"), X, ALU.add))
                dve.tensor_copy(pos_own[:, t, :], posf).then_inc(placed, 1)

            for t in range(NT):
                residual(t, 0)
                if t == 2:
                    then(dve.memset(before(0), 0.0))
                if t >= 2:
                    choose(t - 2)
                residual(t, 1)
                if t == 0:
                    dve.wait_ge(rows_in[2], 16)
                    dve.wait_ge(gffn_in, 16)
                    for side in range(2):
                        last = dve.scalar_tensor_tensor(out=rows[2][:, side, :], in0=rows[2][:, side, :], scalar=1.0, in1=g_ffn,
                                                        op0=ALU.add, op1=ALU.mult)
                    last.then_inc(scale2_ready, 1)
                    dve.wait_ge(rows_in[1], 16)
                second_norm(t)
                if t >= 2:
                    place(t - 2)
            choose(NT - 2)
            place(NT - 2)
            choose(NT - 1)
            place(NT - 1)

            dve.sem_inc(hid_done, 2)
            dve.wait_ge(placed, NT)

            def rows_evacuate(pair, half):
                dve.tensor_copy(xeT[:, pair, 4 * half:4 * half + 4, :],
                                bank[half][:, :].rearrange("p (k s) -> p k s", k=4)).then_inc(xe_ready, 1)

            def hidden(p_):
                tt(hid[0:BLK, p_, :].rearrange("p (c q) -> p q c", c=2),
                   sgate[BLK:2 * BLK, p_, :].rearrange("p (q c) -> p q c", c=2),
                   bank[2 + p_][BLK:2 * BLK, 0:DE].rearrange("p (q c) -> p q c", c=2), ALU.mult).then_inc(hid_done, 1)

            def overflow_rows():
                flat2 = lambda lo: rt[:, lo:lo + NT * EXPERTS]
                total = before(NT)
                nov = rt[:, 1824:1856]
                grid = rt[:, BOTH:BOTH + EXPERTS * MAX_SPLIT].rearrange("p (e m) -> p e m", e=EXPERTS)
                tt(rt[:, 60:65], rt[:, 170:175], rt[:, 165:170], ALU.subtract).then_inc(exp_in, 1)
                then(tt(grid, over(total, MAX_SPLIT), row_over(k("splits"), EXPERTS), ALU.is_gt))
                then(dve.tensor_reduce(nov, grid, X, ALU.add))
                run = [rt[:, 1728:1776], rt[:, 1776:1824]]
                then(dve.memset(rt[:, 1728:1824], 0.0))
                then(dve.tensor_copy(run[0][:, 16:48], nov))
                cur = 0
                for hop in (1, 2, 4, 8, 16):
                    then(tt(run[1 - cur][:, 16:48], run[cur][:, 16:48], run[cur][:, 16 - hop:48 - hop], ALU.add))
                    cur = 1 - cur
                ends = run[cur][:, 16:48]
                jump = rt[:, 1856:1888]
                then(tt(jump, ends, nov, ALU.subtract))
                then(dve.tensor_scalar(jump, jump, float(BLK), float(OV_ROW0 - BLK), ALU.mult, ALU.add))
                then(tt(jump, jump, k("block_row"), ALU.subtract))
                beyond, row = rt[:, 2112:2272], flat2(RANK)
                te = lambda r: r.rearrange("p (t e) -> p t e", t=NT)
                then(dve.tensor_scalar(beyond, row, float(BLK), None, ALU.is_ge))
                then(tt(te(row), te(row), row_over(k("block_row"), NT), ALU.add))
                then(tt(te(rt[:, 2272:2432]), te(beyond), row_over(jump, NT), ALU.mult))
                then(tt(row, row, rt[:, 2272:2432], ALU.add))
                then(dve.tensor_scalar(beyond, beyond, float(-FAR), float(FAR), ALU.mult, ALU.add))
                then(tt(beyond, beyond, row, ALU.add))
                pos2 = rt[:, 2440:2450].rearrange("p (t j) -> p t j", j=2)
                pos3 = rt[:, 2450:2460].rearrange("p (t j) -> p t j", j=2)
                for j in range(2):
                    sel = flat2(CHOICE[j])
                    then(tt(rt[:, 2272:2432], sel, beyond, ALU.mult))
                    then(dve.tensor_reduce(pos3[:, :, j], te(rt[:, 2272:2432]), X, ALU.add))
                    then(tt(sel, sel, row, ALU.mult))
                    then(dve.tensor_reduce(pos2[:, :, j], te(sel), X, ALU.add))
                then(dve.tensor_copy(posi[:, :, :], pos2))
                then(dve.tensor_copy(pos_ov[:, :, :], pos3))
                return ends

            def weights_and_table(ends):
                dve.wait_ge(exp_out, 1)
                gsum, e21, w = rt[:, 0:5], rt[:, 65:70], rt[:, 5:10]
                then(dve.tensor_reduce(gsum, rt[:, 40:60].rearrange("p (t g) -> p t g", t=NT), X, ALU.add))
                then(dve.tensor_scalar(w, e21, 1.0, None, ALU.add))
                then(tt(w, w, gsum, ALU.mult))
                then(dve.reciprocal(w, w))
                then(dve.tensor_copy(wsel[:, :, 0], w))
                then(tt(wsel[:, :, 1], w, e21, ALU.mult))
                tab = rt[:, 2464:2465 + OVB]
                own = rt[:, 500:500 + OVB * EXPERTS].rearrange("p (b e) -> p b e", b=OVB)
                then(tt(own, row_over(ends, OVB), over(k("ov_index"), EXPERTS), ALU.is_le))
                then(dve.tensor_reduce(tab[:, 0:OVB], own, X, ALU.add))
                then(dve.tensor_scalar(tab[:, 0:OVB], tab[:, 0:OVB], float(EXPERTS - 1), None, ALU.min))
                pair_on = rt[:, 2490:2490 + OVB // 2]
                then(tt(pair_on, k("ov_index").rearrange("p (m two) -> p m two", two=2)[:, :, 0],
                        ends[:, EXPERTS - 1:EXPERTS].broadcast_to([P, OVB // 2]), ALU.is_lt))
                then(dve.tensor_reduce(tab[:, OVB:OVB + 1], pair_on, X, ALU.add))
                dve.tensor_copy(ov_tab[:, :], tab).then_inc(routed, 1)

            ends = overflow_rows()
            for half in range(2):
                dve.wait_ge(xe_mm, half + 1)
                rows_evacuate(0, half)
            weights_and_table(ends)
            with dve.Fori(0, EXPERTS // NSLOT) as i:
                for j in range(NSLOT):
                    n = i * NSLOT + j
                    dve.wait_ge(silu_done, n + 1)
                    hidden(j % 2)
                    dve.wait_ge(xe_mm, n + 3)
                    rows_evacuate(1 - j // 2, j % 2)
            count = dve.value_load(ov_tab[0:1, OVB:OVB + 1], min_val=0, max_val=OVB // 2 - 1)
            with dve.If(count > 0):
                with dve.Fori(0, count) as m:
                    for j in range(2):
                        dve.wait_ge(silu_done, m * 2 + (EXPERTS + 1 + j))
                        hidden(j)
                    for half in range(2):
                        dve.wait_ge(xe_mm, m * 2 + (EXPERTS + 3 + half))
                        rows_evacuate(0, half)

            dve.wait_ge(gfin_in, 16)
            dve.wait_ge(rows_in[3], 16)
            dve.wait_ge(routed, 1)

            def combine(t):
                g0, g1 = got[:, t, 0, :], got[:, t, 1, :]
                dve.wait_ge(got_in[t], 32)
                dve.wait_ge(part0_ready, t + 1)
                then(dve.scalar_tensor_tensor(out=g0, in0=g1, scalar=wsel[:, t, 1:2], in1=g0, op0=ALU.mult, op1=ALU.add))
                then(tt(g0, g0, rows[3][:, min(t, 1), :], ALU.mult))
                tt(x[:, t, :], x[:, t, :], g0, ALU.add).then_inc(x2_ready, 1)

            def final_norm(t):
                dve.wait_ge(ssq3_done, t + 1)
                dve.tensor_scalar(stat[:, 1, t:t + 1], stat[:, 0, t:t + 1], 1.0 / D, EPS, ALU.mult, ALU.add).then_inc(ms3_done, 1)
                dve.wait_ge(root3_done, t + 1)
                then(dve.reciprocal(stat[:, 3, t:t + 1], stat[:, 2, t:t + 1]))
                if t >= 2:
                    dve.wait_ge(stored[t % 2], 16 * (t // 2))
                dve.wait_ge(x2_ready, t + 1)
                dve.scalar_tensor_tensor(out=outb[:, t % 2, :], in0=x[:, t, :], scalar=stat[:, 3, t:t + 1], in1=g_fin,
                                         op0=ALU.mult, op1=ALU.mult).then_inc(out_ready, 1)

            combine(0)
            for t in range(NT):
                if t + 1 < NT:
                    combine(t + 1)
                final_norm(t)


_OUTS = [((1, P, D), "float32"), ((1, LAT, D), "float32"), ((1, 1, HEADS, DH, DH), "float32"),
         ((1, 1, HEADS, DH, DH), "float32")]
_INS = ["x_prompt", "x_sample", "state_ret_fwd", "state_ret_bwd", "c", "c_ctx", "norm_mix_g", "norm_ffn_g", "w_ada",
        "b_ada", "w_in", "conv_w", "ret_decay_fwd", "ret_decay_bwd", "w_out", "w_router_group", "b_router_group",
        "w_router_expert", "b_router_expert", "w_gate_e", "w_up_e", "w_down_e", "final_norm_g"]


def kernel(**inputs):
    import concourse.bacc as bacc
    from concourse.bass_utils import run_bass_kernel_spmd as run

    kept, early, rope = const_table()
    arrays = {f"in_{n}": np.ascontiguousarray(inputs[n]) for n in _INS}
    arrays["in_final_norm_g"] = arrays["in_final_norm_g"].reshape(1, D)
    arrays["in_c_kept"], arrays["in_c_early"], arrays["in_c_rope"] = kept, early, rope
    nc = bacc.Bacc("TRN2", target_bir_lowering=False, num_devices=1)
    a = {n[3:]: nc.dram_tensor(n, v.shape, mybir.dt.from_np(v.dtype), kind="ExternalInput").ap() for n, v in arrays.items()}
    outs = [nc.dram_tensor(f"out_{i}", s, mybir.dt.from_np(np.dtype(d)), kind="ExternalOutput").ap()
            for i, (s, d) in enumerate(_OUTS)]
    layer(nc, a, *outs)
    r = run(nc, [arrays], core_ids=[0])
    return tuple(r.results[0][f"out_{i}"] for i in range(len(_OUTS)))
```

```python
from contextlib import ExitStack

import numpy as np

import concourse.bass as bass
from concourse import mybir

P = 128
D = 1024
KT = D // P
NT = 5
TOK = NT * P
LAT = TOK - P
GRID_W = 64
CB = 4
HEADS = 4
DH = 128
W = HEADS * DH
SL = 512
EXPERTS = 32
GROUPS = 4
PER_GROUP = 8
DE = 256
BLK = 64
OVB = 22
MAX_SPLIT = TOK // BLK - 1
OV_ROW0 = EXPERTS * BLK
ROWS = OV_ROW0 + OVB * BLK
EPS = 1e-6
NSLOT = 4
SLOT = KT * 2 * DE + 2 * D
ADA_FIRST = 4
ADA_ALL = 12
N_IN = 7
IN_ORDER = (1, 2, 0, 3, 4, 5, 6)
FIRST_EXPERT_ITEM = ADA_ALL + N_IN + 2
POOL_SUMS = (1, 2, 3)
X_TURNS = ((0, 1), (2, 3), (4,), ())
MOD_TURNS = ((4, 5), (6, 7), (8, 9), (10,), (11,))
FAR = 65536
QUARTER = SL // 4
PIECE = KT * QUARTER
PIECES = 4 * N_IN
CONV_PIECES = 12
HALF_TOK = TOK // 2
SLOTS = (3, 0, 1, 2) + (0, 1, 2, 0, 1, 2, 0) + (1, 2, 0, 3, 1, 2, 0, 3) + (1, 2)
E_SLOTS = (0, 3, 1, 2)
CHOICE = (640, 1280)
RANK = 256
BEFORE = 1920
BOTH = 1440

F32 = mybir.dt.float32
F32R = mybir.dt.float32r
I32 = mybir.dt.int32
ALU = mybir.AluOpType
ACT = mybir.ActivationFunctionType
X = mybir.AxisListType.X

CONSTS = {}


def const_table():
    i = np.arange(P, dtype=np.float64)
    parts = {}
    parts["ident"] = np.eye(P)
    parts["before"] = (i[:, None] < i[None, :]) * 1.0
    parts["ones"] = np.ones((P, 1))
    parts["sel_pair"] = np.stack([i % 32 == 0, i % 32 == 1], 1) * 1.0
    bias = np.zeros((P, ADA_ALL, 32))
    for s in range(ADA_ALL):
        bias[s, s, 0:2] = 1.0
    parts["sel_bias"] = bias.reshape(P, -1)
    parts["k_pos"] = np.stack([P - 1 - i, i], 1)
    bc = lambda row: np.repeat(np.asarray(row, np.float64).reshape(1, -1), P, 0)
    parts["desc_group"] = bc(GROUPS - np.arange(GROUPS))
    parts["desc_inner"] = bc(PER_GROUP - np.arange(PER_GROUP))
    parts["splits"] = bc(BLK * (1 + np.arange(MAX_SPLIT)))
    parts["block_row"] = bc(BLK * np.arange(EXPERTS))
    parts["ov_index"] = bc(np.arange(OVB))
    early = {}
    early["fwd_gap"] = np.maximum(i[None, :] - i[:, None], 0)
    early["bwd_gap"] = np.maximum(i[:, None] - i[None, :], 0)
    early["fwd_on"] = (i[None, :] >= i[:, None]) * 1.0
    early["bwd_on"] = (i[:, None] >= i[None, :]) * 1.0
    early["q_pos_f"] = bc(i + 1)
    early["q_pos_b"] = bc(P - i)
    pos = np.arange(LAT)
    pairs = DH // 4
    freqs = (10000.0 ** (-(np.arange(pairs, dtype=np.float32) * 2.0 / (DH // 2)))).astype(np.float32)
    ang = np.concatenate([(pos // GRID_W).astype(np.float32)[:, None] * freqs,
                          (pos % GRID_W).astype(np.float32)[:, None] * freqs], -1)
    cos, sin = np.cos(ang.astype(np.float64)), np.sin(ang.astype(np.float64))
    c2 = np.repeat(cos, 2, 1)
    s2 = np.stack([-sin, sin], -1).reshape(LAT, DH)
    chunked = lambda a: a.reshape(LAT // P, P, DH).transpose(1, 0, 2).reshape(P, -1)
    rope = np.concatenate([chunked(c2), chunked(s2)], 1)
    at = 0
    for name, a in parts.items():
        CONSTS[name] = (at, at + a.shape[1])
        at += a.shape[1]
    at = 0
    for name, a in early.items():
        CONSTS[name] = (at, at + a.shape[1])
        at += a.shape[1]
    pack = lambda d: np.ascontiguousarray(np.concatenate(list(d.values()), 1).astype(np.float32))
    return pack(parts), pack(early), np.ascontiguousarray(rope.astype(np.float32))


def layer(nc, a, y_prompt, y_sample, new_f, new_b):
    kept_w = a["c_kept"].shape[1]
    early_w = a["c_early"].shape[1]
    xs_rows = nc.dram_tensor("expert_in_rows", (ROWS, D), F32, kind="Internal").ap()
    mod_rows = nc.dram_tensor("mod_rows", (4, 2, D), F32, kind="Internal").ap()
    y_rows = nc.dram_tensor("expert_out_rows", (ROWS, D), F32, kind="Internal").ap()

    with ExitStack() as ctx:
        def sb(name, shape, dt=F32):
            return ctx.enter_context(nc.sbuf_tensor(name, shape, dt))

        def sem(name):
            return ctx.enter_context(nc.semaphore(name))

        bank = [ctx.enter_context(nc.psum_tensor(f"bank{b}", [P, SL], F32)) for b in range(8)]

        def offset_of(words):
            return nc.sbuf_base - 4 * words

        def over_it(name, words, offset):
            return nc.alloc_sbuf_tensor_at(name, [P, words], F32R, offset=offset)

        ring = sb("ring", [P, NSLOT, SLOT])
        slot3 = offset_of(SLOT)
        w_hi = [over_it(f"w_hi{b}", PIECE, slot3 + 8 * PIECE * b) for b in range(2)]
        w_lo = [over_it(f"w_lo{b}", PIECE, slot3 + 8 * PIECE * b + 4 * PIECE) for b in range(2)]
        x = sb("x", [P, NT, D])
        xn_lo = over_it("xn_lo", KT * TOK, offset_of(NT * D))[:, :].rearrange("p (k t) -> p k t", k=KT)
        kept = sb("kept", [P, kept_w])
        cs = sb("cs", [P, KT, 32])
        cvec = sb("cvec", [P, 2, KT])
        b_ada = sb("b_ada_rows", [ADA_ALL, SL])
        modsum = sb("modsum", [P, SL])
        shift = sb("shift", [P, KT, 2])
        scale = sb("scale", [P, KT, 2])
        g_mix = sb("g_mix", [P, KT])
        conv_w = sb("conv_taps", [P, 3, CB])
        decay = sb("decay", [P, 6, 8])
        kdec = sb("kdec", [P, 2, HEADS])
        cdec = sb("cdec", [P, 2, HEADS])
        tail = [ring[:, s, KT * SL:SLOT] for s in range(NSLOT)]
        mask = tail[0][:, 0:512].rearrange("p (h n) -> p h n", h=HEADS)
        qdec = tail[0][:, 512:1536].rearrange("p (d h n) -> p d h n", d=2, h=HEADS)
        rope = tail[1][:, 0:1024].rearrange("p (d c n) -> p d c n", d=2, c=4)
        state_c = tail[1][:, 1024:2048].rearrange("p (d n) -> p d n", d=2)
        modrow = tail[2][:, 0:1024].rearrange("p (h n) -> p h n", h=2)
        stat = sb("stat", [P, 4, NT])
        hstat = sb("hstat", [P, 3, HEADS])
        w_router = sb("w_router", [P, KT, GROUPS + EXPERTS])
        b_router = sb("b_router", [P, GROUPS + EXPERTS])
        logits = sb("logits", [P, NT, GROUPS + EXPERTS])

        arena_a = sb("arena_a", [P, KT * TOK])
        xn_hi = over_it("xn_hi", KT * TOK, offset_of(KT * TOK))[:, :].rearrange("p (k t) -> p k t", k=KT)
        arena_b = sb("arena_b", [P, 4 * NT * W])
        arena_c = sb("arena_c", [P, CB * TOK])
        arena_d = sb("arena_d", [P, CB * TOK])

        def k(name):
            lo, hi = CONSTS[name]
            return kept[:, lo:hi]

        ident = k("ident")

        xnT = arena_b[:, 5120:10240].rearrange("p (k t) -> p k t", k=KT)
        q = arena_b[:, 0:2560].rearrange("p (t n) -> p t n", t=NT)
        kk = arena_b[:, 2560:5120].rearrange("p (t n) -> p t n", t=NT)
        v = arena_b[:, 5120:7680].rearrange("p (t n) -> p t n", t=NT)
        gate = arena_b[:, 7680:10240].rearrange("p (t n) -> p t n", t=NT)
        xs = arena_b[:, 0:2048].rearrange("p (b n) -> p b n", b=2)
        early = arena_b[:, 2560:2560 + early_w]
        decay_tmp = tail[2][:, 1024:2048].rearrange("p (b h n) -> p b h n", b=2, h=HEADS)
        zeros = tail[2][:, 0:1024]
        u = arena_c[:, :].rearrange("p (m t) -> p m t", m=CB)
        yconvT = arena_d[:, :].rearrange("p (m t) -> p m t", m=CB)
        rope_tmp = arena_c[:, 0:1024].rearrange("p (b n) -> p b n", b=2)

        def e(name):
            lo, hi = CONSTS[name]
            return early[:, lo:hi]

        yretT = arena_a[:, 0:2560].rearrange("p (t m n) -> p t m n", t=NT, m=CB)
        sbk = tail[3].rearrange("p (c n) -> p c n", c=4)
        sfw = tail[0][:, 1536:2048]
        qT, kT, qTf0, qTb0, sm = (arena_c[:, 512 * n:512 * n + 512] for n in range(5))
        qTf = [qTf0, tail[2][:, 1024:1536]]
        qTb = [qTb0, tail[2][:, 1536:2048]]
        kd = rope[:, 0, :, :].rearrange("p c n -> p (c n)")

        rows = [arena_b[:, 2 * D * c:2 * D * c + 2 * D].rearrange("p (s n) -> p s n", s=2) for c in range(4)]
        xn2T = arena_b[:, 8192:10240].rearrange("p (b k t) -> p b k t", b=2, k=KT)
        xn2 = [arena_a[:, D * ((t + 3) % NT):D * ((t + 3) % NT) + D] for t in range(NT)]
        part = arena_c[:, 0:512]
        square = arena_c[:, 512:1536]
        g_ffn = arena_c[:, 1536:2560]

        rt = arena_d[:, :]

        xe = arena_c[:, 0:2048].rearrange("p (b n) -> p b n", b=2)
        xeT = arena_b[:, 0:2048].rearrange("p (b k s) -> p b k s", b=2, k=KT)
        sgate = arena_b[:, 9216:9728].rearrange("p (b n) -> p b n", b=2)
        hid = arena_b[:, 9728:10240].rearrange("p (b n) -> p b n", b=2)
        hidT = arena_b[:, 2048:2304].rearrange("p (b c s) -> p b c s", b=2, c=2)
        ysb = arena_b[:, 8192:9216].rearrange("p (b n) -> p b n", b=2)
        posi = sb("posi", [P, NT, 2], I32)
        pos_own = sb("pos_own", [P, NT, 2], I32)
        pos_ov = sb("pos_ov", [P, NT, 2], I32)
        wsel = sb("wsel", [P, NT, 2])
        ov_tab = sb("ov_tab", [P, OVB + 1], I32)

        flat = ring[:, :, :].rearrange("p s n -> p (s n)")
        got = flat[:, 0:2 * NT * D].rearrange("p (t j n) -> p t j n", t=NT, j=2)
        outb = flat[:, 2 * NT * D:(2 * NT + 2) * D].rearrange("p (b n) -> p b n", b=2)
        sq7 = flat[:, (2 * NT + 2) * D:(2 * NT + 3) * D]
        g_fin = arena_a[:, 0:D]

        ring_in = [sem(f"ring_in{s}") for s in range(NSLOT)]
        c_in, kept_in, x_in, small_in = sem("c_in"), sem("kept_in"), sem("x_in"), sem("small_in")
        decay_in, g_mix_in = sem("decay_in"), sem("g_mix_in")
        state_in, gffn_in, gfin_in = sem("state_in"), sem("gffn_in"), sem("gfin_in")
        cs_zero, cs_ready = sem("cs_zero"), sem("cs_ready")
        mod_mm, mod_ev, modrow_mm, modcol_mm, modrow_ev, mod_out = (sem(n) for n in (
            "mod_mm", "mod_ev", "modrow_mm", "modcol_mm", "modrow_ev", "mod_out"))
        rows_in = [sem(f"rows_in{c}") for c in range(4)]
        scale2_ready = sem("scale2_ready")
        col_ready = sem("col_ready")
        ssq_done, ms_done, root_done, rstd_done = (sem(n) for n in ("ssq_done", "ms_done", "root_done", "rstd_done"))
        xs_ready, xT_mm, xT_act, xT_dve, xn_act, xn_dve = (sem(n) for n in (
            "xs_ready", "xT_mm", "xT_act", "xT_dve", "xn_act", "xn_dve"))
        xn_hi_ready, xn_lo_ready, w_hi_ready, w_lo_ready, quarter_mm, x_again = (sem(n) for n in (
            "xn_hi_ready", "xn_lo_ready", "w_hi_ready", "w_lo_ready", "quarter_mm", "x_again"))
        dec_e, dec_u, dec_ln, dec_lg, dec_act, dec_done = (sem(n) for n in (
            "dec_e", "dec_u", "dec_ln", "dec_lg", "dec_act", "dec_done"))
        zero_set, zero_out = sem("zero_set"), sem("zero_out")
        proj_mm, conv_c_ev, conv_h_ev, conv_b_ev = (sem(n) for n in ("proj_mm", "conv_c_ev", "conv_h_ev", "conv_b_ev"))
        qkvg_ev, rope_done = sem("qkvg_ev"), sem("rope_done")
        kd_ready, st_mm, st_ready, new_out = sem("kd_ready"), sem("st_mm"), sem("st_ready"), sem("new_out")
        qkT_mm, kT_ev, qT_ev, sc_mm, sm_ready, o_mm = (sem(n) for n in (
            "qkT_mm", "kT_ev", "qT_ev", "sc_mm", "sm_ready", "o_mm"))
        osq_done, oms_done, oroot_done, yr_ready, yT_mm, yT_ev = (sem(n) for n in (
            "osq_done", "oms_done", "oroot_done", "yr_ready", "yT_mm", "yT_ev"))
        wout_mm, x1_ready = sem("wout_mm"), sem("x1_ready")
        ssq2_done, ms2_done, root2_done, xn2_ready, xn2T_mm, xn2T_ev, rt_mm, lg_ready = (sem(n) for n in (
            "ssq2_done", "ms2_done", "root2_done", "xn2_ready", "xn2T_mm", "xn2T_ev", "rt_mm", "lg_ready"))
        exp_in, exp_out, chosen, rank_mm, placed, routed, xs_out, ov_out, ov_done = (sem(n) for n in (
            "exp_in", "exp_out", "chosen", "rank_mm", "placed", "routed", "xs_out", "ov_out", "ov_done"))
        xe_in = [sem("xe_in0"), sem("xe_in1")]
        xe_mm, xe_ready, gu_mm, silu_done, hid_done, ht_mm, ht_ready, down_mm, y_ev = (sem(n) for n in (
            "xe_mm", "xe_ready", "gu_mm", "silu_done", "hid_done", "ht_mm", "ht_ready", "down_mm", "y_ev"))
        y_out = [sem("y_out0"), sem("y_out1")]
        y_all = sem("y_all")
        got_in = [sem(f"got_in{t}") for t in range(NT)]
        part0_ready = sem("part0_ready")
        x2_ready = [sem(f"x2_ready{t}") for t in range(NT)]
        gated, ssq3_done, ms3_done, root3_done, out_ready = (sem(n) for n in (
            "gated", "ssq3_done", "ms3_done", "root3_done", "out_ready"))
        stored = [sem("stored0"), sem("stored1")]
        step = sem("dve_step")

        ada_v = a["w_ada"][0].rearrange("(p k) n -> p k n", k=KT)
        win_v = a["w_in"][0].rearrange("(p k) n -> p k n", k=KT)
        wout_v = a["w_out"][0].rearrange("(k p) n -> p k n", p=P)

        items = ([("ada", s) for s in range(ADA_FIRST)] + [("in", s) for s in range(N_IN)]
                 + [("ada", s) for s in range(ADA_FIRST, ADA_ALL)] + [("out", s) for s in range(2)])
        assert len(items) == FIRST_EXPERT_ITEM

        def proj_groups(n):
            return CB * min(n, 3) + NT * max(n - 3, 0)

        def st_bank(n):
            return 2 if n < 5 else 4

        def slot_of(item):
            return SLOTS[item]

        def landed(eng, item):
            eng.wait_ge(ring_in[slot_of(item)], 16 * SLOTS[:item + 1].count(SLOTS[item]))

        def wide(item):
            return ring[:, slot_of(item), 0:KT * SL].rearrange("p (k n) -> p k n", k=KT)

        early_uses = [SLOTS.count(s) for s in range(NSLOT)]
        e_slot = E_SLOTS

        def bank_of(n):
            return bank[(4 + n) % 8]

        def used_up(eng, piece):
            if piece < CONV_PIECES:
                eng.wait_ge(proj_mm, piece + 1)
            elif piece % 4 == 3:
                eng.wait_ge(proj_mm, proj_groups(piece // 4 + 1))
            else:
                eng.wait_ge(quarter_mm, (piece - CONV_PIECES) // 4 * 3 + piece % 4 + 1)

        def piece_of(w, piece):
            j = piece % 4
            if piece < CONV_PIECES:
                return w[:, :, QUARTER * j:QUARTER * j + QUARTER]
            return w[:, 2 * j:2 * j + 2, :]

        def as_piece(buf, piece):
            return buf[:, :].rearrange("p (k n) -> p k n", k=KT if piece < CONV_PIECES else 2)

        def w_gate(s):
            return ring[:, s, 0:KT * DE].rearrange("p (k n) -> p k n", k=KT)

        def w_up(s):
            return ring[:, s, KT * DE:2 * KT * DE].rearrange("p (k n) -> p k n", k=KT)

        def w_down(s):
            return ring[:, s, 2 * KT * DE:SLOT].rearrange("p (h n) -> p h n", h=2)

        def released(eng, slot, item):
            before = [n for n in range(item) if SLOTS[n] == slot]
            if not before:
                return
            kind, s = items[before[-1]]
            if slot == 3 and len(before) == 1:
                eng.wait_ge(proj_mm, proj_groups(N_IN))
            elif kind == "ada":
                eng.wait_ge(mod_mm, s + 1)
            elif kind == "in":
                eng.wait_ge(w_lo_ready, 4 * (s + 1))
            else:
                eng.wait_ge(wout_mm, 2 * NT - 1 + s)

        block = ctx.enter_context(nc.Block())

        @block.sync
        def _(sp):
            sp.dma_start(cvec[:, 0, :], a["c_ctx"].rearrange("(p k) -> p k", k=KT)).then_inc(c_in, 16)
            sp.dma_start(cvec[:, 1, :], a["c"][0].rearrange("(p k) -> p k", k=KT)).then_inc(c_in, 16)
            sp.dma_start(b_ada[:, :], a["b_ada"].rearrange("a (s n) -> (a s) n", n=SL)).then_inc(c_in, 16)
            sp.dma_start(kept[:, :], a["c_kept"]).then_inc(kept_in, 16)
            sp.dma_start(x[:, 0, :], a["x_prompt"][0]).then_inc(x_in, 16)
            sp.dma_start(x[:, 1:, :], a["x_sample"][0].rearrange("(t p) n -> p t n", p=P)).then_inc(x_in, 16)

            def expert_weights(s, gate_src, up_src, down_src):
                sp.dma_start(w_gate(s), gate_src).then_inc(ring_in[s], 16)
                sp.dma_start(w_up(s), up_src).then_inc(ring_in[s], 16)
                sp.dma_start(w_down(s), down_src).then_inc(ring_in[s], 16)

            for n, (kind, s) in enumerate(items):
                released(sp, slot_of(n), n)
                if kind == "ada":
                    src = ada_v[:, :, SL * s:SL * s + SL]
                elif kind == "in":
                    src = win_v[:, :, SL * IN_ORDER[s]:SL * IN_ORDER[s] + SL]
                else:
                    src = wout_v[:, :, SL * s:SL * s + SL]
                sp.dma_start(wide(n), src).then_inc(ring_in[slot_of(n)], 16)
            sp.wait_ge(new_out, 32)
            sp.wait_ge(mod_out, 16 * 4)
            for c in range(4):
                sp.wait_ge(rows_in[c], 16)
            gv = a["w_gate_e"][0].rearrange("e (p k) n -> e p k n", k=KT)
            uv = a["w_up_e"][0].rearrange("e (p k) n -> e p k n", k=KT)
            dv = a["w_down_e"][0].rearrange("e (p h) n -> e p h n", h=2)
            for j in range(NSLOT):
                released(sp, e_slot[j], FIRST_EXPERT_ITEM)
                expert_weights(e_slot[j], gv[j], uv[j], dv[j])
            with sp.Fori(1, EXPERTS // NSLOT) as i:
                for j in range(NSLOT):
                    sp.wait_ge(down_mm, i * NSLOT + (j + 1 - NSLOT))
                    ex = bass.ds(i * NSLOT + j, 1)
                    expert_weights(e_slot[j], gv[ex].rearrange("e p k n -> (e p) k n"),
                                   uv[ex].rearrange("e p k n -> (e p) k n"),
                                   dv[ex].rearrange("e p h n -> (e p) h n"))
            sp.wait_ge(routed, 1)
            count = sp.value_load(ov_tab[0:1, OVB:OVB + 1], min_val=0, max_val=OVB // 2 - 1)
            with sp.If(count > 0):
                with sp.Fori(0, count) as m:
                    for j in range(2):
                        sp.wait_ge(down_mm, m * 2 + (EXPERTS - 1 + j))
                        who = sp.value_load(ov_tab[0:1, bass.ds(m * 2 + j, 1)], min_val=0, max_val=EXPERTS - 1)
                        ex = bass.ds(who, 1)
                        expert_weights(e_slot[j], gv[ex].rearrange("e p k n -> (e p) k n"),
                                       uv[ex].rearrange("e p k n -> (e p) k n"),
                                       dv[ex].rearrange("e p h n -> (e p) h n"))
            sp.wait_ge(y_out[0], count * 32 + 32 * (1 + EXPERTS // 2))
            sp.wait_ge(y_out[1], count * 32 + 32 * (1 + EXPERTS // 2))
            sp.sem_inc(y_all, 1)
            for t in range(NT):
                sp.wait_ge(out_ready, t + 1)
                dst = y_prompt[0] if t == 0 else y_sample[0, P * (t - 1):P * t, :]
                sp.dma_start(dst, outb[:, t % 2, :]).then_inc(stored[t % 2], 16)
            sp.wait_ge(stored[0], 16 * 3)
            sp.wait_ge(stored[1], 16 * 2)

        @block.gpsimd
        def _(pool):
            pool.dma_start(g_mix[:, :], a["norm_mix_g"][0].rearrange("(p k) -> p k", k=KT)).then_inc(g_mix_in, 16)
            pool.wait_ge(zero_set, 1)
            for p_ in range(PIECES):
                pool.wait_ge(w_hi_ready, p_ + 1)
                w = wide(ADA_FIRST + p_ // 4)
                pool.tensor_tensor(as_piece(w_lo[p_ % 2], p_), piece_of(w, p_), as_piece(w_hi[p_ % 2], p_),
                                   ALU.subtract).then_inc(w_lo_ready, 1)
                if p_ == 1:
                    pool.dma_start(tail[1][:, 0:1024], a["c_rope"]).then_inc(small_in, 16)
                    for tap in range(3):
                        pool.dma_start(conv_w[:, tap, :], a["conv_w"][0, tap].rearrange("(m p) -> p m", p=P),
                                       allow_slow_non_contiguous=True).then_inc(small_in, 16)
                if p_ == 2:
                    pool.dma_start(w_router[:, :, 0:GROUPS],
                                   a["w_router_group"][0].rearrange("(p k) n -> p k n", k=KT)).then_inc(small_in, 16)
                    pool.dma_start(w_router[:, :, GROUPS:],
                                   a["w_router_expert"][0].rearrange("(p k) n -> p k n", k=KT)).then_inc(small_in, 16)
                    pool.dma_start(b_router[:, 0:GROUPS], a["b_router_group"].partition_broadcast(P)).then_inc(small_in, 16)
                    pool.dma_start(b_router[:, GROUPS:], a["b_router_expert"].partition_broadcast(P)).then_inc(small_in, 16)
                if p_ == 3:
                    pool.dma_start(sbk[:, 3, :].rearrange("p (h n) -> p h n", h=HEADS),
                                   a["state_ret_bwd"][0, 0].rearrange("h d e -> d h e")).then_inc(state_in, 16)
                    pool.dma_start(sfw.rearrange("p (h n) -> p h n", h=HEADS),
                                   a["state_ret_fwd"][0, 0].rearrange("h d e -> d h e")).then_inc(state_in, 16)
                if p_ == 5:
                    zin = zeros.rearrange("p (a n) -> p a n", a=1)
                    pool.dma_start(xs_rows.rearrange("(a p) n -> p a n", p=P),
                                   zin.broadcast_to([P, ROWS // P, D])).then_inc(zero_out, 16)
                    pool.dma_start(y_rows[OV_ROW0:, :].rearrange("(a p) n -> p a n", p=P),
                                   zin.broadcast_to([P, OVB * BLK // P, D])).then_inc(zero_out, 16)
            pool.wait_ge(st_ready, 5)
            for d, dst in enumerate((new_f, new_b)):
                pool.dma_start(dst[0, 0].rearrange("h d e -> d h e"),
                               state_c[:, d, :].rearrange("p (h n) -> p h n", h=HEADS)).then_inc(new_out, 16)
            def mod_rows_out(c):
                pool.wait_ge(modrow_ev, 2 * c + 2)
                pool.dma_start(mod_rows[c].rearrange("s (h n) -> s h n", h=2), modrow[32 * c:32 * c + 2, :, :]).then_inc(mod_out, 16)

            def rows_back(c):
                pool.dma_start(rows[c], mod_rows[c].partition_broadcast(P)).then_inc(rows_in[c], 16)

            for c in range(3):
                mod_rows_out(c)
            pool.wait_ge(yT_mm, NT)
            pool.wait_ge(o_mm, NT)
            pool.wait_ge(mod_out, 16 * 3)
            rows_back(0)
            pool.dma_start(g_ffn, a["norm_ffn_g"].partition_broadcast(P)).then_inc(gffn_in, 16)
            rows_back(2)
            rows_back(1)
            mod_rows_out(3)
            pool.wait_ge(mod_out, 16 * 4)
            rows_back(3)
            pool.wait_ge(zero_out, 32)
            for t in range(NT):
                pool.wait_ge(placed, t + 1)
                for j in range(2):
                    pool.indirect_dma_start(xs_rows, bass.IndirectOffsetOnAxis(ap=pos_own[:, t, j:j + 1], axis=0),
                                            xn2[t], None, bounds_check=OV_ROW0 - 1, oob_is_err=False).then_inc(xs_out, 16)
            pool.wait_ge(routed, 1)
            count = pool.value_load(ov_tab[0:1, OVB:OVB + 1], min_val=0, max_val=OVB // 2 - 1)
            with pool.If(count > 0):
                for t in range(NT):
                    for j in range(2):
                        pool.indirect_dma_start(xs_rows, bass.IndirectOffsetOnAxis(ap=pos_ov[:, t, j:j + 1], axis=0),
                                                xn2[t], None, bounds_check=ROWS - 1, oob_is_err=False).then_inc(ov_out, 16)
                pool.wait_ge(ov_out, 16 * 2 * NT)
            pool.sem_inc(ov_done, 1)
            pool.wait_ge(xs_out, 16 * 2 * NT)
            pool.dma_start(g_fin, a["final_norm_g"].partition_broadcast(P)).then_inc(gfin_in, 16)
            pool.wait_ge(y_all, 1)
            for t in range(NT):
                for j in range(2):
                    pool.indirect_dma_start(got[:, t, j, :], None, y_rows,
                                            bass.IndirectOffsetOnAxis(ap=posi[:, t, j:j + 1], axis=0)).then_inc(got_in[t], 16)
            for n, t in enumerate(POOL_SUMS):
                pool.wait_ge(gated, n + 1)
                pool.tensor_tensor(x[:, t, :], x[:, t, :], got[:, t, 0, :], ALU.add).then_inc(x2_ready[t], 1)

        @block.scalar
        def _(act):
            act.dma_start(decay[:, 0, 0:4], a["ret_decay_fwd"].partition_broadcast(P)).then_inc(decay_in, 16)
            act.dma_start(decay[:, 0, 4:8], a["ret_decay_bwd"].partition_broadcast(P)).then_inc(decay_in, 16)
            act.dma_start(early, a["c_early"]).then_inc(decay_in, 16)
            act.wait_ge(c_in, 16 * 3)
            act.wait_ge(cs_zero, 1)
            for s in range(2):
                act.activation(cs[:, :, s], cvec[:, s, :], ACT.Silu).then_inc(cs_ready, 1)
            act.wait_ge(x_in, 32)
            for t in range(NT):
                if t >= 2:
                    act.wait_ge(ssq_done, t - 1)
                act.activation(xs[:, t % 2, :], x[:, t, :], ACT.Square, accum_out=stat[:, 0, t:t + 1]).then_inc(ssq_done, 1)
            act.wait_ge(ms_done, 1)
            act.activation(stat[:, 2, :], stat[:, 1, :], ACT.Sqrt).then_inc(root_done, 1)
            act.wait_ge(rstd_done, 1)
            act.wait_ge(ssq_done, NT)

            def xT_evacuate(t):
                act.wait_ge(xT_mm, 2 * t + 2)
                act.activation(xnT[:, 4:8, P * t:P * t + P], bank[5 + 2 * (t % 2)][:, :].rearrange("p (k t) -> p k t", k=4),
                               ACT.Copy).then_inc(xT_act, 1)

            for t in range(NT):
                if t >= 2:
                    act.wait_ge(xT_mm, 2 * (t - 1))
                act.activation(xs[:, t % 2, :].rearrange("p (k q) -> p q k", q=P),
                               x[:, t, :].rearrange("p (q k) -> p q k", q=P), ACT.Copy,
                               scale=stat[:, 3, t:t + 1]).then_inc(xs_ready, 1)
                if t >= 1:
                    xT_evacuate(t - 1)
            xT_evacuate(NT - 1)

            def high_part(piece):
                if piece >= 2:
                    used_up(act, piece - 2)
                if piece % 4 == 0:
                    landed(act, ADA_FIRST + piece // 4)
                if piece == 0:
                    act.wait_ge(mod_mm, 1)
                w = wide(ADA_FIRST + piece // 4)
                act.activation(as_piece(w_hi[piece % 2], piece), piece_of(w, piece), ACT.Copy).then_inc(w_hi_ready, 1)

            high_part(0)
            act.wait_ge(col_ready, 2)
            act.wait_ge(xT_dve, 1)
            act.wait_ge(xT_act, 1)
            for kt in range(KT):
                act.activation(xnT[:, kt, 0:P], xnT[:, kt, 0:P], ACT.Identity, scale=scale[:, kt, 0:1],
                               bias=shift[:, kt, 0:1]).then_inc(xn_act, 1)
                act.wait_ge(xn_act, kt + 1)
                act.wait_ge(xn_dve, kt + 1)
                act.activation(xn_hi[:, kt, :], xnT[:, kt, :], ACT.Copy).then_inc(xn_hi_ready, 1)
                if kt == KT // 2:
                    high_part(1)

            def projected(n):
                s, t = n // NT, n % NT
                act.wait_ge(proj_mm, proj_groups(3) + n + 1)
                src = bank_of(n)[:, :]
                if s == 0:
                    ins = act.activation(q[:, t, :], src, ACT.Copy)
                elif s == 1:
                    ins = act.activation(kk[:, t, :], src, ACT.Copy, scale=float(DH) ** -0.5)
                elif s == 2:
                    ins = act.activation(v[:, t, :], src, ACT.Copy)
                else:
                    ins = act.activation(gate[:, t, :], src, ACT.Silu)
                ins.then_inc(qkvg_ev, 1)

            for p_ in range(PIECES):
                n = NT * ((p_ - CONV_PIECES) // 4)
                if p_ >= CONV_PIECES and p_ % 4 == 3:
                    for t in range(NT - 1):
                        projected(n + t)
                if p_ + 2 < PIECES:
                    high_part(p_ + 2)
                if p_ < CB:
                    act.wait_ge(proj_mm, p_ + 1)
                    for g in range(2):
                        last = act.activation(u[:, p_, HALF_TOK * g:HALF_TOK * g + HALF_TOK],
                                              bank[2 * g + p_ % 2][:, 0:HALF_TOK], ACT.Copy)
                    last.then_inc(conv_c_ev, 1)
                if p_ >= CONV_PIECES and p_ % 4 == 3:
                    projected(n + NT - 1)
                if p_ == 0:
                    act.wait_ge(decay_in, 16 * 3)
                    act.activation(decay[:, 1, :], decay[:, 0, :], ACT.Exp).then_inc(dec_e, 1)
                    act.wait_ge(dec_u, 1)
                    act.activation(decay[:, 3, :], decay[:, 2, :], ACT.Ln).then_inc(dec_ln, 1)
                if p_ == 1:
                    act.wait_ge(dec_lg, 1)
                    for h in range(HEADS):
                        act.activation(decay_tmp[:, 0, h, :], e("fwd_gap"), ACT.Exp, scale=decay[:, 5, h:h + 1])
                        act.activation(decay_tmp[:, 1, h, :], e("bwd_gap"), ACT.Exp, scale=decay[:, 5, 4 + h:5 + h])
                        act.activation(qdec[:, 0, h, :], e("q_pos_f"), ACT.Exp, scale=decay[:, 5, h:h + 1])
                        act.activation(qdec[:, 1, h, :], e("q_pos_b"), ACT.Exp, scale=decay[:, 5, 4 + h:5 + h])
                    for d in range(2):
                        act.activation(cdec[:, d, :], decay[:, 5, 4 * d:4 * d + 4], ACT.Exp, scale=float(P))
                        if d == 0:
                            act.wait_ge(kept_in, 16)
                        last = act.activation(kdec[:, d, :], decay[:, 5, 4 * d:4 * d + 4], ACT.Exp, scale=k("k_pos")[:, d:d + 1])
                    last.then_inc(dec_act, 1)
            act.wait_ge(proj_mm, proj_groups(N_IN))
            act.dma_start(x[:, 0, :], a["x_prompt"][0]).then_inc(x_again, 16)
            act.dma_start(x[:, 1:, :], a["x_sample"][0].rearrange("(t p) n -> p t n", p=P)).then_inc(x_again, 16)
            act.wait_ge(zero_out, 32)
            def keys_T(t):
                act.wait_ge(qkT_mm, t + 1)
                if t >= 1:
                    act.wait_ge(sc_mm, t)
                act.activation(kT, bank[1][:, :], ACT.Copy).then_inc(kT_ev, 1)

            def mod_sum(s):
                n = s - ADA_FIRST
                act.wait_ge(mod_mm, s + 1)
                if n >= 1:
                    act.wait_ge(modrow_mm, n)
                act.activation(modsum[:, :], bank[6][:, :], ACT.Copy).then_inc(mod_ev, 1)

            def mod_row(s):
                n = s - ADA_FIRST
                c = n // 2
                act.wait_ge(modrow_mm, n + 1)
                act.activation(modrow[32 * c:32 * c + 2, n % 2, :], bank[7][32 * c:32 * c + 2, :], ACT.Copy).then_inc(modrow_ev, 1)

            keys_T(0)
            for t in range(NT):
                if t + 1 < NT:
                    keys_T(t + 1)
                act.wait_ge(o_mm, t + 1)
                act.activation(q[:, t, :], bank[3][:, :], ACT.Square).then_inc(osq_done, 1)
                act.wait_ge(oms_done, t + 1)
                act.activation(hstat[:, 1, :], hstat[:, 0, :], ACT.Sqrt).then_inc(oroot_done, 1)
                mod_sum(MOD_TURNS[t][0])
                if t >= 1:
                    mod_row(MOD_TURNS[t - 1][-1])
                act.wait_ge(yT_mm, t + 1)
                act.activation(yretT[:, t, :, :], bank[5][:, :].rearrange("p (m t) -> p m t", m=CB),
                               ACT.Copy).then_inc(yT_ev, 1)
                if len(MOD_TURNS[t]) > 1:
                    mod_row(MOD_TURNS[t][0])
                    mod_sum(MOD_TURNS[t][1])
            mod_row(MOD_TURNS[-1][-1])
            for t in range(NT):
                act.wait_ge(x1_ready, 2 * t + 2)
                if t >= 1:
                    act.wait_ge(ssq2_done, t)
                act.activation(square, x[:, t, :], ACT.Square, accum_out=stat[:, 0, t:t + 1]).then_inc(ssq2_done, 1)
                act.wait_ge(ms2_done, t + 1)
                act.activation(stat[:, 2, t:t + 1], stat[:, 1, t:t + 1], ACT.Sqrt).then_inc(root2_done, 1)
                if t >= 2:
                    act.wait_ge(rt_mm, t - 1)
                for half in range(2):
                    act.wait_ge(xn2T_mm, 2 * t + half + 1)
                    act.activation(xn2T[:, t % 2, 4 * half:4 * half + 4, :],
                                   bank[4 + half][:, :].rearrange("p (k t) -> p k t", k=4), ACT.Copy).then_inc(xn2T_ev, 1)

            def load_rows(p_, at):
                act.dma_start(xe[:, p_, :], xs_rows[bass.ds(at, P), :]).then_inc(xe_in[p_], 16)

            act.sem_inc(y_out[0], 32)
            act.sem_inc(y_out[1], 32)
            act.sem_inc(y_ev, 2)
            act.wait_ge(xs_out, 16 * 2 * NT)
            act.wait_ge(ssq2_done, NT)
            act.wait_ge(xn2_ready, NT)
            for n in range(2):
                act.dma_start(xe[:, n, :], xs_rows[P * n:P * n + P, :]).then_inc(xe_in[n], 16)

            def silu(n, p_):
                act.wait_ge(gu_mm, n + 1)
                act.activation(sgate[BLK:2 * BLK, p_, :], bank[2 + p_][0:BLK, 0:DE], ACT.Silu).then_inc(silu_done, 1)

            def results(n, p_, stored_before):
                act.wait_ge(ht_mm, n + 1)
                act.activation(hidT[:, p_, :, :], bank[4 + p_][:, 0:2 * BLK].rearrange("p (c s) -> p c s", c=2),
                               ACT.Copy).then_inc(ht_ready, 1)
                act.wait_ge(down_mm, n + 1)
                act.wait_ge(y_out[p_], stored_before)
                act.activation(ysb[:, p_, :], bank[6 + p_][:, :], ACT.Copy).then_inc(y_ev, 1)
                act.wait_ge(y_ev, n + 3)
                for half in range(2):
                    act.dma_start(y_rows[bass.ds(n * BLK, BLK), SL * half:SL * half + SL],
                                  ysb[BLK * half:BLK * half + BLK, p_, :]).then_inc(y_out[p_], 16)

            act.wait_ge(exp_in, 1)
            act.activation(rt[:, 40:60], rt[:, 20:40], ACT.Exp)
            act.activation(rt[:, 65:70], rt[:, 60:65], ACT.Exp).then_inc(exp_out, 1)
            with act.Fori(0, EXPERTS // NSLOT) as i:
                for j in range(NSLOT):
                    n = i * NSLOT + j
                    silu(n, j % 2)
                    if j == 2:
                        act.wait_ge(ov_done, 1)
                    if j % 2 == 0:
                        load_rows(j // 2, n * BLK + 2 * P)
                    results(n, j % 2, i * (32 * NSLOT // 2) + 32 * (1 + j // 2))
            act.wait_ge(routed, 1)
            count = act.value_load(ov_tab[0:1, OVB:OVB + 1], min_val=0, max_val=OVB // 2 - 1)
            with act.If(count > 0):
                with act.Fori(0, count) as m:
                    act.wait_ge(xe_mm, m * 2 + (EXPERTS + 2))
                    load_rows(0, m * P + (EXPERTS // 2 + 1) * P)
                    for j in range(2):
                        silu(m * 2 + (EXPERTS + j), j)
                    for j in range(2):
                        results(m * 2 + (EXPERTS + j), j, m * 32 + 32 * (1 + EXPERTS // 2))
            act.wait_ge(xe_in[0], 16 * (EXPERTS // 4 + 1))
            act.wait_ge(xe_in[1], 16 * (EXPERTS // 4 + 1))
            def first_part(t):
                act.wait_ge(got_in[t], 32)
                act.activation(got[:, t, 0, :], got[:, t, 0, :], ACT.Copy, scale=wsel[:, t, 0:1]).then_inc(part0_ready, 1)

            act.wait_ge(routed, 1)
            first_part(0)
            first_part(1)
            for t in range(NT):
                if t + 2 < NT:
                    first_part(t + 2)
                act.wait_ge(x2_ready[t], 1)
                if t >= 1:
                    act.wait_ge(ssq3_done, t)
                act.activation(sq7, x[:, t, :], ACT.Square, accum_out=stat[:, 0, t:t + 1]).then_inc(ssq3_done, 1)
                act.wait_ge(ms3_done, t + 1)
                act.activation(stat[:, 2, t:t + 1], stat[:, 1, t:t + 1], ACT.Sqrt).then_inc(root3_done, 1)

        @block.tensor
        def _(pe):
            def mod_slice(s, item, out):
                landed(pe, item)
                w = wide(item)
                pe.matmul(out[0:32, :], k("sel_bias")[0:ADA_ALL, 32 * s:32 * s + 32], b_ada[:, :], start=True, stop=False)
                for kt in range(KT):
                    j = kt % 4
                    last = pe.matmul(out[32 * j:32 * j + 32, :], cs[:, kt, :], w[:, kt, :],
                                     start=(0 < kt < 4), stop=(kt >= 4))
                last.then_inc(mod_mm, 1)

            pe.wait_ge(kept_in, 16)
            pe.wait_ge(c_in, 16 * 3)
            pe.wait_ge(cs_ready, 2)
            def normed_T(t):
                pe.wait_ge(xs_ready, t + 1)
                if t >= 2:
                    pe.wait_ge(xT_dve, t - 1)
                    pe.wait_ge(xT_act, t - 1)
                for half in range(2):
                    for c in range(4):
                        kt = 4 * half + c
                        last = pe.transpose(bank[4 + 2 * (t % 2) + half][:, P * c:P * c + P],
                                            xs[:, t % 2, P * kt:P * kt + P], ident)
                    last.then_inc(xT_mm, 1)

            for s in range(ADA_FIRST):
                if s >= 2:
                    pe.wait_ge(mod_ev, s - 1)
                mod_slice(s, s, bank[s % 2])
                for t in X_TURNS[s]:
                    normed_T(t)
                pe.wait_ge(mod_ev, s + 1)
                half = s % 2
                ms = modsum[:, :].rearrange("p (q k) -> p k q", k=KT)
                for kt in range(KT):
                    last = pe.matmul(bank[2 + s // 2][64 * half:64 * half + 64, 2 * kt:2 * kt + 2], ms[:, kt, :],
                                     k("sel_pair"), start=True, stop=True)
                last.then_inc(modcol_mm, 1)
            def split_product(out, lhs, rhs, start, stop):
                pe.matmul(out, lhs[0], rhs[0], start=start, stop=False)
                pe.matmul(out, lhs[0], rhs[1], start=False, stop=False)
                return pe.matmul(out, lhs[1], rhs[0], start=False, stop=stop)

            for n in range(CONV_PIECES):
                pe.wait_ge(w_lo_ready, n + 1)
                if n >= 2:
                    done = (conv_c_ev, conv_h_ev, conv_b_ev)[(n - 2) // CB]
                    pe.wait_ge(done, (n - 2) % CB + 1)
                w = [as_piece(b[n % 2], n) for b in (w_hi, w_lo)]
                for kt in range(KT):
                    if n == 0:
                        pe.wait_ge(xn_lo_ready, kt + 1)
                    for g in range(2):
                        cols = slice(HALF_TOK * g, HALF_TOK * g + HALF_TOK)
                        last = split_product(bank[2 * g + n % 2][:, 0:HALF_TOK], [b[:, kt, :] for b in w],
                                             [b[:, kt, cols] for b in (xn_hi, xn_lo)], kt == 0, kt == KT - 1)
                last.then_inc(proj_mm, 1)

            def state_update(c, n):
                pe.wait_ge(kd_ready, n + 1)
                if n >= 1:
                    pe.wait_ge(st_ready, n)
                for h in range(HEADS):
                    last = pe.matmul(bank[st_bank(n)][:, DH * h:DH * h + DH], kd[:, DH * h:DH * h + DH], v[:, c, DH * h:DH * h + DH],
                                     start=True, stop=True)
                last.then_inc(st_mm, 1)

            for piece in range(CONV_PIECES, PIECES):
                s, j = (piece - CONV_PIECES) // 4, piece % 4
                pe.wait_ge(w_lo_ready, piece + 1)
                w = [as_piece(b[piece % 2], piece) for b in (w_hi, w_lo)]
                for t in range(NT):
                    n = NT * s + t
                    if j == 0 and n >= 8:
                        pe.wait_ge(qkvg_ev, n - 7)
                    if piece == CONV_PIECES and t == NT - 1:
                        pe.wait_ge(conv_b_ev, CB)
                    cols = slice(P * t, P * t + P)
                    for c in range(2):
                        kt = 2 * j + c
                        last = split_product(bank_of(n)[:, :], [b[:, kt, cols] for b in (xn_hi, xn_lo)],
                                             [b[:, c, :] for b in w], kt == 0, kt == KT - 1)
                    if j == 3:
                        last.then_inc(proj_mm, 1)
                if j < 3:
                    last.then_inc(quarter_mm, 1)
                if s == 3:
                    if j == 0:
                        pe.wait_ge(qkvg_ev, 3 * NT)
                    state_update((4, 3, 2, 0)[j], j)
            state_update(0, 4)
            pe.wait_ge(qkvg_ev, 4 * NT)
            pe.wait_ge(rope_done, 8)
            pe.wait_ge(conv_b_ev, CB)
            pe.wait_ge(dec_done, 1)

            def query_key_T(t):
                if t >= 1:
                    pe.wait_ge(kT_ev, t)
                    pe.wait_ge(qT_ev, t)
                for h in range(HEADS):
                    pe.transpose(bank[0][:, P * h:P * h + P], q[:, t, DH * h:DH * h + DH], ident)
                for h in range(HEADS):
                    last = pe.transpose(bank[1][:, P * h:P * h + P], kk[:, t, DH * h:DH * h + DH], ident)
                last.then_inc(qkT_mm, 1)

            def scores(t):
                if t == 0:
                    pe.wait_ge(st_ready, 5)
                pe.wait_ge(kT_ev, t + 1)
                pe.wait_ge(qT_ev, t + 1)
                if t >= 1:
                    pe.wait_ge(sm_ready, t)
                for h in range(HEADS):
                    last = pe.matmul(bank[2][:, P * h:P * h + P], kT[:, P * h:P * h + P], qT[:, P * h:P * h + P],
                                     start=True, stop=True)
                last.then_inc(sc_mm, 1)

            def mod_row(s):
                c = (s - ADA_FIRST) // 2
                pe.wait_ge(mod_ev, s + 1)
                if s > ADA_FIRST:
                    pe.wait_ge(modrow_ev, s - ADA_FIRST)
                pe.matmul(bank[7][32 * c:32 * c + 2, :], k("sel_pair"), modsum[:, :], start=True, stop=True).then_inc(modrow_mm, 1)

            query_key_T(0)
            scores(0)
            for t in range(NT):
                if t + 1 < NT:
                    query_key_T(t + 1)
                pe.wait_ge(st_ready, 5 + max(t - 1, 0))
                pe.wait_ge(sm_ready, t + 1)
                if t >= 1:
                    pe.wait_ge(yr_ready, t)
                    pe.wait_ge(state_in, 32)
                for h in range(HEADS):
                    cols = slice(DH * h, DH * h + DH)
                    last = pe.matmul(bank[3][:, cols], sm[:, cols], v[:, t, cols], start=True, stop=(t == 0))
                    if t >= 1:
                        pe.matmul(bank[3][:, cols], qTf[t % 2][:, cols], sfw[:, cols], start=False, stop=False)
                        last = pe.matmul(bank[3][:, cols], qTb[t % 2][:, cols], sbk[:, t - 1, cols], start=False, stop=True)
                last.then_inc(o_mm, 1)
                if 1 <= t <= 3:
                    state_update(t, 4 + t)
                s = MOD_TURNS[t][0]
                mod_slice(s, N_IN + s, bank[6])
                if t + 1 < NT:
                    scores(t + 1)
                mod_row(s)
                pe.wait_ge(yr_ready, t + 1)
                if t >= 1:
                    pe.wait_ge(yT_ev, t)
                for h in range(HEADS):
                    last = pe.transpose(bank[5][:, P * h:P * h + P], q[:, t, DH * h:DH * h + DH], ident)
                last.then_inc(yT_mm, 1)
                for s in MOD_TURNS[t][1:]:
                    mod_slice(s, N_IN + s, bank[6])
                    mod_row(s)
            pe.wait_ge(yT_ev, NT)
            pe.wait_ge(modrow_ev, ADA_ALL - ADA_FIRST)

            def project(t, half):
                n = 2 * t + half
                if t == 0:
                    landed(pe, ADA_ALL + N_IN + half)
                if n >= 4:
                    pe.wait_ge(x1_ready, n - 3)
                w = wide(ADA_ALL + N_IN + half)
                for kt in range(KT):
                    lhs = yconvT[:, kt, P * t:P * t + P] if kt < CB else yretT[:, t, kt - CB, :]
                    last = pe.matmul(bank[n % 4][:, :], lhs, w[:, kt, :], start=(kt == 0), stop=(kt == KT - 1))
                last.then_inc(wout_mm, 1)

            def router_T(t):
                pe.wait_ge(xn2_ready, t + 1)
                for kt in range(KT):
                    if t >= 1 and kt % 4 == 0:
                        pe.wait_ge(xn2T_ev, 2 * t - 1 + kt // 4)
                    last = pe.transpose(bank[4 + kt // 4][:, P * (kt % 4):P * (kt % 4) + P], xn2[t][:, P * kt:P * kt + P], ident)
                    if kt % 4 == 3:
                        last.then_inc(xn2T_mm, 1)

            def router(t):
                pe.wait_ge(xn2T_ev, 2 * t + 2)
                if t >= 1:
                    pe.wait_ge(lg_ready, t)
                for kt in range(KT):
                    last = pe.matmul(bank[6][:, 0:GROUPS + EXPERTS], xn2T[:, t % 2, kt, :], w_router[:, kt, :],
                                     start=(kt == 0), stop=(kt == KT - 1))
                last.then_inc(rt_mm, 1)

            def ranks(t):
                pe.wait_ge(chosen, t + 1)
                if t >= 1:
                    pe.wait_ge(placed, t)
                both = rt[:, BOTH + EXPERTS * (t % 2):BOTH + EXPERTS * (t % 2) + EXPERTS]
                pe.matmul(bank[7][:, 0:32], k("before"), both, start=True, stop=True)
                pe.matmul(bank[7][:, 32:64], k("ones").broadcast_to([P, P]), both, start=True, stop=True).then_inc(rank_mm, 1)

            pe.wait_ge(small_in, 16 * 8)
            for t in range(NT):
                project(t, 0)
                if t >= 1:
                    router_T(t - 1)
                if t == NT - 1:
                    router(t - 1)
                project(t, 1)
                if 1 <= t < NT - 1:
                    router(t - 1)
                if t >= 2:
                    ranks(t - 2)
            router_T(NT - 1)
            ranks(NT - 2)
            router(NT - 1)
            ranks(NT - 1)

            def rows_T(p_, tiles):
                for kt in tiles:
                    last = pe.transpose(bank[kt // 4][:, P * (kt % 4):P * (kt % 4) + P], xe[:, p_, P * kt:P * kt + P], ident)
                    if kt % 4 == 3:
                        last.then_inc(xe_mm, 1)

            def gate_up(s, p_, pair, hid_before=None):
                for kt in range(KT):
                    lhs = xeT[:, pair, kt, BLK * p_:BLK * p_ + BLK]
                    pe.matmul(bank[2 + p_][0:BLK, 0:DE], lhs, w_gate(s)[:, kt, :], start=(kt == 0), stop=(kt == KT - 1))
                    if hid_before is not None and kt == KT - 1:
                        pe.wait_ge(hid_done, hid_before)
                    last = pe.matmul(bank[2 + p_][BLK:2 * BLK, 0:DE], lhs, w_up(s)[:, kt, :],
                                     start=(kt == 0), stop=(kt == KT - 1))
                last.then_inc(gu_mm, 1)

            def hidden_T(p_):
                for c in range(2):
                    last = pe.transpose(bank[4 + p_][:, BLK * c:BLK * c + BLK], hid[0:BLK, p_, P * c:P * c + P],
                                        ident[0:BLK, 0:BLK])
                last.then_inc(ht_mm, 1)

            def down(s, p_, hid_next=None):
                for c in range(2):
                    for half in range(2):
                        if hid_next is not None and c == 1 and half == 1:
                            pe.wait_ge(hid_done, hid_next)
                        last = pe.matmul(bank[6 + p_][BLK * half:BLK * half + BLK, :], hidT[:, p_, c, :],
                                         w_down(s)[:, c, SL * half:SL * half + SL], start=(c == 0), stop=(c == 1))
                last.then_inc(down_mm, 1)

            pe.wait_ge(placed, NT)
            pe.wait_ge(xe_in[0], 16)
            rows_T(0, range(KT))
            with pe.Fori(0, EXPERTS // NSLOT) as i:
                for j in range(NSLOT):
                    n = i * NSLOT + j
                    s, p_, pair = e_slot[j], j % 2, j // 2
                    pe.wait_ge(ring_in[s], i * 48 + (16 * early_uses[s] + 48))
                    pe.wait_ge(xe_ready, i * NSLOT + 2 * (pair + 1))
                    pe.wait_ge(hid_done, n + 1)
                    gate_up(s, p_, pair)
                    pe.wait_ge(xe_in[1 - pair], i * 16 + 16 * (1 + pair))
                    rows_T(1 - pair, range(4 * p_, 4 * p_ + 3))
                    pe.wait_ge(hid_done, n + 3)
                    rows_T(1 - pair, range(4 * p_ + 3, 4 * p_ + 4))
                    hidden_T(p_)
                    pe.wait_ge(ht_ready, n + 1)
                    pe.wait_ge(y_ev, n + 1)
                    down(s, p_)
            pe.wait_ge(routed, 1)
            count = pe.value_load(ov_tab[0:1, OVB:OVB + 1], min_val=0, max_val=OVB // 2 - 1)
            with pe.If(count > 0):
                with pe.Fori(0, count) as m:
                    for j in range(2):
                        s = e_slot[j]
                        pe.wait_ge(ring_in[s], m * 48 + (16 * early_uses[s] + 48 * (EXPERTS // NSLOT + 1)))
                        if j == 0:
                            pe.wait_ge(xe_ready, m * 2 + (EXPERTS + 2))
                        gate_up(s, j, 0, None if j == 0 else m * 2 + (EXPERTS + 3))
                    for j in range(2):
                        hidden_T(j)
                        pe.wait_ge(ht_ready, m * 2 + (EXPERTS + 1 + j))
                        pe.wait_ge(y_ev, m * 2 + (EXPERTS + 1 + j))
                        down(e_slot[j], j, m * 2 + (EXPERTS + 4) if j == 0 else None)
                    pe.wait_ge(xe_in[0], m * 16 + 16 * (EXPERTS // 4 + 2))
                    rows_T(0, range(KT))

        @block.vector
        def _(dve):
            steps = [0]

            def then(ins):
                steps[0] += 1
                ins.then_inc(step, 1)
                dve.wait_ge(step, steps[0])

            def tt(out, in0, in1, op):
                return dve.tensor_tensor(out, in0, in1, op)

            dve.memset(cs[:, :, :], 0.0).then_inc(cs_zero, 1)
            dve.memset(zeros, 0.0).then_inc(zero_set, 1)
            dve.wait_ge(ssq_done, NT)
            dve.tensor_scalar(stat[:, 1, :], stat[:, 0, :], 1.0 / D, EPS, ALU.mult, ALU.add).then_inc(ms_done, 1)
            dve.wait_ge(root_done, 1)
            dve.reciprocal(stat[:, 3, :], stat[:, 2, :]).then_inc(rstd_done, 1)
            for s in range(ADA_FIRST):
                dve.wait_ge(mod_mm, s + 1)
                if s >= 1:
                    dve.wait_ge(modcol_mm, s)
                dve.tensor_copy(modsum[:, :], bank[s % 2][:, :]).then_inc(mod_ev, 1)
                for t in X_TURNS[s]:
                    dve.wait_ge(xT_mm, 2 * t + 1)
                    dve.tensor_copy(xnT[:, 0:4, P * t:P * t + P],
                                    bank[4 + 2 * (t % 2)][:, :].rearrange("p (k t) -> p k t", k=4)).then_inc(xT_dve, 1)
            dve.wait_ge(modcol_mm, ADA_FIRST)
            dve.wait_ge(g_mix_in, 16)
            pair = lambda b: bank[b][:, 0:2 * KT].rearrange("p (k s) -> p k s", s=2)
            dve.tensor_copy(shift[:, :, :], pair(2)).then_inc(col_ready, 1)
            dve.scalar_tensor_tensor(out=scale[:, :, :], in0=pair(3), scalar=1.0,
                                     in1=g_mix[:, :].rearrange("p (k a) -> p k a", a=1).broadcast_to([P, KT, 2]),
                                     op0=ALU.add, op1=ALU.mult).then_inc(col_ready, 1)
            dve.wait_ge(col_ready, 2)
            dve.wait_ge(xT_act, NT)
            dve.wait_ge(xT_dve, NT)
            for kt in range(KT + 1):
                if kt < KT:
                    dve.tensor_scalar(xnT[:, kt, P:], xnT[:, kt, P:], scale[:, kt, 1:2], shift[:, kt, 1:2],
                                      ALU.mult, ALU.add).then_inc(xn_dve, 1)
                if kt >= 1:
                    dve.wait_ge(xn_hi_ready, kt)
                    tt(xn_lo[:, kt - 1, :], xnT[:, kt - 1, :], xn_hi[:, kt - 1, :], ALU.subtract).then_inc(xn_lo_ready, 1)
            dve.wait_ge(dec_e, 1)
            dve.tensor_scalar(decay[:, 2, :], decay[:, 1, :], -1.0, 1.0, ALU.mult, ALU.add).then_inc(dec_u, 1)
            dve.wait_ge(dec_u, 1)
            then(dve.tensor_scalar(decay[:, 4, :], decay[:, 2, :], -1.0, 1.0, ALU.mult, ALU.add))
            then(dve.tensor_scalar(decay[:, 5, :], decay[:, 4, :], 0.0, None, ALU.is_equal))
            then(tt(decay[:, 4, :], decay[:, 4, :], decay[:, 5, :], ALU.add))
            then(dve.reciprocal(decay[:, 4, :], decay[:, 4, :]))
            dve.wait_ge(dec_ln, 1)
            then(tt(decay[:, 3, :], decay[:, 3, :], decay[:, 5, :], ALU.subtract))
            then(tt(decay[:, 3, :], decay[:, 3, :], decay[:, 4, :], ALU.mult))
            tt(decay[:, 5, :], decay[:, 3, :], decay[:, 1, :], ALU.mult).then_inc(dec_lg, 1)
            dve.wait_ge(dec_act, 1)

            def heads_of(row):
                return row.rearrange("p (a n) -> p a n", a=1).broadcast_to([P, HEADS, P])

            then(tt(mask[:, :, :], decay_tmp[:, 0], heads_of(e("fwd_on")), ALU.mult))
            then(tt(decay_tmp[:, 1], decay_tmp[:, 1], heads_of(e("bwd_on")), ALU.mult))
            tt(mask[:, :, :], mask[:, :, :], decay_tmp[:, 1], ALU.add).then_inc(dec_done, 1)
            for m in range(CB):
                dve.wait_ge(proj_mm, CB + m + 1)
                dve.wait_ge(conv_c_ev, CB)
                for g in range(2):
                    cols = slice(HALF_TOK * g, HALF_TOK * g + HALF_TOK)
                    last = tt(u[:, m, cols], u[:, m, cols], bank[2 * g + m % 2][:, 0:HALF_TOK], ALU.mult)
                last.then_inc(conv_h_ev, 1)
            dve.wait_ge(small_in, 16 * 8)
            dve.wait_ge(conv_h_ev, CB)
            spans = ((0, P, P), (P, TOK, GRID_W))
            for m in range(CB):
                for lo, hi, w in spans:
                    o = yconvT[:, m, lo:hi].rearrange("p (r w) -> p r w", w=w)
                    i_ = u[:, m, lo:hi].rearrange("p (r w) -> p r w", w=w)
                    then(dve.tensor_scalar(o, i_, conv_w[:, 1, m:m + 1], None, ALU.mult))
                    then(dve.scalar_tensor_tensor(out=o[:, :, 1:], in0=i_[:, :, 0:w - 1], scalar=conv_w[:, 0, m:m + 1],
                                                  in1=o[:, :, 1:], op0=ALU.mult, op1=ALU.add))
                    then(dve.scalar_tensor_tensor(out=o[:, :, 0:w - 1], in0=i_[:, :, 1:], scalar=conv_w[:, 2, m:m + 1],
                                                  in1=o[:, :, 0:w - 1], op0=ALU.mult, op1=ALU.add))
                dve.wait_ge(proj_mm, 2 * CB + m + 1)
                for g in range(2):
                    cols = slice(HALF_TOK * g, HALF_TOK * g + HALF_TOK)
                    last = tt(yconvT[:, m, cols], yconvT[:, m, cols], bank[2 * g + m % 2][:, 0:HALF_TOK], ALU.mult)
                last.then_inc(conv_b_ev, 1)
            for n in range(2 * (NT - 1)):
                dst = (q, kk)[n // (NT - 1)]
                t = n % (NT - 1) + 1
                dve.wait_ge(qkvg_ev, NT * (n // (NT - 1)) + t + 1)
                heads = lambda r: r.rearrange("p (a n) -> p a n", a=1).broadcast_to([P, HEADS, DH])
                cur = dst[:, t, :].rearrange("p (h n) -> p h n", h=HEADS)
                pairs = cur.rearrange("p h (n two) -> p h n two", two=2)
                t0 = rope_tmp[:, 0, :].rearrange("p (h n) -> p h n", h=HEADS)
                t1 = rope_tmp[:, 1, :].rearrange("p (h n two) -> p h n two", h=HEADS, two=2)
                sn = heads(rope[:, 1, t - 1, :]).rearrange("p h (n two) -> p h n two", two=2)
                if n:
                    dve.wait_ge(rope_done, n)
                tt(t0, cur, heads(rope[:, 0, t - 1, :]), ALU.mult)
                tt(t1[:, :, :, 0], pairs[:, :, :, 1], sn[:, :, :, 0], ALU.mult)
                then(tt(t1[:, :, :, 1], pairs[:, :, :, 0], sn[:, :, :, 1], ALU.mult))
                tt(cur, t0, rope_tmp[:, 1, :].rearrange("p (h n) -> p h n", h=HEADS), ALU.add).then_inc(rope_done, 1)

            def col_heads(c):
                return c.rearrange("p (h a) -> p h a", a=1).broadcast_to([P, HEADS, DH])

            def decay_keys(c, d, before):
                if before:
                    dve.wait_ge(st_mm, before)
                tt(kd.rearrange("p (h n) -> p h n", h=HEADS), kk[:, c, :].rearrange("p (h n) -> p h n", h=HEADS),
                   col_heads(kdec[:, d, :]), ALU.mult).then_inc(kd_ready, 1)

            dve.wait_ge(rope_done, 8)
            dve.wait_ge(state_in, 32)
            for n, c in enumerate((4, 3, 2)):
                decay_keys(c, 1, n)
                then(tt(sbk[:, c - 2, :].rearrange("p (h n) -> p h n", h=HEADS),
                        sbk[:, c - 1, :].rearrange("p (h n) -> p h n", h=HEADS), col_heads(cdec[:, 1, :]), ALU.mult))
                dve.wait_ge(st_mm, n + 1)
                tt(sbk[:, c - 2, :], sbk[:, c - 2, :], bank[st_bank(n)][:, :], ALU.add).then_inc(st_ready, 1)
                dve.wait_ge(st_ready, n + 1)
            for d in range(2):
                decay_keys(0, d, 3 + d)
                dve.wait_ge(st_mm, 4 + d)
                dve.tensor_copy(state_c[:, d, :], bank[st_bank(3 + d)][:, :]).then_inc(st_ready, 1)
            dve.wait_ge(qkvg_ev, 4 * NT)
            as_heads = lambda r: r.rearrange("p (h n) -> p h n", h=HEADS)

            def queries_T(t):
                dve.wait_ge(qkT_mm, t + 1)
                if t >= 1:
                    if t >= 3:
                        dve.wait_ge(o_mm, t - 1)
                    tt(qTf[t % 2], bank[0][:, :], qdec[:, 0, :, :].rearrange("p h n -> p (h n)"), ALU.mult)
                    tt(qTb[t % 2], bank[0][:, :], qdec[:, 1, :, :].rearrange("p h n -> p (h n)"), ALU.mult)
                    dve.wait_ge(sc_mm, t)
                dve.tensor_copy(qT, bank[0][:, :]).then_inc(qT_ev, 1)

            def masked(t):
                dve.wait_ge(sc_mm, t + 1)
                if t >= 1:
                    dve.wait_ge(o_mm, t)
                tt(sm, bank[2][:, :], mask[:, :, :].rearrange("p h n -> p (h n)"), ALU.mult).then_inc(sm_ready, 1)

            queries_T(0)
            masked(0)
            for t in range(NT):
                if t + 1 < NT:
                    queries_T(t + 1)
                if 1 <= t <= 3:
                    decay_keys(t, 0, 4 + t)
                dve.wait_ge(osq_done, t + 1)
                then(dve.tensor_reduce(hstat[:, 2, :], as_heads(q[:, t, :]), X, ALU.add))
                dve.tensor_scalar(hstat[:, 0, :], hstat[:, 2, :], 1.0 / DH, EPS, ALU.mult, ALU.add).then_inc(oms_done, 1)
                then(tt(q[:, t, :], bank[3][:, :], gate[:, t, :], ALU.mult))
                dve.wait_ge(oroot_done, t + 1)
                then(dve.reciprocal(hstat[:, 2, :], hstat[:, 1, :]))
                tt(as_heads(q[:, t, :]), as_heads(q[:, t, :]), col_heads(hstat[:, 2, :]), ALU.mult).then_inc(yr_ready, 1)
                if 1 <= t <= 3:
                    then(tt(as_heads(sfw), as_heads(sfw), col_heads(cdec[:, 0, :]), ALU.mult))
                    dve.wait_ge(st_mm, 5 + t)
                    tt(sfw, sfw, bank[4][:, :], ALU.add).then_inc(st_ready, 1)
                    dve.wait_ge(st_ready, 5 + t)
                if t + 1 < NT:
                    masked(t + 1)

            dve.wait_ge(rows_in[0], 16)
            dve.wait_ge(x_again, 32)

            def residual(t, half):
                n = 2 * t + half
                cols = slice(SL * half, SL * half + SL)
                dve.wait_ge(wout_mm, n + 1)
                if n:
                    dve.wait_ge(x1_ready, n)
                then(tt(part, bank[n % 4][:, :], rows[0][:, min(t, 1), cols], ALU.mult))
                tt(x[:, t, cols], x[:, t, cols], part, ALU.add).then_inc(x1_ready, 1)

            def second_norm(t):
                dve.wait_ge(x1_ready, 2 * t + 2)
                dve.wait_ge(scale2_ready, 1)
                dve.wait_ge(ssq2_done, t + 1)
                dve.tensor_scalar(stat[:, 1, t:t + 1], stat[:, 0, t:t + 1], 1.0 / D, EPS, ALU.mult, ALU.add).then_inc(ms2_done, 1)
                dve.wait_ge(root2_done, t + 1)
                then(dve.reciprocal(stat[:, 3, t:t + 1], stat[:, 2, t:t + 1]))
                side = min(t, 1)
                as_qk = lambda r: r.rearrange("p (q k) -> p q k", q=P)
                dst = xn2[t].rearrange("p (k q) -> p q k", q=P)
                then(dve.scalar_tensor_tensor(out=dst, in0=as_qk(x[:, t, :]), scalar=stat[:, 3, t:t + 1],
                                              in1=as_qk(rows[2][:, side, :]), op0=ALU.mult, op1=ALU.mult))
                tt(dst, dst, as_qk(rows[1][:, side, :]), ALU.add).then_inc(xn2_ready, 1)

            def over(ap, n):
                return ap.rearrange("p (t a) -> p t a", a=1).broadcast_to([P, ap.shape[1], n])

            def row_over(ap, n):
                return ap.rearrange("p (a m) -> p a m", a=1).broadcast_to([P, n, ap.shape[1]])

            eq4, eq8, top = rt[:, 100:104], rt[:, 104:112], rt[:, 112:113]
            ohg, oh1, oh2 = rt[:, 116:120], rt[:, 120:128], rt[:, 128:136]
            inner, inner2 = rt[:, 136:144], rt[:, 144:152]
            best = lambda j, t: rt[:, 160 + 5 * j + t:161 + 5 * j + t]
            choice = lambda j, t: rt[:, CHOICE[j] + 32 * t:CHOICE[j] + 32 * t + 32]
            both = lambda t: rt[:, BOTH + 32 * (t % 2):BOTH + 32 * (t % 2) + 32]
            rank = lambda t: rt[:, RANK + 32 * t:RANK + 32 * t + 32]
            before = lambda t: rt[:, BEFORE + 32 * t:BEFORE + 32 * t + 32]
            spread = rt[:, 200:232].rearrange("p (g j) -> p g j", g=GROUPS)
            own_row = rt[:, 800:832]
            far = rt[:, 832:864]
            posf = rt[:, 864:866]

            def first_max(values, desc, best, out):
                n = [P, values.shape[1]]
                tmp = eq4 if n[1] == GROUPS else eq8
                then(dve.tensor_reduce(best, values, X, ALU.max))
                then(dve.scalar_tensor_tensor(out=tmp, in0=values, scalar=best, in1=desc, op0=ALU.is_equal, op1=ALU.mult))
                then(dve.tensor_reduce(top, tmp, X, ALU.max))
                then(tt(out, tmp, top.broadcast_to(n), ALU.is_equal))

            def choose(t):
                dve.wait_ge(rt_mm, t + 1)
                tt(logits[:, t, :], bank[6][:, 0:GROUPS + EXPERTS], b_router[:, :], ALU.add).then_inc(lg_ready, 1)
                dve.wait_ge(lg_ready, t + 1)
                lgg, lge = logits[:, t, 0:GROUPS], logits[:, t, GROUPS:]
                first_max(lgg, k("desc_group"), best(0, t), ohg)
                tt(rt[:, 20 + 4 * t:24 + 4 * t], lgg, best(0, t).broadcast_to([P, GROUPS]), ALU.subtract)
                then(tt(spread, lge.rearrange("p (g j) -> p g j", g=GROUPS), over(ohg, PER_GROUP), ALU.mult))
                then(dve.tensor_reduce(inner, spread.rearrange("p g j -> p j g"), X, ALU.add))
                first_max(inner, k("desc_inner"), best(1, t), oh1)
                then(dve.scalar_tensor_tensor(out=inner2, in0=oh1, scalar=-1e30, in1=inner, op0=ALU.mult, op1=ALU.add))
                first_max(inner2, k("desc_inner"), best(2, t), oh2)
                for j, oh in enumerate((oh1, oh2)):
                    then(tt(choice(j, t).rearrange("p (g j) -> p g j", g=GROUPS), row_over(oh, GROUPS), over(ohg, PER_GROUP),
                            ALU.mult))
                tt(both(t), choice(0, t), choice(1, t), ALU.add).then_inc(chosen, 1)

            def place(t):
                dve.wait_ge(rank_mm, t + 1)
                then(tt(rank(t), bank[7][:, 0:32], before(t), ALU.add))
                then(tt(before(t + 1), bank[7][:, 32:64], before(t), ALU.add))
                then(dve.tensor_scalar(far, rank(t), float(BLK), float(FAR), ALU.is_ge, ALU.mult))
                then(tt(own_row, rank(t), k("block_row"), ALU.add))
                then(tt(own_row, own_row, far, ALU.add))
                for j in range(2):
                    then(tt(spread.rearrange("p g j -> p (g j)"), choice(j, t), own_row, ALU.mult))
                    then(dve.tensor_reduce(posf[:, j:j + 1], spread.rearrange("p g j -> p (g j)"), X, ALU.add))
                dve.tensor_copy(pos_own[:, t, :], posf).then_inc(placed, 1)

            for t in range(NT):
                residual(t, 0)
                if t == 2:
                    then(dve.memset(before(0), 0.0))
                if t >= 2:
                    choose(t - 2)
                if t == NT - 1:
                    choose(t - 1)
                residual(t, 1)
                if t == 0:
                    dve.wait_ge(rows_in[2], 16)
                    dve.wait_ge(gffn_in, 16)
                    for side in range(2):
                        last = dve.scalar_tensor_tensor(out=rows[2][:, side, :], in0=rows[2][:, side, :], scalar=1.0, in1=g_ffn,
                                                        op0=ALU.add, op1=ALU.mult)
                    last.then_inc(scale2_ready, 1)
                    dve.wait_ge(rows_in[1], 16)
                second_norm(t)
                if t >= 2:
                    place(t - 2)
            place(NT - 2)
            choose(NT - 1)
            place(NT - 1)

            dve.sem_inc(hid_done, 2)
            dve.wait_ge(placed, NT)

            def rows_evacuate(pair, half):
                dve.tensor_copy(xeT[:, pair, 4 * half:4 * half + 4, :],
                                bank[half][:, :].rearrange("p (k s) -> p k s", k=4)).then_inc(xe_ready, 1)

            def hidden(p_):
                tt(hid[0:BLK, p_, :].rearrange("p (c q) -> p q c", c=2),
                   sgate[BLK:2 * BLK, p_, :].rearrange("p (q c) -> p q c", c=2),
                   bank[2 + p_][BLK:2 * BLK, 0:DE].rearrange("p (q c) -> p q c", c=2), ALU.mult).then_inc(hid_done, 1)

            def overflow_rows():
                flat2 = lambda lo: rt[:, lo:lo + NT * EXPERTS]
                total = before(NT)
                nov = rt[:, 1824:1856]
                grid = rt[:, BOTH:BOTH + EXPERTS * MAX_SPLIT].rearrange("p (e m) -> p e m", e=EXPERTS)
                tt(rt[:, 60:65], rt[:, 170:175], rt[:, 165:170], ALU.subtract).then_inc(exp_in, 1)
                then(tt(grid, over(total, MAX_SPLIT), row_over(k("splits"), EXPERTS), ALU.is_gt))
                then(dve.tensor_reduce(nov, grid, X, ALU.add))
                run = [rt[:, 1728:1776], rt[:, 1776:1824]]
                then(dve.memset(rt[:, 1728:1824], 0.0))
                then(dve.tensor_copy(run[0][:, 16:48], nov))
                cur = 0
                for hop in (1, 2, 4, 8, 16):
                    then(tt(run[1 - cur][:, 16:48], run[cur][:, 16:48], run[cur][:, 16 - hop:48 - hop], ALU.add))
                    cur = 1 - cur
                ends = run[cur][:, 16:48]
                jump = rt[:, 1856:1888]
                then(tt(jump, ends, nov, ALU.subtract))
                then(dve.tensor_scalar(jump, jump, float(BLK), float(OV_ROW0 - BLK), ALU.mult, ALU.add))
                then(tt(jump, jump, k("block_row"), ALU.subtract))
                beyond, row = rt[:, 2112:2272], flat2(RANK)
                te = lambda r: r.rearrange("p (t e) -> p t e", t=NT)
                then(dve.tensor_scalar(beyond, row, float(BLK), None, ALU.is_ge))
                then(tt(te(row), te(row), row_over(k("block_row"), NT), ALU.add))
                then(tt(te(rt[:, 2272:2432]), te(beyond), row_over(jump, NT), ALU.mult))
                then(tt(row, row, rt[:, 2272:2432], ALU.add))
                then(dve.tensor_scalar(beyond, beyond, float(-FAR), float(FAR), ALU.mult, ALU.add))
                then(tt(beyond, beyond, row, ALU.add))
                pos2 = rt[:, 2440:2450].rearrange("p (t j) -> p t j", j=2)
                pos3 = rt[:, 2450:2460].rearrange("p (t j) -> p t j", j=2)
                for j in range(2):
                    sel = flat2(CHOICE[j])
                    then(tt(rt[:, 2272:2432], sel, beyond, ALU.mult))
                    then(dve.tensor_reduce(pos3[:, :, j], te(rt[:, 2272:2432]), X, ALU.add))
                    then(tt(sel, sel, row, ALU.mult))
                    then(dve.tensor_reduce(pos2[:, :, j], te(sel), X, ALU.add))
                then(dve.tensor_copy(posi[:, :, :], pos2))
                then(dve.tensor_copy(pos_ov[:, :, :], pos3))
                return ends

            def weights_and_table(ends):
                dve.wait_ge(exp_out, 1)
                gsum, e21, w = rt[:, 0:5], rt[:, 65:70], rt[:, 5:10]
                then(dve.tensor_reduce(gsum, rt[:, 40:60].rearrange("p (t g) -> p t g", t=NT), X, ALU.add))
                then(dve.tensor_scalar(w, e21, 1.0, None, ALU.add))
                then(tt(w, w, gsum, ALU.mult))
                then(dve.reciprocal(w, w))
                then(dve.tensor_copy(wsel[:, :, 0], w))
                then(tt(wsel[:, :, 1], w, e21, ALU.mult))
                tab = rt[:, 2464:2465 + OVB]
                own = rt[:, 500:500 + OVB * EXPERTS].rearrange("p (b e) -> p b e", b=OVB)
                then(tt(own, row_over(ends, OVB), over(k("ov_index"), EXPERTS), ALU.is_le))
                then(dve.tensor_reduce(tab[:, 0:OVB], own, X, ALU.add))
                then(dve.tensor_scalar(tab[:, 0:OVB], tab[:, 0:OVB], float(EXPERTS - 1), None, ALU.min))
                pair_on = rt[:, 2490:2490 + OVB // 2]
                then(tt(pair_on, k("ov_index").rearrange("p (m two) -> p m two", two=2)[:, :, 0],
                        ends[:, EXPERTS - 1:EXPERTS].broadcast_to([P, OVB // 2]), ALU.is_lt))
                then(dve.tensor_reduce(tab[:, OVB:OVB + 1], pair_on, X, ALU.add))
                dve.tensor_copy(ov_tab[:, :], tab).then_inc(routed, 1)

            ends = overflow_rows()
            for half in range(2):
                dve.wait_ge(xe_mm, half + 1)
                rows_evacuate(0, half)
            weights_and_table(ends)
            with dve.Fori(0, EXPERTS // NSLOT) as i:
                for j in range(NSLOT):
                    n = i * NSLOT + j
                    dve.wait_ge(silu_done, n + 1)
                    hidden(j % 2)
                    dve.wait_ge(xe_mm, n + 3)
                    rows_evacuate(1 - j // 2, j % 2)
            count = dve.value_load(ov_tab[0:1, OVB:OVB + 1], min_val=0, max_val=OVB // 2 - 1)
            with dve.If(count > 0):
                with dve.Fori(0, count) as m:
                    for j in range(2):
                        dve.wait_ge(silu_done, m * 2 + (EXPERTS + 1 + j))
                        hidden(j)
                    for half in range(2):
                        dve.wait_ge(xe_mm, m * 2 + (EXPERTS + 3 + half))
                        rows_evacuate(0, half)

            dve.wait_ge(gfin_in, 16)
            dve.wait_ge(rows_in[3], 16)
            dve.wait_ge(routed, 1)

            def combine(t):
                g0, g1 = got[:, t, 0, :], got[:, t, 1, :]
                dve.wait_ge(got_in[t], 32)
                dve.wait_ge(part0_ready, t + 1)
                then(dve.scalar_tensor_tensor(out=g0, in0=g1, scalar=wsel[:, t, 1:2], in1=g0, op0=ALU.mult, op1=ALU.add))
                if t in POOL_SUMS:
                    tt(g0, g0, rows[3][:, min(t, 1), :], ALU.mult).then_inc(gated, 1)
                else:
                    then(tt(g0, g0, rows[3][:, min(t, 1), :], ALU.mult))
                    tt(x[:, t, :], x[:, t, :], g0, ALU.add).then_inc(x2_ready[t], 1)

            def final_norm(t):
                dve.wait_ge(ssq3_done, t + 1)
                dve.tensor_scalar(stat[:, 1, t:t + 1], stat[:, 0, t:t + 1], 1.0 / D, EPS, ALU.mult, ALU.add).then_inc(ms3_done, 1)
                dve.wait_ge(root3_done, t + 1)
                then(dve.reciprocal(stat[:, 3, t:t + 1], stat[:, 2, t:t + 1]))
                if t >= 2:
                    dve.wait_ge(stored[t % 2], 16 * (t // 2))
                dve.wait_ge(x2_ready[t], 1)
                dve.scalar_tensor_tensor(out=outb[:, t % 2, :], in0=x[:, t, :], scalar=stat[:, 3, t:t + 1], in1=g_fin,
                                         op0=ALU.mult, op1=ALU.mult).then_inc(out_ready, 1)

            combine(0)
            combine(1)
            for t in range(NT):
                if t + 2 < NT:
                    combine(t + 2)
                final_norm(t)


_OUTS = [((1, P, D), "float32"), ((1, LAT, D), "float32"), ((1, 1, HEADS, DH, DH), "float32"),
         ((1, 1, HEADS, DH, DH), "float32")]
_INS = ["x_prompt", "x_sample", "state_ret_fwd", "state_ret_bwd", "c", "c_ctx", "norm_mix_g", "norm_ffn_g", "w_ada",
        "b_ada", "w_in", "conv_w", "ret_decay_fwd", "ret_decay_bwd", "w_out", "w_router_group", "b_router_group",
        "w_router_expert", "b_router_expert", "w_gate_e", "w_up_e", "w_down_e", "final_norm_g"]


def kernel(**inputs):
    import concourse.bacc as bacc
    from concourse.bass_utils import run_bass_kernel_spmd as run

    kept, early, rope = const_table()
    arrays = {f"in_{n}": np.ascontiguousarray(inputs[n]) for n in _INS}
    arrays["in_final_norm_g"] = arrays["in_final_norm_g"].reshape(1, D)
    arrays["in_c_kept"], arrays["in_c_early"], arrays["in_c_rope"] = kept, early, rope
    nc = bacc.Bacc("TRN2", target_bir_lowering=False, num_devices=1)
    a = {n[3:]: nc.dram_tensor(n, v.shape, mybir.dt.from_np(v.dtype), kind="ExternalInput").ap() for n, v in arrays.items()}
    outs = [nc.dram_tensor(f"out_{i}", s, mybir.dt.from_np(np.dtype(d)), kind="ExternalOutput").ap()
            for i, (s, d) in enumerate(_OUTS)]
    layer(nc, a, *outs)
    r = run(nc, [arrays], core_ids=[0])
    return tuple(r.results[0][f"out_{i}"] for i in range(len(_OUTS)))
```
